# Optimizing a Trainium2 kernel written in Bass

```python
import math
import jax, jax.numpy as jnp
from jax import lax
import numpy as np

D_MODEL = 1024
BATCH = 1
SEQ = 512
DEPTH = 1

SSM_EXPAND = 2
SSM_D_INNER = SSM_EXPAND * D_MODEL
SSM_HEAD_DIM = 64
SSM_N_HEADS = SSM_D_INNER // SSM_HEAD_DIM
SSM_N_GROUPS = 4
SSM_D_STATE = 128
SSM_CONV = 4
SSM_CHUNK = 128
SSM_CONV_DIM = SSM_D_INNER + 2 * SSM_N_GROUPS * SSM_D_STATE

ATT_HEAD_DIM = 128
ATT_HEADS_PER_GROUP = 4
ATT_PATTERNS = ((128, 1), (512, 4), (2048, 16))
ATT_N_HEADS = ATT_HEADS_PER_GROUP * len(ATT_PATTERNS)
ATT_QKV_DIM = 3 * ATT_N_HEADS * ATT_HEAD_DIM
ATT_OUT_DIM = ATT_HEADS_PER_GROUP * ATT_HEAD_DIM
ATT_BLOCK = 128
ROPE_THETA = 10000.0

N_BRANCH = 2
D_FF = -(-8 * D_MODEL // (3 * 256)) * 256
IN_PROJ_SIZES = (SSM_D_INNER, SSM_CONV_DIM, SSM_N_HEADS, ATT_QKV_DIM, N_BRANCH * D_MODEL)
IN_PROJ_DIM = sum(IN_PROJ_SIZES)
EPS = 1e-6


def rmsnorm(x, g):
    xf = x.astype(jnp.float32)
    y = xf * lax.rsqrt(jnp.mean(xf * xf, axis=-1, keepdims=True) + EPS)
    return (y * g.astype(jnp.float32)).astype(x.dtype)

def rope(t, pos):
    half = t.shape[-1] // 2
    inv = ROPE_THETA ** (-jnp.arange(half, dtype=jnp.float32) / half)
    ang = pos.astype(jnp.float32)[:, None] * inv[None, :]
    cos = jnp.cos(ang)[None, :, None, :]
    sin = jnp.sin(ang)[None, :, None, :]
    t1, t2 = t[..., :half], t[..., half:]
    return jnp.concatenate([t1 * cos - t2 * sin, t2 * cos + t1 * sin], axis=-1)

def segsum(a):
    T = a.shape[-1]
    xx = jnp.broadcast_to(a[..., :, None], a.shape + (T,))
    cs = jnp.cumsum(jnp.where(jnp.tril(jnp.ones((T, T), bool), -1), xx, 0.0), axis=-2)
    return jnp.where(jnp.tril(jnp.ones((T, T), bool)), cs, -jnp.inf)

def causal_depthwise_conv(u, w, b):
    K, C = w.shape
    out = lax.conv_general_dilated(u, w[:, None, :], window_strides=(1,), padding=[(K - 1, 0)],
                                   dimension_numbers=('NWC', 'WIO', 'NWC'), feature_group_count=C)
    return out + b

def ssd_chunked(xs, dt, A, Bm, Cm):
    b, S, H, P = xs.shape
    G, N = Bm.shape[-2:]
    J = H // G
    Q = SSM_CHUNK
    nc = S // Q
    xdt = (xs * dt[..., None]).reshape(b, nc, Q, G, J, P)
    a = (dt * A).reshape(b, nc, Q, G, J).transpose(0, 1, 3, 4, 2)
    a_cs = jnp.cumsum(a, axis=-1)
    Br = Bm.reshape(b, nc, Q, G, N)
    Cr = Cm.reshape(b, nc, Q, G, N)
    tri = jnp.tril(jnp.ones((Q, Q), bool))
    Lmat = jnp.exp(jnp.where(tri, a_cs[..., :, None] - a_cs[..., None, :], -jnp.inf))
    CB = jnp.einsum('bclgn,bcsgn->bcgls', Cr, Br)
    y_diag = jnp.einsum('bcgjls,bcsgjp->bclgjp', CB[:, :, :, None] * Lmat, xdt)
    decay_states = jnp.exp(a_cs[..., -1:] - a_cs)
    states = jnp.einsum('bclgn,bcgjl,bclgjp->bcgjpn', Br, decay_states, xdt)
    chunk_tot = jnp.pad(a_cs[..., -1].transpose(0, 2, 3, 1), ((0, 0), (0, 0), (0, 0), (1, 0)))
    decay_chunk = jnp.exp(segsum(chunk_tot))
    states = jnp.concatenate([jnp.zeros_like(states[:, :1]), states], axis=1)
    new_states = jnp.einsum('bgjzc,bcgjpn->bzgjpn', decay_chunk, states)
    prev_states = new_states[:, :-1]
    y_off = jnp.einsum('bclgn,bcgjpn,bcgjl->bclgjp', Cr, prev_states, jnp.exp(a_cs))
    return (y_diag + y_off).reshape(b, S, H, P)

def mamba2_branch(z, xBC, dt_raw, conv_w, conv_b, dt_bias, a_log, d_skip, ssm_norm):
    b, S, _ = z.shape
    xBC = jax.nn.silu(causal_depthwise_conv(xBC, conv_w, conv_b)).astype(jnp.float32)
    gn = SSM_N_GROUPS * SSM_D_STATE
    xs = xBC[..., :SSM_D_INNER].reshape(b, S, SSM_N_HEADS, SSM_HEAD_DIM)
    Bm = xBC[..., SSM_D_INNER:SSM_D_INNER + gn].reshape(b, S, SSM_N_GROUPS, SSM_D_STATE)
    Cm = xBC[..., SSM_D_INNER + gn:].reshape(b, S, SSM_N_GROUPS, SSM_D_STATE)
    dt = jax.nn.softplus(dt_raw.astype(jnp.float32) + dt_bias.astype(jnp.float32))
    A = -jnp.exp(a_log.astype(jnp.float32))
    y = ssd_chunked(xs, dt, A, Bm, Cm) + d_skip.astype(jnp.float32)[:, None] * xs
    y = y.reshape(b, S, SSM_D_INNER) * jax.nn.silu(z.astype(jnp.float32))
    yg = y.reshape(b, S, SSM_N_GROUPS, SSM_D_INNER // SSM_N_GROUPS)
    yg = yg * lax.rsqrt(jnp.mean(yg * yg, axis=-1, keepdims=True) + EPS)
    y = yg.reshape(b, S, SSM_D_INNER) * ssm_norm.astype(jnp.float32)
    return y.astype(z.dtype)

def dilated_window_group(q, k, v, window, dilation):
    b, S, h, d = q.shape
    r = dilation
    w_sub = window // r
    L = S // r
    nb = -(-L // ATT_BLOCK)
    Lp = nb * ATT_BLOCK

    def to_blocks(t):
        t = t.reshape(b, L, r, h, d).transpose(0, 2, 1, 3, 4)
        t = jnp.pad(t, ((0, 0), (0, 0), (0, Lp - L), (0, 0), (0, 0)))
        return t.reshape(b, r, nb, ATT_BLOCK, h, d)

    def with_prev(t):
        prev = jnp.pad(t[:, :, :-1], ((0, 0), (0, 0), (1, 0), (0, 0), (0, 0), (0, 0)))
        return jnp.concatenate([prev, t], axis=3)

    qb = to_blocks(q)
    kk = with_prev(to_blocks(k))
    vv = with_prev(to_blocks(v))
    s = jnp.einsum('brnqhd,brnkhd->brnhqk', qb, kk) * (d ** -0.5)
    qi = jnp.arange(ATT_BLOCK)[:, None]
    kj = jnp.arange(2 * ATT_BLOCK)[None, :]
    dist = qi + ATT_BLOCK - kj
    band = (dist >= 0) & (dist <= w_sub)
    has_prev = (jnp.arange(nb) > 0)[:, None, None] | (kj >= ATT_BLOCK)[None]
    mask = band[None] & has_prev
    s = jnp.where(mask[None, None, :, None], s, -jnp.inf)
    m = jnp.max(s, axis=-1, keepdims=True)
    p = jnp.exp(s - m)
    den = jnp.sum(p, axis=-1, keepdims=True)
    o = jnp.einsum('brnhqk,brnkhd->brnqhd', p / den, vv)
    lse = (m + jnp.log(den))[..., 0].transpose(0, 1, 2, 4, 3)
    o = o.reshape(b, r, Lp, h, d)[:, :, :L].transpose(0, 2, 1, 3, 4).reshape(b, S, h, d)
    lse = lse.reshape(b, r, Lp, h)[:, :, :L].transpose(0, 2, 1, 3).reshape(b, S, h)
    return o, lse

def dilated_attention_branch(q, k, v):
    outs, lses = [], []
    for gi, (window, dilation) in enumerate(ATT_PATTERNS):
        sl = slice(gi * ATT_HEADS_PER_GROUP, (gi + 1) * ATT_HEADS_PER_GROUP)
        o, lse = dilated_window_group(q[:, :, sl], k[:, :, sl], v[:, :, sl], window, dilation)
        outs.append(o)
        lses.append(lse)
    o = jnp.stack(outs, axis=0)
    wts = jax.nn.softmax(jnp.stack(lses, axis=0), axis=0)
    return jnp.sum(wts[..., None] * o, axis=0)

def first_inputs(seed: int = 0) -> dict:
    key = jax.random.key(seed)
    ks = jax.random.split(key, 20)
    f32 = jnp.float32

    def nrm(k, shape, scale):
        return jax.random.normal(k, shape, f32) * scale

    dt0 = jnp.exp(jax.random.uniform(ks[6], (DEPTH, SSM_N_HEADS), f32,
                                     minval=math.log(1e-3), maxval=math.log(1e-1)))
    return {
        "x": nrm(ks[0], (BATCH, SEQ, D_MODEL), 1.0),
        "norm_mix": 1.0 + nrm(ks[1], (DEPTH, D_MODEL), 0.05),
        "w_in": nrm(ks[2], (DEPTH, D_MODEL, IN_PROJ_DIM), D_MODEL ** -0.5),
        "b_gate": nrm(ks[3], (DEPTH, N_BRANCH * D_MODEL), 0.01),
        "conv_w": nrm(ks[4], (DEPTH, SSM_CONV, SSM_CONV_DIM), SSM_CONV ** -0.5),
        "conv_b": nrm(ks[5], (DEPTH, SSM_CONV_DIM), 0.01),
        "dt_bias": dt0 + jnp.log(-jnp.expm1(-dt0)),
        "a_log": jnp.log(jax.random.uniform(ks[7], (DEPTH, SSM_N_HEADS), f32, minval=1.0, maxval=16.0)),
        "d_skip": 1.0 + nrm(ks[8], (DEPTH, SSM_N_HEADS), 0.1),
        "ssm_norm": 1.0 + nrm(ks[9], (DEPTH, SSM_D_INNER), 0.05),
        "w_ssm_out": nrm(ks[10], (DEPTH, SSM_D_INNER, D_MODEL), SSM_D_INNER ** -0.5),
        "w_att_out": nrm(ks[11], (DEPTH, ATT_OUT_DIM, D_MODEL), ATT_OUT_DIM ** -0.5),
        "w_mix_out": nrm(ks[12], (DEPTH, D_MODEL, D_MODEL), D_MODEL ** -0.5),
        "norm_ffn": 1.0 + nrm(ks[13], (DEPTH, D_MODEL), 0.05),
        "w_ffn_gate": nrm(ks[14], (DEPTH, D_MODEL, D_FF), D_MODEL ** -0.5),
        "w_ffn_up": nrm(ks[15], (DEPTH, D_MODEL, D_FF), D_MODEL ** -0.5),
        "w_ffn_down": nrm(ks[16], (DEPTH, D_FF, D_MODEL), D_FF ** -0.5),
        "norm_final": 1.0 + nrm(ks[17], (D_MODEL,), 0.05),
    }

def first_block(x, norm_mix, w_in, b_gate, conv_w, conv_b, dt_bias, a_log, d_skip, ssm_norm,
              w_ssm_out, w_att_out, w_mix_out, norm_ffn, w_ffn_gate, w_ffn_up, w_ffn_down, norm_final):
    b, S, _ = x.shape
    pos = jnp.arange(S)
    offs = [0]
    for sz in IN_PROJ_SIZES[:-1]:
        offs.append(offs[-1] + sz)
    for l in range(DEPTH):
        h = rmsnorm(x, norm_mix[l])
        proj = h @ w_in[l]
        z, xBC, dt_raw, qkv, gate_logits = jnp.split(proj, offs[1:], axis=-1)

        y_ssm = mamba2_branch(z, xBC, dt_raw, conv_w[l], conv_b[l], dt_bias[l], a_log[l],
                              d_skip[l], ssm_norm[l]) @ w_ssm_out[l]

        qkv = qkv.astype(jnp.float32).reshape(b, S, 3, ATT_N_HEADS, ATT_HEAD_DIM)
        q = rope(qkv[:, :, 0], pos)
        k = rope(qkv[:, :, 1], pos)
        v = qkv[:, :, 2]
        y_att = dilated_attention_branch(q, k, v).reshape(b, S, ATT_OUT_DIM).astype(x.dtype) @ w_att_out[l]

        gates = jax.nn.sigmoid((gate_logits + b_gate[l]).astype(jnp.float32))
        gates = gates.reshape(b, S, N_BRANCH, D_MODEL).astype(x.dtype)
        mixed = gates[:, :, 0] * y_ssm + gates[:, :, 1] * y_att
        x = x + mixed @ w_mix_out[l]

        h = rmsnorm(x, norm_ffn[l])
        x = x + (jax.nn.silu(h @ w_ffn_gate[l]) * (h @ w_ffn_up[l])) @ w_ffn_down[l]
    return rmsnorm(x, norm_final)


DEPTH_2 = 2

N_A_LAYERS = DEPTH_2 // 2
N_B_LAYERS = DEPTH_2 - N_A_LAYERS
A_HEADS = 8
A_HEAD_DIM = D_MODEL // A_HEADS // 2
B_HEADS = 16
B_HEAD_DIM = D_MODEL // B_HEADS
D_FF_2 = 2816
CONV_WIDTH = 3
N_BUCKETS = 32
MAX_DISTANCE = 128
Q_BLOCK = 128
RMS_EPS = 1e-6
SUBLN_EPS = 1e-5
NEG_INF = -1e30


def rms_norm(x, gain, eps=RMS_EPS):
    xf = x.astype(jnp.float32)
    y = xf * lax.rsqrt(jnp.mean(xf * xf, axis=-1, keepdims=True) + eps)
    return (y * gain.astype(jnp.float32)).astype(x.dtype)

def t5_bucket(dist):
    max_exact = N_BUCKETS // 2
    d = jnp.maximum(dist, 0)
    log_ratio = jnp.log(jnp.maximum(d, 1).astype(jnp.float32) / max_exact) / math.log(MAX_DISTANCE / max_exact)
    large = jnp.minimum(max_exact + (log_ratio * (N_BUCKETS - max_exact)).astype(jnp.int32), N_BUCKETS - 1)
    return jnp.where(d < max_exact, d, large)

def lambda_init_fn(layer_idx):
    return 0.8 - 0.6 * math.exp(-0.3 * layer_idx)

def diff_attention(x, w_qkv, w_o, lam_q1, lam_k1, lam_q2, lam_k2, subln_g, rel_bias, lambda_init):
    B, S, _ = x.shape
    qkv = x @ w_qkv
    nq = 2 * A_HEADS * A_HEAD_DIM
    q, k, v = jnp.split(qkv, [nq, 2 * nq], axis=-1)
    q = q.reshape(B, S, A_HEADS, 2, A_HEAD_DIM).astype(jnp.float32) * (A_HEAD_DIM ** -0.5)
    k = k.reshape(B, S, A_HEADS, 2, A_HEAD_DIM).astype(jnp.float32)
    v = v.reshape(B, S, A_HEADS, 2 * A_HEAD_DIM).astype(jnp.float32)
    lam = (jnp.exp(jnp.sum(lam_q1.astype(jnp.float32) * lam_k1.astype(jnp.float32)))
           - jnp.exp(jnp.sum(lam_q2.astype(jnp.float32) * lam_k2.astype(jnp.float32)))
           + lambda_init)
    outs = []
    for i in range(S // Q_BLOCK):
        q0 = i * Q_BLOCK
        k_end = q0 + Q_BLOCK
        dist = jnp.arange(q0, k_end)[:, None] - jnp.arange(k_end)[None, :]
        bias = jnp.moveaxis(rel_bias[t5_bucket(dist)].astype(jnp.float32), -1, 0)
        logits = jnp.einsum('bqhcd,bkhcd->bchqk', q[:, q0:k_end], k[:, :k_end]) + bias[None, None]
        logits = jnp.where(dist >= 0, logits, NEG_INF)
        p = jax.nn.softmax(logits, axis=-1)
        attn = p[:, 0] - lam * p[:, 1]
        outs.append(jnp.einsum('bhqk,bkhe->bqhe', attn, v[:, :k_end]))
    o = jnp.concatenate(outs, axis=1)
    o = rms_norm(o, subln_g, SUBLN_EPS) * (1.0 - lambda_init)
    return o.reshape(B, S, A_HEADS * 2 * A_HEAD_DIM).astype(x.dtype) @ w_o

def shared_kv(h, kv_norm, w_kvf, b_f):
    B, S, _ = h.shape
    kvf = rms_norm(h, kv_norm) @ w_kvf
    k, v, f_logit = jnp.split(kvf, [B_HEADS * B_HEAD_DIM, 2 * B_HEADS * B_HEAD_DIM], axis=-1)
    k = k.reshape(B, S, B_HEADS, B_HEAD_DIM).astype(jnp.float32)
    v = v.reshape(B, S, B_HEADS, B_HEAD_DIM).astype(jnp.float32)
    log_f = jax.nn.log_sigmoid(f_logit.astype(jnp.float32) + b_f.astype(jnp.float32))
    c = jnp.cumsum(log_f, axis=1)
    return k, v, jnp.transpose(c, (0, 2, 1))

def forgetting_attention(x, w_q, w_o, k, v, c):
    B, S, _ = x.shape
    q = (x @ w_q).reshape(B, S, B_HEADS, B_HEAD_DIM).astype(jnp.float32) * (B_HEAD_DIM ** -0.5)
    outs = []
    for i in range(S // Q_BLOCK):
        q0 = i * Q_BLOCK
        k_end = q0 + Q_BLOCK
        dist = jnp.arange(q0, k_end)[:, None] - jnp.arange(k_end)[None, :]
        decay = c[:, :, q0:k_end, None] - c[:, :, None, :k_end]
        logits = jnp.einsum('bqhd,bkhd->bhqk', q[:, q0:k_end], k[:, :k_end]) + decay
        logits = jnp.where(dist >= 0, logits, NEG_INF)
        p = jax.nn.softmax(logits, axis=-1)
        outs.append(jnp.einsum('bhqk,bkhd->bqhd', p, v[:, :k_end]))
    o = jnp.concatenate(outs, axis=1)
    return o.reshape(B, S, B_HEADS * B_HEAD_DIM).astype(x.dtype) @ w_o

def conv_ffn(x, w_in, conv_w, conv_b, w_out):
    u = x @ w_in
    u = lax.conv_general_dilated(u, conv_w[:, None, :].astype(u.dtype), window_strides=(1,),
                                 padding=[(CONV_WIDTH - 1, 0)],
                                 dimension_numbers=('NWC', 'WIO', 'NWC'),
                                 feature_group_count=2 * D_FF_2) + conv_b
    gate, val = jnp.split(u, 2, axis=-1)
    return (jax.nn.gelu(gate) * val) @ w_out

def second_inputs(seed: int = 0) -> dict:
    key = jax.random.key(seed)
    ks = iter(jax.random.split(key, 32))
    nrm = lambda shape, s: jax.random.normal(next(ks), shape, jnp.float32) * s
    gain = lambda shape: 1.0 + nrm(shape, 0.05)
    D, F = D_MODEL, D_FF_2
    return {
        "x": nrm((BATCH, SEQ, D), 1.0),
        "rel_bias": nrm((N_BUCKETS, A_HEADS), 0.2),
        "a_norm_pre": gain((N_A_LAYERS, D)),
        "a_norm_post": gain((N_A_LAYERS, D)),
        "a_w_qkv": nrm((N_A_LAYERS, D, 3 * 2 * A_HEADS * A_HEAD_DIM), D ** -0.5),
        "a_lam_q1": nrm((N_A_LAYERS, A_HEAD_DIM), 0.1),
        "a_lam_k1": nrm((N_A_LAYERS, A_HEAD_DIM), 0.1),
        "a_lam_q2": nrm((N_A_LAYERS, A_HEAD_DIM), 0.1),
        "a_lam_k2": nrm((N_A_LAYERS, A_HEAD_DIM), 0.1),
        "a_subln": gain((N_A_LAYERS, 2 * A_HEAD_DIM)),
        "a_w_o": nrm((N_A_LAYERS, 2 * A_HEADS * A_HEAD_DIM, D), D ** -0.5),
        "kv_norm": gain((D,)),
        "w_kvf": jnp.concatenate([nrm((D, 2 * B_HEADS * B_HEAD_DIM), D ** -0.5),
                                  nrm((D, B_HEADS), 0.1 * D ** -0.5)], axis=-1),
        "b_f": 3.0 + nrm((B_HEADS,), 0.1),
        "b_norm_pre": gain((N_B_LAYERS, D)),
        "b_norm_post": gain((N_B_LAYERS, D)),
        "b_w_q": nrm((N_B_LAYERS, D, B_HEADS * B_HEAD_DIM), D ** -0.5),
        "b_w_o": nrm((N_B_LAYERS, B_HEADS * B_HEAD_DIM, D), D ** -0.5),
        "ffn_norm_pre": gain((DEPTH_2, D)),
        "ffn_norm_post": gain((DEPTH_2, D)),
        "ffn_w_in": nrm((DEPTH_2, D, 2 * F), D ** -0.5),
        "ffn_conv_w": nrm((DEPTH_2, CONV_WIDTH, 2 * F), CONV_WIDTH ** -0.5),
        "ffn_conv_b": nrm((DEPTH_2, 2 * F), 0.02),
        "ffn_w_out": nrm((DEPTH_2, F, D), F ** -0.5),
    }

def second_block(x, rel_bias, a_norm_pre, a_norm_post, a_w_qkv, a_lam_q1, a_lam_k1, a_lam_q2, a_lam_k2,
              a_subln, a_w_o, kv_norm, w_kvf, b_f, b_norm_pre, b_norm_post, b_w_q, b_w_o,
              ffn_norm_pre, ffn_norm_post, ffn_w_in, ffn_conv_w, ffn_conv_b, ffn_w_out):
    h = x
    for l in range(DEPTH_2):
        if l < N_A_LAYERS:
            a = diff_attention(rms_norm(h, a_norm_pre[l]), a_w_qkv[l], a_w_o[l],
                               a_lam_q1[l], a_lam_k1[l], a_lam_q2[l], a_lam_k2[l],
                               a_subln[l], rel_bias, lambda_init_fn(l))
            h = h + rms_norm(a, a_norm_post[l])
        else:
            if l == N_A_LAYERS:
                k_sh, v_sh, c_sh = shared_kv(h, kv_norm, w_kvf, b_f)
            j = l - N_A_LAYERS
            a = forgetting_attention(rms_norm(h, b_norm_pre[j]), b_w_q[j], b_w_o[j], k_sh, v_sh, c_sh)
            h = h + rms_norm(a, b_norm_post[j])
        f = conv_ffn(rms_norm(h, ffn_norm_pre[l]), ffn_w_in[l], ffn_conv_w[l], ffn_conv_b[l], ffn_w_out[l])
        h = h + rms_norm(f, ffn_norm_post[l])
    return h


def setup_inputs(seed=0):
    out = dict(first_inputs(seed))
    for name, value in second_inputs(seed + 1).items():
        if name != "x":
            out[name + "_2"] = value
    return out


def reference(
    x, norm_mix, w_in, b_gate, conv_w, conv_b, dt_bias, a_log, d_skip, ssm_norm, w_ssm_out,
    w_att_out, w_mix_out, norm_ffn, w_ffn_gate, w_ffn_up, w_ffn_down, norm_final, rel_bias_2,
    a_norm_pre_2, a_norm_post_2, a_w_qkv_2, a_lam_q1_2, a_lam_k1_2, a_lam_q2_2, a_lam_k2_2,
    a_subln_2, a_w_o_2, kv_norm_2, w_kvf_2, b_f_2, b_norm_pre_2, b_norm_post_2, b_w_q_2,
    b_w_o_2, ffn_norm_pre_2, ffn_norm_post_2, ffn_w_in_2, ffn_conv_w_2, ffn_conv_b_2,
    ffn_w_out_2,
):
    x = first_block(
        x, norm_mix, w_in, b_gate, conv_w, conv_b, dt_bias, a_log, d_skip, ssm_norm, w_ssm_out,
        w_att_out, w_mix_out, norm_ffn, w_ffn_gate, w_ffn_up, w_ffn_down, norm_final,
    )
    return second_block(
        x, rel_bias_2, a_norm_pre_2, a_norm_post_2, a_w_qkv_2, a_lam_q1_2, a_lam_k1_2,
        a_lam_q2_2, a_lam_k2_2, a_subln_2, a_w_o_2, kv_norm_2, w_kvf_2, b_f_2, b_norm_pre_2,
        b_norm_post_2, b_w_q_2, b_w_o_2, ffn_norm_pre_2, ffn_norm_post_2, ffn_w_in_2,
        ffn_conv_w_2, ffn_conv_b_2, ffn_w_out_2,
    )


_drawn_inputs = setup_inputs


def setup_inputs(seed=0):
    import zlib

    import numpy as np

    out = dict(_drawn_inputs(seed))
    spreads = {}
    factors = {'b_gate': 8.0,
     'conv_b': 3.439,
     'a_lam_q1_2': 3.432,
     'a_lam_k1_2': 2.911,
     'b_f_2': 21.8,
     'b_norm_pre_2': 4.758}
    for name, (base, spread) in spreads.items():
        noise = np.random.default_rng([zlib.crc32(name.encode()), seed]).standard_normal(out[name].shape)
        drawn = base * np.exp(spread * noise) if base else spread * noise
        out[name] = __import__('jax').numpy.asarray(drawn.astype(out[name].dtype))
    for name, factor in factors.items():
        out[name] = (out[name] * factor).astype(out[name].dtype)
    return out
```

```python
import math
from contextlib import ExitStack

import numpy as np
import concourse.bass as bass
from concourse import mybir

F32 = mybir.dt.float32
F32R = mybir.dt.float32r
BF16 = mybir.dt.bfloat16
ACT = mybir.ActivationFunctionType
ALU = mybir.AluOpType
AX = mybir.AxisListType

P = 128
S = 512
NB = S // P
D = 1024
DC = D // P
PANEL = 256
SLAB = 4
RAW = 4
SPL = 2
EPS, SUB_EPS = 1e-6, 1e-5
NEG = -1e30

DI, HD, NG, NS, KCONV = 2048, 64, 4, 128, 4
NH = DI // HD
HG = NH // NG
GW = DI // NG
XBC = DI + 2 * NG * NS
AH, AG = 4, 3
ADIM = 128
QKV0 = DI + XBC + NH
GATE0 = QKV0 + 3 * AH * AG * ADIM
DFF = 2816
FT = DFF // P
FP = DFF // PANEL
H2 = 8
PAIRS = 4
BH = 16
BUCKETS = 32
LINE = S + P
LAM0 = 0.8 - 0.6 * math.exp(0.0)

VEC = [("norm_mix", 8), ("b_gate", 16), ("conv_w", 96), ("conv_b", 24), ("norm_ffn", 8), ("norm_final", 8),
       ("a_norm_pre_2", 8), ("a_norm_post_2", 8), ("a_subln_2", 1), ("kv_norm_2", 8), ("b_norm_pre_2", 8),
       ("b_norm_post_2", 8), ("ffn_norm_pre_2", 16), ("ffn_norm_post_2", 16), ("ffn_conv_w_2", 264),
       ("ffn_conv_b_2", 88)]
COL, NCOL = {}, 0
for _n, _w in VEC:
    COL[_n] = NCOL
    NCOL += _w

K512, K1024, K2816 = (2, 2), (4, 4), (4, 4, 4, 4, 4, 2)
STREAM = [("C", 2, K1024), ("B", 2, K1024), ("dt", 1, K1024), (("xs", 0), 2, K1024)]
for _g in range(NG):
    STREAM.append((("z", _g), 2, K1024))
    if _g:
        STREAM.append((("so", _g - 1), 4, K512))
    if _g < NG - 1:
        STREAM.append((("xs", _g + 1), 2, K1024))
QKV1 = lambda j: [(n, j, gi) for gi in range(AG) for n in ("q1", "k1", "v1")]
STREAM += [(k, 1, K1024) for k in QKV1(0)[:2]] + [(("so", 3), 4, K512)]
STREAM += [(k, 1, K1024) for k in QKV1(0)[2:] + QKV1(1)]
STREAM += [("gates", 8, K1024), ("ao", 4, K512), ("mix", 4, K1024), ("ffn1", 2 * FP, K1024), ("down1", 4, K2816)]
STREAM += [((n, j), 1, K1024) for j in range(PAIRS) for n in ("q2", "k2", "v2")]
STREAM += [("awo", 4, K1024), (("fin", 0), 2 * FP, K1024), (("fout", 0), 4, K2816), ("f", 1, K1024)]
STREAM += [((n, j), 1, K1024) for j in range(PAIRS) for n in ("q3", "k3", "v3")]
STREAM += [("bwo", 4, K1024), (("fin", 1), 2 * FP, K1024), (("fout", 1), 4, K2816)]
PAN, SLB, SPLIT, NPAN = {}, {}, {}, {}
_p = _s = 0
for _k, _n, _c in STREAM:
    PAN[_k], SLB[_k], SPLIT[_k], NPAN[_k] = _p, _s, _c, _n
    _p += _n
    _s += _n * len(_c)
SLABS = _s


def slab_end(key, panel):
    return SLB[key] + (panel + 1) * len(SPLIT[key])


SCAN = []
for _g in range(NG):
    _u = 4 * _g
    _z, _so, _xs = ("z", _g), ("so", _g - 1), ("xs", _g + 1)
    SCAN += [("mm", _z, 0)] + [("Cp", _u - 2)] * (_g > 0) + [("xt", _u + 2), ("xt", _u + 3), ("G", _g), ("A", _u)]
    SCAN += [("N", _u - 1)] * (_g > 0) + [("epi", _z, 0), ("mm", _z, 1)] + [("Cp", _u - 1)] * (_g > 0) + [("A", _u + 1), ("epi", _z, 1)]
    for _h in range(4):
        if _g:
            SCAN.append(("mm", _so, _h))
        SCAN += ([("Bp", _u)], [("A", _u + 2), ("N", _u)], [("Bp", _u + 1)], [("A", _u + 3), ("N", _u + 1)])[_h]
        if _g:
            SCAN.append(("epi", _so, _h))
    _next = [(_xs, 0), (_xs, 1)] if _g < NG - 1 else [(k, 0) for k in QKV1(0)[:2]]
    SCAN += [("mm", *_next[0]), ("Cp", _u), ("Bp", _u + 2), ("Cp", _u + 1)]
    if _g < NG - 1:
        SCAN.append(("epi", *_next[0]))
    SCAN += [("mm", *_next[1]), ("N", _u + 2), ("Bp", _u + 3)]
    if _g < NG - 1:
        SCAN += [("xt", _u + 4), ("xt", _u + 5), ("epi", *_next[1])]
    else:
        SCAN += [("Cp", _u + 2), ("N", _u + 3), ("Cp", _u + 3), ("epi", *_next[0]), ("epi", *_next[1])]
for _h in range(4):
    SCAN += [("mm", ("so", 3), _h), ("epi", ("so", 3), _h)]
USE0 = {t: n for n, t in enumerate([("xt", 0), ("xt", 1)] + [t for t in SCAN if t[0] in ("xt", "Cp")])}
USE1, READ1, LAST1 = {}, {}, {}
_last = None
for _t in SCAN:
    if _t[0] == "G" or _t[0] == "A" or (_t[0] == "Bp" and _t[1] % NB < NB - 1):
        USE1[_t] = len(USE1)
        LAST1[_t] = _last
        _last = _t
        if _t[0] != "Bp":
            READ1[_t] = len(READ1)
YSTEPS = [0]
for _u in range(16):
    YSTEPS.append(YSTEPS[-1] + (3 if _u % NB == 0 else 5))
STSTEPS = [0]
for _u in range(16):
    STSTEPS.append(STSTEPS[-1] + (1, 2, 2, 0)[_u % NB])

ATT1 = []
_fill = [("half", k, 0, h) for k in QKV1(1) for h in range(2)], [("half", "gates", n, h) for n in range(8) for h in range(2)]
for _j in range(2):
    fill = list(_fill[_j])
    for _u in range(8 * _j, 8 * _j + 8):
        ATT1.append(("S", _u))
        if _u:
            ATT1.append(("X", _u - 1))
        for _part in ("T", "V"):
            take = 2 if len(fill) > 2 * (8 * _j + 8 - _u) - (_part == "V") else 1
            for t in fill[:take]:
                ATT1.append(t)
                if t[3] == 1:
                    ATT1.append(("epi", t[1], t[2]))
            fill = fill[take:]
            ATT1.append((_part, _u))
ATT1.append(("X", 15))


def w1(qb):
    return (qb + 1) * P, P if qb == 0 else 2 * P


def nblk(qb):
    return 2 * (qb + 1) + (1 if qb == 0 else 2)


TB, TA, TV = [0], [0], [0]
for _u in range(16):
    _n = -(-nblk(_u % 4) // 4)
    TB.append(TB[-1] + _n)
    TA.append(TA[-1] + (_n + 1) // 2)
    TV.append(TV[-1] + _n // 2)


def order2(names):
    out = [("S", 0), ("S", 1), ("M", 0), ("D", 0)]
    late = []
    for j in range(PAIRS):
        fill = [("half", (n, j + 1), 0, h) for n in names for h in range(2)] if j < PAIRS - 1 else []
        for u in range(8 * j, 8 * j + 8):
            if u < 31:
                out.append(("M", u + 1))
            out += [("W", u - 1)] * (u > 0 and names[0] == "q3") + [("T", u)]
            if u < 30:
                out.append(("S", u + 2))
            out += [("W", u - 1)] * (u > 0 and names[0] != "q3")
            if u < 31:
                out.append(("D", u + 1))
            out += late
            late = []
            out.append(("V", u))
            if u:
                out.append(("X", u - 1))
            if fill:
                t = fill.pop(0)
                out.append(t)
                if t[3] == 1:
                    late = [("epi", t[1], t[2])]
    return out + [("W", 31), ("X", 31)]
WEIGHTS = ["w_in", "w_ssm_out", "w_att_out", "w_mix_out", "w_ffn_gate", "w_ffn_up", "w_ffn_down", "a_w_qkv_2", "a_w_o_2", "w_kvf_2",
           "b_w_q_2", "b_w_o_2", "ffn_w_in_2_0", "ffn_w_in_2_1", "ffn_w_out_2_0", "ffn_w_out_2_1"]


def build(nc, I, out):
    ctx = ExitStack()
    with ctx:
        def sem(n):
            return ctx.enter_context(nc.semaphore(n))

        class Region:
            def __init__(self, at, end):
                self.at, self.end = at, end

            def put(self, n, shape, dt=F32):
                size = -(-int(np.prod(shape[1:])) * (2 if dt == BF16 else 4) // 32) * 32
                assert self.at + size <= self.end, (n, self.at + size - self.end)
                t = nc.alloc_sbuf_tensor_at(n, list(shape), dt, offset=self.at)
                self.at += size
                return t

        KB = 1024
        BASE = -(-nc.sbuf_base // 64) * 64
        TOP = nc.sbuf_usable_end // 64 * 64
        r = Region(BASE, TOP)
        raw = [r.put(f"raw{i}", [P, SLAB, PANEL]) for i in range(RAW)]
        whi = [r.put(f"whi{i}", [P, SLAB, PANEL], F32R) for i in range(SPL)]
        wlo = [r.put(f"wlo{i}", [P, SLAB, PANEL], F32R) for i in range(SPL)]
        opA_hi = r.put("opA_hi", [P, DC, S], F32R)
        opA_lo = r.put("opA_lo", [P, DC, S], F32R)
        vec = r.put("vec", [P, NCOL])
        ident = r.put("ident", [P, P])
        zero = r.put("zero", [P, 1])
        ones = r.put("ones", [P, P])
        tri = r.put("tri", [P, P])
        norm_tmp = r.at
        sq = r.put("sq", [P, 2, S])
        acc = r.put("acc", [P, S])
        diag = r.put("diag", [P, NB, P])
        rstd_bc = r.put("rstd_bc", [P, S])
        std = r.put("std", [P, NB])
        rstd_col = r.put("rstd_col", [P, NB])
        lamv = r.put("lamv", [P, 4, 64])
        lamt = r.put("lamt", [P, 2, 64])
        lams = r.put("lams", [P, 8])
        subg = r.put("subg", [P, 1])
        dsk = r.put("dsk", [P, NH])
        dtv = r.put("dtv", [NH, 4])
        bfv = r.put("bfv", [BH, 2])
        mask1 = r.put("mask1", [P, 2 * S + 2 * P], BF16)
        ident_bf = r.put("ident_bf", [P, P], BF16)
        A0 = r.at
        XT_AT = TOP - 16 * KB
        XT = Region(XT_AT, TOP).put("XT", [P, DC, S])
        r = Region(A0, XT_AT)
        oneh = r.put("oneh", [BUCKETS, LINE])
        relb = r.put("relb", [BUCKETS, H2])
        relw = r.put("relw", [BUCKETS, H2, P])
        future = r.put("future", [P, LINE])
        line = r.put("line", [P, H2, LINE])
        mask_in = r.put("mask_in", [P, 2 * S + 2 * P])
        r = Region(A0, TOP)
        yT_hi = r.put("yT_hi", [P, 4, S], F32R)
        yT_lo = r.put("yT_lo", [P, 4, S], F32R)
        y_ssm = r.put("y_ssm", [P, DC, S])
        AFTER_Y = r.at
        xs_tok = r.put("xs_tok", [P, 2, NB, GW])
        zbuf = r.put("zbuf", [P, NB, GW])
        bcf = r.put("bcf", [P, 2 * NG, S])
        btok = r.put("btok", [P, NB, P])
        tokc = r.put("tokc", [P, NB, 4, NH])
        acs_row = r.put("acs_row", [P, 2, HG, P])
        M_AT = r.at
        M = r.put("M", [P, 2, HG, P])
        xdt = r.put("xdt", [P, 2, GW])
        xdd_at = r.at
        xdd = r.put("xdd", [P, 2, GW])
        state = r.put("state", [P, GW])
        y_at = r.at
        yb = r.put("yb", [P, GW])
        yt = r.put("yt", [P, GW])
        yoffb = r.put("yoffb", [P, GW])
        yn = r.put("yn", [P, 3, GW])
        cbm = r.put("cbm", [P, 2, P])
        gain = r.put("gain", [P, 2, GW])
        etot = r.put("etot", [P, 2, HG])
        ystat = r.put("ystat", [P, 2, 4])
        cu = r.put("cu", [P, 2, S + KCONV - 1])
        cacc = Region(norm_tmp, norm_tmp + 4 * KB).put("cacc", [P, 2, S])
        xsf = Region(norm_tmp + 4 * KB, norm_tmp + 8 * KB).put("xsf", [P, 2, S])
        pack = Region(y_at, TOP).put("pack", [P, S])
        r = Region(A0, A0 + 16 * KB)
        dx, da, de, dr, dz, dz2, dq, ddt = [r.put(n, [NH, S]) for n in ("dx", "da", "de", "dr", "dz", "dz2", "dq", "ddt")]
        r = Region(xdd_at, xdd_at + 4 * KB)
        dacs, ddec = r.put("dacs", [NH, S]), r.put("ddec", [NH, S])
        r = Region(A0, TOP)
        o1_hi = r.put("o1_hi", [P, AH, S], F32R)
        o1_lo = r.put("o1_lo", [P, AH, S], F32R)
        assert r.at == A0 + 16 * KB
        r.at = AFTER_Y
        q1, k1, v1, pair_at = [], [], [], []
        for j in range(2):
            pair_at.append(r.at)
            q1.append(r.put(f"q1_{j}", [P, 2 * AG, S]))
            k1.append(r.put(f"k1_{j}", [P, 2 * AG, S]))
            v1.append(r.put(f"v1_{j}", [P, NB, AG * PANEL]))
        prob = r.put("prob", [P, 2 * S + 2 * P])
        probT = r.put("probT", [P, 10, P])
        osb = r.put("osb", [P, 2, P])
        cosr = r.put("cosr", [P, S])
        sinr = r.put("sinr", [P, S])
        rsin = r.put("rsin", [P, 2, S])
        astat = r.put("astat", [P, 2, 8])
        r = Region(pair_at[0], pair_at[1])
        mixed = r.put("mixed", [P, DC, S])
        gate1 = r.put("gate1", [P, DC, S])
        r = Region(pair_at[1], XT_AT)
        mix_hi = r.put("mix_hi", [P, DC, S], F32R)
        mix_lo = r.put("mix_lo", [P, DC, S], F32R)
        gtmp = Region(norm_tmp, norm_tmp + 4 * KB).put("gtmp", [P, 2, S])
        r = Region(A0, XT_AT)
        hid_hi = r.put("hid_hi", [P, FT, S], F32R)
        hid_lo = r.put("hid_lo", [P, FT, S], F32R)
        F_AT = r.at
        fu = r.put("fu", [P, 4, S + 2])
        facc = r.put("facc", [P, 4, S])
        fg = r.put("fg", [P, 2, S])
        branch = Region(F_AT, XT_AT).put("branch", [P, DC, S])
        r = Region(A0, XT_AT)
        opB_hi = r.put("opB_hi", [P, DC, S], F32R)
        opB_lo = r.put("opB_lo", [P, DC, S], F32R)
        tbias = Region(A0, A0 + 16 * KB).put("tbias", [P, H2, S])
        q2 = [r.put(f"q2_{j}", [P, 2, S]) for j in range(2)]
        k2 = [r.put(f"k2_{j}", [P, 2, S]) for j in range(2)]
        v2 = [r.put(f"v2_{j}", [P, NB, PANEL]) for j in range(2)]
        oT = r.put("oT", [P, DC, S])
        sc = r.put("sc", [P, 2, 2, S])
        pT = r.put("pT", [P, 2, NB, P])
        dif = Region(A0 + 16 * KB, A0 + 20 * KB).put("dif", [P, 2, S])
        osb2 = r.put("osb2", [P, 2, P])
        osq = r.put("osq", [P, P])
        bstat = r.put("bstat", [P, 4, 16])
        ccol = r.put("ccol", [P, NB, BH])
        negc = r.put("negc", [P, 2, 2, S])
        r = Region(A0 + 64 * KB, A0 + 80 * KB)
        fx, fa, fe, fr, fz, fz2, fq, fc = [r.put(n, [BH, S]) for n in ("fx", "fa", "fe", "fr", "fz", "fz2", "fq", "fc")]
        PS = ctx.enter_context(nc.psum_tensor("PS", [P, 4, S], F32))
        AUX = ctx.enter_context(nc.psum_tensor("AUX", [P, 4, S], F32))
        x_in = [sem(f"x_in{n}") for n in range(4)]
        const_in = sem("const_in")
        w_loaded = [sem(f"w_loaded{n}") for n in range(RAW)]
        slab_go, w_high, slab_split = sem("slab_go"), sem("w_high"), sem("slab_split")
        zero_ready = sem("zero_ready")
        slab_done = sem("slab_done")
        evicted = sem("evicted")
        op_hi, op_ready = sem("op_hi"), sem("op_ready")
        sq_ready, acc_ready = sem("sq_ready"), sem("acc_ready")
        ss_done, std_ready, rstd_ready = sem("ss_done"), sem("std_ready"), sem("rstd_ready")
        diag_ready, bc_done, bc_ready = sem("diag_ready"), sem("bc_done"), sem("bc_ready")
        relw_ready, line_mm, line_ready, bias_out, tbias_in = (sem(n) for n in ("relw_ready", "line_mm", "line_ready", "bias_out", "tbias_in"))
        pads = sem("pads")
        conv_t0, conv_tap, xbc_ready = sem("conv_t0"), sem("conv_tap"), sem("xbc_ready")
        sp_act, sp_step = sem("sp_act"), sem("sp_step")
        a_neg, pack_act, pack_tr, tokc_ready, acs_out = (sem(n) for n in ("a_neg", "pack_act", "pack_tr", "tokc_ready", "acs_out"))
        acs_in = [sem(f"acs_in{n}") for n in range(2)]
        gain_in = [sem(f"gain_in{n}") for n in range(2)]
        aux0_done, aux0_read, aux1_done, aux1_read = (sem(n) for n in ("aux0_done", "aux0_read", "aux1_done", "aux1_read"))
        decay_step, decay_exp, m_step, xdt_ready, xdd_ready = (sem(n) for n in ("decay_step", "decay_exp", "m_step", "xdt_ready", "xdd_ready"))
        ydiag_done, yoff_done, y_step, y_stat, y_rstd, yn_ready, y_hi = (sem(n) for n in ("ydiag_done", "yoff_done", "y_step", "y_stat", "y_rstd", "yn_ready", "y_hi"))
        state_step, z_ready = sem("state_step"), sem("z_ready")
        rope_in, rope_scaled, rope_done = sem("rope_in"), sem("rope_scaled"), sem("rope_done")
        s1_done, max1, negmax1, exp1, den1, rden1 = (sem(n) for n in ("s1_done", "max1", "negmax1", "exp1", "den1", "rden1"))
        tr1_done, pT1_act, pT1_dve, pv1_done, o1_read, ot1_done, o1_high, o1_ready = (
            sem(n) for n in ("tr1_done", "pT1_act", "pT1_dve", "pv1_done", "o1_read", "ot1_done", "o1_high", "o1_ready"))
        gate_sig, gate_mul, mix_sum, mix_high, mix_ready = (sem(n) for n in ("gate_sig", "gate_mul", "mix_sum", "mix_high", "mix_ready"))
        fgate, fprod, hid_high, hid_ready = (sem(n) for n in ("fgate", "fprod", "hid_high", "hid_ready"))
        fconv_t0, fconv_tap = sem("fconv_t0"), sem("fconv_tap")
        res_scaled, res_ready = sem("res_scaled"), sem("res_ready")
        lam_step, lam_act = sem("lam_step"), sem("lam_act")
        s2_done, sc_ready, max2, negmax2, exp2, r2_step = (sem(n) for n in ("s2_done", "sc_ready", "max2", "negmax2", "exp2", "r2_step"))
        tr2_done, pT2_act, pT2_dve, pv2_done, o2_stat, o2_rstd, o2_read, ot2_done, oT_ready = (
            sem(n) for n in ("tr2_done", "pT2_act", "pT2_dve", "pv2_done", "o2_stat", "o2_rstd", "o2_read", "ot2_done", "oT_ready"))
        c_out, c_tr, ccol_ready = sem("c_out"), sem("c_tr"), sem("ccol_ready")
        negc_in = [sem(f"negc_in{n}") for n in range(2)]
        stored = sem("stored")

        acs_dram = nc.dram_tensor("acs_dram", (NH, S), F32, kind="Internal").ap()
        c_dram = nc.dram_tensor("c_dram", (BH, S), F32, kind="Internal").ap()
        bias_dram = nc.dram_tensor("bias_dram", (H2, P, LINE), F32, kind="Internal").ap()

        W = {n: I[n].rearrange("(c p) n -> p c n", p=P) for n in WEIGHTS}
        xT = I["xT"]
        N_CONST = 12

        def wait(eng, s, v):
            if not isinstance(v, int) or v > 0:
                eng.wait_ge(s, v)

        def source(key, panel, i):
            name = key if isinstance(key, str) else key[0]
            a = None if isinstance(key, str) else key[1]
            flat = (panel + 2 * i) * PANEL
            twin = panel % 2, (panel // 2 + i) * PANEL
            if name in ("C", "B", "xs", "z"):
                first = {"C": DI + DI + NG * NS, "B": DI + DI, "xs": DI + GW * (a or 0), "z": GW * (a or 0)}[name]
                return W["w_in"], 0, first + flat, PANEL
            if name == "dt":
                return W["w_in"], 0, DI + XBC, NH
            if name in ("q1", "k1", "v1"):
                part = ("q1", "k1", "v1").index(name)
                return W["w_in"], 0, QKV0 + part * AH * AG * ADIM + (key[2] * AH + 2 * a) * ADIM, PANEL
            if name == "gates":
                return W["w_in"], 0, GATE0 + twin[0] * D + twin[1], PANEL
            if name == "so":
                return W["w_ssm_out"], 4 * a, flat, PANEL
            if name == "ffn1":
                return W[("w_ffn_gate", "w_ffn_up")[twin[0]]], 0, twin[1], PANEL
            if name == "fin":
                return W[f"ffn_w_in_2_{a}"], 0, twin[0] * DFF + twin[1], PANEL
            if name in ("q2", "k2", "v2"):
                return W["a_w_qkv_2"], 0, ("q2", "k2", "v2").index(name) * D + a * PANEL, PANEL
            if name in ("k3", "v3"):
                return W["w_kvf_2"], 0, ("k3", "v3").index(name) * D + a * PANEL, PANEL
            if name == "q3":
                return W["b_w_q_2"], 0, a * PANEL, PANEL
            if name == "f":
                return W["w_kvf_2"], 0, 2 * D, BH
            return W[{"ao": "w_att_out", "mix": "w_mix_out", "down1": "w_ffn_down", "awo": "a_w_o_2", "bwo": "b_w_o_2",
                      "fout": f"ffn_w_out_2_{a}"}[name]], 0, flat, PANEL

        def psum_fm(key, panel, m):
            return PS[:, 2 * ((PAN[key] + panel) % 2) + m, :]

        def psum_tm(key, panel):
            b = 2 * ((PAN[key] + panel) % 2)
            return PS[:, b:b + 2, :].rearrange("p b (t n) -> p (b t) n", n=PANEL)

        TOKEN_MAJOR = ("z", "v1", "v2", "v3")
        block = ctx.enter_context(nc.Block())

        @block.sync
        def _(sp):
            def load_x(n):
                sp.dma_start(XT[:, 2 * n:2 * n + 2, :], xT.rearrange("(c p) t -> p c t", p=P)[:, 2 * n:2 * n + 2, :]).then_inc(x_in[n], 16)

            def fetch(key, panel, i=0):
                w, c0, col, n = source(key, panel, i)
                for k, chunks in enumerate(SPLIT[key]):
                    s = SLB[key] + panel * len(SPLIT[key]) + k
                    wait(sp, slab_split, s + 2 * len(SPLIT[key]) * i - RAW + 1)
                    cols = slice(col, col + n) if isinstance(col, int) else bass.ds(col, n)
                    sp.dma_start(raw[s % RAW][:, 0:chunks, 0:n], w[:, c0:c0 + chunks, cols]).then_inc(w_loaded[s % RAW], 16)
                    c0 += chunks

            for n in range(4):
                load_x(n)
            for key, n, _ in STREAM:
                if n < 8 and key not in ("down1", ("fout", 0), ("fout", 1)):
                    for panel in range(n):
                        fetch(key, panel)
                else:
                    with sp.Fori(0, n // 2) as i:
                        fetch(key, 0, i)
                        fetch(key, 1, i)
            for c in range(DC):
                sp.wait_ge(res_ready, 4 * DC + c + 1)
                sp.dma_start(out[c * P:(c + 1) * P, :], XT[:, c, :]).then_inc(stored, 16)
            sp.wait_ge(stored, 16 * DC)

        @block.gpsimd
        def _(pool):
            def split(s, i):
                slot, raw_slot = s % SPL, s % RAW
                wait(pool, w_loaded[raw_slot], 16 * (s // RAW + i + 1))
                wait(pool, slab_done, s + RAW * i - SPL + 1)
                pool.sem_inc(slab_go, 1)
                nc.gpsimd.tensor_tensor(whi[slot][:], raw[raw_slot][:], zero[:, 0:1].unsqueeze(2).broadcast_to([P, SLAB, PANEL]),
                                        ALU.add).then_inc(w_high, 1)
                wait(pool, w_high, s + RAW * i + 1)
                nc.gpsimd.tensor_tensor(wlo[slot][:], raw[raw_slot][:], whi[slot][:].bitcast(F32), ALU.subtract).then_inc(slab_split, 1)

            nc.gpsimd.memset(zero[:], 0.0).then_inc(zero_ready, 1)
            pool.wait_ge(zero_ready, 1)
            for s in range(RAW):
                split(s, 0)
            with pool.Fori(0, SLABS // RAW - 1) as i:
                for s in range(RAW):
                    split(RAW + s, i)
            for s in range(SLABS // RAW * RAW, SLABS):
                split(s, 0)

        @block.tensor
        def _(pe):
            def operand(key):
                name = key if isinstance(key, str) else key[0]
                return {"so": (yT_hi, yT_lo), "ao": (o1_hi, o1_lo), "mix": (mix_hi, mix_lo), "down1": (hid_hi, hid_lo),
                        "fout": (hid_hi, hid_lo), "q3": (opB_hi, opB_lo)}.get(name, (opA_hi, opA_lo))

            FIRST_USE = {"C": (op_ready, 0), "ffn1": (op_ready, 8), ("q2", 0): (op_ready, 16), "awo": (op_ready, 24),
                         ("fin", 0): (op_ready, 32), "f": (op_ready, 40), ("q3", 0): (op_ready, 48), "bwo": (op_ready, 56),
                         ("fin", 1): (op_ready, 64), "mix": (mix_ready, 0), "down1": (hid_ready, 0),
                         ("fout", 0): (hid_ready, FT), ("fout", 1): (hid_ready, 2 * FT)}

            def slab(key, panel, k, i=0):
                name = key if isinstance(key, str) else key[0]
                hi, lo = operand(key)
                p = PAN[key] + panel
                nk = len(SPLIT[key])
                s = SLB[key] + panel * nk + k
                if k == 0:
                    wait(pe, evicted, 2 * (p + 2 * i) - 2)
                    if name == "so" and panel == 0:
                        pe.wait_ge(aux0_read, USE0[("Cp", 4 * key[1] + 3)] + 1)
                    if name == "ao" and panel == 0:
                        pe.wait_ge(o1_ready, 16)
                wait(pe, slab_split, s + 2 * nk * i + 1)
                wh, wl = whi[s % SPL], wlo[s % SPL]
                c0 = sum(SPLIT[key][:k])
                total = sum(SPLIT[key])
                if name in TOKEN_MAJOR:
                    for t in range(NB):
                        o = psum_tm(key, panel)[:, t, :]
                        for c in range(SPLIT[key][k]):
                            xh, xl = hi[:, c0 + c, t * P:(t + 1) * P], lo[:, c0 + c, t * P:(t + 1) * P]
                            for n, (a, b) in enumerate(((xh, wh), (xl, wh), (xh, wl))):
                                last = nc.tensor.matmul(o, a, b[:, c, :], start=t % 2 == 0 and c0 + c + n == 0,
                                                        stop=c0 + c == total - 1 and n == 2, skip_group_check=True)
                else:
                    for c in range(SPLIT[key][k]):
                        if panel == 0 and key in FIRST_USE:
                            ready, base = FIRST_USE[key]
                            pe.wait_ge(ready, base + c0 + c + 1)
                        for m in range(1 if name in ("dt", "f") else 2):
                            ah, al = wh[:, c, m * P:(m + 1) * P], wl[:, c, m * P:(m + 1) * P]
                            for n, (a, b) in enumerate(((ah, hi), (ah, lo), (al, hi))):
                                last = nc.tensor.matmul(psum_fm(key, panel, m), a, b[:, c0 + c, :], start=c0 + c + n == 0,
                                                        stop=c0 + c == total - 1 and n == 2)
                last.then_inc(slab_done, 1)

            def panel_mm(key, panel, i=0):
                for k in range(len(SPLIT[key])):
                    slab(key, panel, k, i)

            def token_squares(k):
                pe.wait_ge(acc_ready, 8 * (k + 1))
                for t in range(NB):
                    last = nc.tensor.matmul(AUX[:, 3, t:t + 1], acc[:, t * P:(t + 1) * P], ones[:, 0:1], start=True, stop=True)
                last.then_inc(ss_done, 1)

            def spread(k):
                pe.wait_ge(diag_ready, NB * (k + 1))
                nc.tensor.matmul(AUX[:, 3, :], ones[:], diag[:].rearrange("p t n -> p (t n)"), start=True, stop=True).then_inc(bc_done, 1)

            def after_norm(key, k, panels):
                panel_mm(key, 0)
                token_squares(k)
                panel_mm(key, 1)
                spread(k)
                if panels > 2:
                    with pe.Fori(1, panels // 2) as i:
                        panel_mm(key, 0, i)
                        panel_mm(key, 1, i)

            pe.wait_ge(const_in, 16 * N_CONST)
            pe.wait_ge(relw_ready, 3)
            for h in range(H2):
                if h >= 2:
                    pe.wait_ge(line_ready, 2 * (h - 1))
                b = 2 * (h % 2)
                nc.tensor.matmul(AUX[:, b, :], relw[:, h, :], oneh[:, 0:S], start=True, stop=True)
                nc.tensor.matmul(AUX[:, b + 1, 0:P], relw[:, h, :], oneh[:, S:LINE], start=True, stop=True).then_inc(line_mm, 1)
            pe.wait_ge(line_ready, 2 * H2)

            after_norm("C", 0, 2)
            for key in ("B", "dt", ("xs", 0)):
                for n in range(NPAN[key]):
                    panel_mm(key, n)
            pe.wait_ge(sp_step, 19)
            pe.wait_ge(pack_act, 3)
            for t in range(NB):
                last = nc.tensor.transpose(AUX[:, 3, t * P:(t + 1) * P], pack[:, t * P:(t + 1) * P], ident[:])
            last.then_inc(pack_tr, 1)

            def bank1_free(tok):
                last = LAST1[tok]
                if last is not None and last[0] == "Bp":
                    pe.wait_ge(state_step, STSTEPS[last[1] + 1])
                elif last is not None:
                    pe.wait_ge(aux1_read, READ1[last] + 1)

            def scan_step(tok):
                kind, u = tok[0], tok[1]
                g, c = (u // NB, u % NB) if kind in ("A", "Bp", "Cp") else (u, 0)
                if kind == "xt":
                    pe.wait_ge(xbc_ready, 2 * NG + u + 1)
                    wait(pe, aux0_read, USE0[tok])
                    for t in range(NB):
                        last = nc.tensor.transpose(AUX[:, 0, t * P:(t + 1) * P], xsf[:, u % 2, t * P:(t + 1) * P], ident[:])
                    last.then_inc(aux0_done, 1)
                elif kind == "G":
                    pe.wait_ge(xbc_ready, 2 * NG)
                    bank1_free(tok)
                    for t in range(NB):
                        last = nc.tensor.transpose(AUX[:, 1, t * P:(t + 1) * P], bcf[:, NG + g, t * P:(t + 1) * P], ident[:])
                    last.then_inc(aux1_done, 1)
                elif kind == "A":
                    bank1_free(tok)
                    nc.tensor.matmul(AUX[:, 1, 0:P], bcf[:, NG + g, c * P:(c + 1) * P], bcf[:, g, c * P:(c + 1) * P],
                                     start=True, stop=True).then_inc(aux1_done, 1)
                elif kind == "Bp":
                    pe.wait_ge(m_step, 2 * u + 2)
                    pe.wait_ge(xdt_ready, u + 1)
                    if u:
                        pe.wait_ge(y_step, YSTEPS[u])
                    if u == 0:
                        pe.wait_ge(tokc_ready, 1)
                    for h in range(HG):
                        last = nc.tensor.matmul(AUX[:, 2, h * HD:(h + 1) * HD], M[:, u % 2, h, :], xdt[:, u % 2, h * HD:(h + 1) * HD],
                                                start=True, stop=True)
                    last.then_inc(ydiag_done, 1)
                    if c:
                        pe.wait_ge(state_step, STSTEPS[u])
                        nc.tensor.matmul(AUX[:, 3, :], bcf[:, g, c * P:(c + 1) * P], state[:], start=True, stop=True).then_inc(yoff_done, 1)
                    if c < NB - 1:
                        pe.wait_ge(xdd_ready, u - g + 1)
                        bank1_free(tok)
                        nc.tensor.matmul(AUX[:, 1, :], btok[:, c, :], xdd[:, u % 2, :], start=True, stop=True).then_inc(aux1_done, 1)
                elif kind == "Cp":
                    pe.wait_ge(yn_ready, u + 1)
                    wait(pe, aux0_read, USE0[tok])
                    for n in range(4):
                        last = nc.tensor.transpose(AUX[:, 0, n * P:(n + 1) * P], yn[:, u % 3, n * P:(n + 1) * P], ident[:])
                    last.then_inc(aux0_done, 1)

            scan_step(("xt", 0))
            scan_step(("xt", 1))
            for tok in SCAN:
                if tok[0] == "mm":
                    panel_mm(tok[1], tok[2])
                elif tok[0] != "epi":
                    scan_step(tok)

            for key in QKV1(0)[2:]:
                panel_mm(key, 0)
            for tok in ATT1:
                kind, u = tok[0], tok[1]
                if kind == "half":
                    slab(tok[1], tok[2], tok[3])
                    continue
                if kind == "epi":
                    continue
                h, qb = u // NB, u % NB
                j, hh = h // 2, h % 2
                W1, W0 = w1(qb)
                q0 = qb * P
                if kind == "S":
                    wait(pe, o1_read, u)
                    if qb == 0 and hh == 0:
                        pe.wait_ge(rope_done, 12 * (j + 1))
                    for bank, gi, k0, width, m0 in ((0, 1, 0, W1, S - W1), (1, 2, 0, W1, 2 * S - W1), (2, 0, q0 + P - W0, W0, 2 * S + 2 * P - W0)):
                        nc.tensor.matmul(AUX[:, bank, 0:width], q1[j][:, 2 * gi + hh, q0:q0 + P], k1[j][:, 2 * gi + hh, k0:k0 + width],
                                         start=True, stop=False)
                        last = nc.tensor.matmul(AUX[:, bank, 0:width], ident_bf[:], mask1[:, m0:m0 + width], start=False, stop=True)
                    last.then_inc(s1_done, 1)
                elif kind == "T":
                    pe.wait_ge(exp1, 2 * u + 2)
                    wait(pe, o1_ready, u)
                    nb = nblk(qb)
                    for n in range(nb):
                        last = nc.tensor.transpose(AUX[:, (3, 0, 1)[n // 4], (n % 4) * P:(n % 4 + 1) * P], prob[:, n * P:(n + 1) * P], ident[:])
                        if n % 4 == 3 or n == nb - 1:
                            last.then_inc(tr1_done, 1)
                elif kind == "V":
                    pe.wait_ge(pT1_act, TA[u + 1])
                    wait(pe, pT1_dve, TV[u + 1])
                    if qb == 0 and hh == 0:
                        pe.wait_ge(evicted, 2 * (PAN[("v1", j, AG - 1)] + 1))
                    blocks = [(1, b) for b in range(qb + 1)] + [(2, b) for b in range(qb + 1)] + [(0, b) for b in range(max(qb - 1, 0), qb + 1)]
                    for n, (gi, b) in enumerate(blocks):
                        last = nc.tensor.matmul(AUX[:, 2, 0:P], probT[:, n, :], v1[j][:, b, gi * PANEL + hh * P:gi * PANEL + (hh + 1) * P],
                                                start=n == 0, stop=n == len(blocks) - 1)
                    last.then_inc(pv1_done, 1)
                elif kind == "X":
                    pe.wait_ge(o1_read, u + 1)
                    nc.tensor.transpose(AUX[:, 3, 0:P], osb[:, u % 2, :], ident[:]).then_inc(ot1_done, 1)

            for key in ("ao", "mix"):
                for n in range(4):
                    panel_mm(key, n)
            after_norm("ffn1", 1, 2 * FP)
            with pe.Fori(0, 2) as i:
                panel_mm("down1", 0, i)
                panel_mm("down1", 1, i)
            token_squares(2)
            spread(2)

            def attention(names, fox):
                u_base = 32 * fox

                def scores(u):
                    tile, qb = u // NB, u % NB
                    j, hh = tile // 2, tile % 2
                    width, q0 = (qb + 1) * P, qb * P
                    if qb == 0 and hh == 0:
                        pe.wait_ge(evicted, 2 * (PAN[(names[1], j)] + 1))
                    wait(pe, sc_ready, u_base + u)
                    for e in range(2):
                        rows = slice(64 * e, 64 * e + 64)
                        last = nc.tensor.matmul(AUX[:, e, 0:width], q2[j % 2][rows, hh, q0:q0 + P], k2[j % 2][rows, hh, 0:width],
                                                start=True, stop=True)
                        if fox:
                            last = nc.tensor.matmul(AUX[:, e, q0:width], ident_bf[:], mask1[:, 2 * S + P:2 * S + 2 * P],
                                                    start=False, stop=True, skip_group_check=True)
                    last.then_inc(s2_done, 1)

                for tok in order2(names):
                    kind, u = tok[0], tok[1]
                    if kind == "half":
                        slab(tok[1], tok[2], tok[3])
                    elif kind == "S":
                        scores(u)
                    elif kind in "TVX":
                        tile, qb = u // NB, u % NB
                        j, hh = tile // 2, tile % 2
                        U = u_base + u
                        if kind == "T":
                            if fox:
                                wait(pe, exp2, 2 * U + 2)
                                wait(pe, o2_read, 2 * u + 32)
                            else:
                                pe.wait_ge(r2_step, 4 * u + 4)
                            wait(pe, oT_ready, U - 1)
                            for e in range(1 + fox):
                                for b in range(qb + 1):
                                    src = sc[:, u % 2, e, b * P:(b + 1) * P] if fox else dif[:, u % 2, b * P:(b + 1) * P]
                                    last = nc.tensor.transpose(AUX[:, 2 + e, b * P:(b + 1) * P], src, ident[:])
                                last.then_inc(tr2_done, 1)
                        elif kind == "V":
                            pe.wait_ge(pT2_act, U + 1)
                            if qb == 0 and hh == 0:
                                pe.wait_ge(evicted, 2 * (PAN[(names[2], j)] + 1))
                            if fox:
                                pe.wait_ge(pT2_dve, u + 1)
                                for e in range(2):
                                    for b in range(qb + 1):
                                        last = nc.tensor.matmul(AUX[:, 2, e * 64:e * 64 + 64], pT[:, e, b, :],
                                                                v2[j % 2][:, b, hh * P + e * 64:hh * P + e * 64 + 64], start=b == 0, stop=b == qb)
                            else:
                                wait(pe, o2_read, u)
                                for b in range(qb + 1):
                                    last = nc.tensor.matmul(AUX[:, 3, 0:P], pT[:, u % 2, b, :], v2[j % 2][:, b, hh * P:(hh + 1) * P],
                                                            start=b == 0, stop=b == qb)
                            last.then_inc(pv2_done, 1)
                        elif kind == "X":
                            pe.wait_ge(o2_read, 2 * u + 34 if fox else u + 1)
                            wait(pe, oT_ready, U)
                            nc.tensor.transpose(AUX[:, 2 + fox, 0:P], osb2[:, u % 2, :], ident[:]).then_inc(ot2_done, 1)

            for n, name in enumerate(("q2", "k2", "v2")):
                panel_mm((name, 0), 0)
                if n == 0:
                    token_squares(3)
                if n == 1:
                    spread(3)
            attention(("q2", "k2", "v2"), 0)
            for n in range(4):
                panel_mm("awo", n)
            token_squares(4)
            spread(4)
            after_norm(("fin", 0), 5, 2 * FP)
            with pe.Fori(0, 2) as i:
                panel_mm(("fout", 0), 0, i)
                panel_mm(("fout", 0), 1, i)
            token_squares(6)
            spread(6)
            panel_mm("f", 0)
            token_squares(7)
            panel_mm(("q3", 0), 0)
            spread(7)
            panel_mm(("k3", 0), 0)
            panel_mm(("v3", 0), 0)
            pe.wait_ge(sp_step, 19 + 15)
            for t in range(NB):
                last = nc.tensor.transpose(AUX[:, 3, t * BH:(t + 1) * BH], fc[:, t * P:(t + 1) * P], ident[0:BH, 0:BH])
            last.then_inc(c_tr, 1)
            pe.wait_ge(ccol_ready, 1)
            attention(("q3", "k3", "v3"), 1)
            for n in range(4):
                panel_mm("bwo", n)
            token_squares(8)
            spread(8)
            after_norm(("fin", 1), 9, 2 * FP)
            with pe.Fori(0, 2) as i:
                panel_mm(("fout", 1), 0, i)
                panel_mm(("fout", 1), 1, i)
            token_squares(10)
            spread(10)

        @block.scalar
        def _(act):
            A = nc.scalar.activation

            def col(name, n):
                return vec[:, COL[name] + n:COL[name] + n + 1] if isinstance(n, int) else vec[:, bass.ds(COL[name] + n, 1)]

            def load(dst, src, s):
                act.dma_start(dst, src).then_inc(s, 16)

            for dst, name in ((oneh, "c_onehot"), (future, "c_future"), (vec, "vec"), (ident, "c_ident"), (ones, "c_ones"), (tri, "c_tri"),
                              (mask_in, "c_mask"), (relb, "rel_bias_2"), (dtv, "dtv"), (bfv, "bfv")):
                n = {"dtv": 2, "bfv": 1}.get(name, dst.shape[1])
                load(dst[:, 0:n], I[name], const_in)
            load(dsk[:], bass.AP(tensor=I["d_skip"].tensor, offset=0, ap=[[0, P], [1, NH]]), const_in)
            load(lamv[:].rearrange("p a n -> p (a n)"), bass.AP(tensor=I["lam"].tensor, offset=0, ap=[[0, P], [1, 4 * 64]]), const_in)
            act.wait_ge(const_in, 16 * N_CONST)

            def squares(src, k, c):
                wait(act, acc_ready, 8 * k + c - 1)
                A(sq[:, c % 2, :], src, ACT.Square).then_inc(sq_ready, 1)

            def high(dst, src, gain):
                A(dst, src, ACT.Copy, scale=gain).then_inc(op_hi, 1)

            def norm(k):
                act.wait_ge(ss_done, k + 1)
                A(std[:], AUX[:, 3, 0:NB], ACT.Sqrt, bias=EPS, scale=1.0 / D).then_inc(std_ready, 1)

            for c in range(DC):
                act.wait_ge(x_in[c // 2], 16)
                high(opA_hi[:, c, :], XT[:, c, :], col("norm_mix", c))
                squares(XT[:, c, :], 0, c)
            act.wait_ge(line_ready, 2 * H2)
            act.dma_start(bias_dram.rearrange("h p n -> p h n"), line[:]).then_inc(bias_out, 16)
            norm(0)

            def conv(q):
                tile = q + 20 if q < 4 else q + 12 if q < 8 else q - 8
                return tile

            def conv_panel(key, panel, q0):
                for m in range(2):
                    q = q0 + m
                    act.wait_ge(evicted, 2 * (PAN[key] + panel) + m + 1)
                    if q >= 2:
                        act.wait_ge(xbc_ready, q - 1)
                    tile = conv(q)
                    A(cacc[:, q % 2, :], cu[:, q % 2, KCONV - 1:KCONV - 1 + S], ACT.Identity, bias=col("conv_b", tile),
                      scale=col("conv_w", 24 * (KCONV - 1) + tile)).then_inc(conv_t0, 1)
                for m in range(2):
                    q = q0 + m
                    act.wait_ge(conv_tap, 6 * (q0 // 2) + 5 + m)
                    if q >= 10:
                        act.wait_ge(aux0_done, USE0[("xt", q - 10)] + 1)
                    dst = bcf[:, q, :] if q < 8 else xsf[:, q % 2, :]
                    A(dst, cacc[:, q % 2, :], ACT.Silu).then_inc(xbc_ready, 1)

            conv_panel("C", 0, 0)
            conv_panel("C", 1, 2)
            conv_panel("B", 0, 4)
            conv_panel("B", 1, 6)

            def softplus(p, src, steps, sign, bias, evict):
                a0 = steps
                act.wait_ge(evicted, evict)
                A(p[1][:], src[:], ACT.Abs, bias=bias, scale=sign).then_inc(sp_act, 1)
                act.wait_ge(sp_act, a0 + 1)
                A(p[2][:], p[1][:], ACT.Exp, scale=-1.0).then_inc(sp_act, 1)
                act.wait_ge(sp_act, a0 + 2)
                A(p[1][:], src[:], ACT.Relu, bias=bias, scale=sign).then_inc(sp_act, 1)

            A(dtv[:, 2:3], dtv[:, 1:2], ACT.Exp).then_inc(a_neg, 1)
            softplus((dx, da, de), dx, 0, 1.0, dtv[:, 0:1], 2 * (PAN["dt"] + 1))
            act.wait_ge(sp_step, 13)
            A(pack[0:NH, :], ddt[:], ACT.Copy).then_inc(pack_act, 1)
            act.wait_ge(sp_step, 18)
            load(acs_dram, dacs[:], acs_out)
            A(pack[NH:2 * NH, :], dacs[:], ACT.Copy).then_inc(pack_act, 1)
            for t in range(NB):
                last = A(ddec[:, t * P:(t + 1) * P], dacs[:, t * P:(t + 1) * P], ACT.Exp, bias=dacs[:, (t + 1) * P - 1:(t + 1) * P], scale=-1.0)
            A(pack[3 * NH:4 * NH, :], dacs[:], ACT.Exp).then_inc(pack_act, 1)
            conv_panel(("xs", 0), 0, 8)
            act.wait_ge(acs_out, 16)

            def load_decay(u):
                g, c = u // NB, u % NB
                load(acs_row[:, u % 2], bass.AP(tensor=acs_dram.tensor, offset=g * HG * S + c * P, ap=[[0, P], [S, HG], [1, P]]), acs_in[u % 2])

            def load_gain(g):
                load(gain[:, g % 2, :], bass.AP(tensor=I["ssm_norm"].tensor, offset=g * GW, ap=[[0, P], [1, GW]]), gain_in[g % 2])

            act.wait_ge(op_ready, DC)
            act.wait_ge(sq_ready, DC)
            load_decay(0)
            load_gain(0)
            act.wait_ge(pack_tr, 1)
            A(tokc[:].rearrange("p t k h -> p (t k h)"), AUX[:, 3, :], ACT.Copy).then_inc(tokc_ready, 1)

            def silu_gate(g, panel):
                act.wait_ge(evicted, 2 * (PAN[("z", g)] + panel) + 2)
                part = zbuf[:, :, panel * PANEL:(panel + 1) * PANEL]
                A(part, part, ACT.Silu).then_inc(z_ready, 1)

            def scan_step(tok):
                kind, u = tok[0], tok[1]
                if kind == "xt":
                    act.wait_ge(aux0_done, USE0[tok] + 1)
                    if u >= 8 and u % 4 == 0:
                        act.wait_ge(y_step, YSTEPS[4 * (u // 4 - 1)])
                        act.wait_ge(xdt_ready, 4 * (u // 4 - 1))
                        act.wait_ge(xdd_ready, 3 * (u // 4 - 1))
                    A(xs_tok[:, (u // 4) % 2, :, (u % 4) * P:(u % 4 + 1) * P], AUX[:, 0, :].rearrange("p (t n) -> p t n", n=P),
                      ACT.Copy).then_inc(aux0_read, 1)
                elif kind == "A":
                    act.wait_ge(acs_in[u % 2], 16 * (u // 2 + 1))
                    act.wait_ge(decay_step, 2 * u + 2)
                    A(M[:, u % 2], M[:, u % 2], ACT.Exp).then_inc(decay_exp, 1)
                    A(etot[:, u % 2, :], acs_row[:, u % 2, :, P - 1], ACT.Exp).then_inc(decay_exp, 1)
                    if u < 15:
                        if u:
                            act.wait_ge(decay_step, 2 * u)
                            act.wait_ge(decay_exp, 2 * u)
                        load_decay(u + 1)
                    if u % 4 == 1 and u < 12:
                        if u > 4:
                            act.wait_ge(yn_ready, u - 1)
                        load_gain(u // 4 + 1)
                elif kind == "Bp":
                    act.wait_ge(y_step, YSTEPS[u + 1])
                    if u:
                        act.wait_ge(yn_ready, u)
                    A(yt[:], yb[:], ACT.Square, accum_out=ystat[:, u % 2, 0:1]).then_inc(y_stat, 1)
                    act.wait_ge(y_stat, 2 * u + 1)
                    A(ystat[:, u % 2, 1:2], ystat[:, u % 2, 0:1], ACT.Sqrt, bias=EPS, scale=1.0 / GW).then_inc(y_stat, 1)
                elif kind == "Cp":
                    g, c = u // NB, u % NB
                    act.wait_ge(aux0_done, USE0[tok] + 1)
                    if g:
                        act.wait_ge(slab_done, slab_end(("so", g - 1), 3))
                    A(yT_hi[:, :, c * P:(c + 1) * P], AUX[:, 0, :].rearrange("p (j t) -> p j t", t=P), ACT.Copy).then_inc(y_hi, 1)

            scan_step(("xt", 0))
            scan_step(("xt", 1))
            conv_panel(("xs", 0), 1, 10)
            for tok in SCAN:
                if tok[0] == "epi":
                    key, panel = tok[1], tok[2]
                    if key[0] == "z":
                        silu_gate(key[1], panel)
                    elif key[0] == "xs":
                        conv_panel(key, panel, 8 + 4 * key[1] + 2 * panel)
                elif tok[0] != "mm":
                    scan_step(tok)
                if tok == ("Cp", 15):
                    act.wait_ge(aux0_done, len(USE0))
                    act.wait_ge(yn_ready, 16)
                    act.wait_ge(xbc_ready, 24)
                    load(cosr[:], I["c_cos"], rope_in)
                    load(sinr[:], I["c_sin"], rope_in)

            for tok in ATT1:
                kind, u = tok[0], tok[1]
                if kind == "epi" and tok[1] == "gates":
                    panel = tok[2]
                    for m in range(2):
                        gi, c = panel % 2, 2 * (panel // 2) + m
                        act.wait_ge(evicted, 2 * (PAN["gates"] + panel) + m + 1)
                        A(gate1[:, c, :] if gi else gtmp[:, m, :], gtmp[:, m, :], ACT.Sigmoid, bias=col("b_gate", 8 * gi + c)).then_inc(gate_sig, 1)
                if kind in ("half", "epi"):
                    continue
                h, qb = u // NB, u % NB
                W1, W0 = w1(qb)
                if kind == "S":
                    act.wait_ge(negmax1, u + 1)
                    wait(act, tr1_done, TB[u])
                    wait(act, den1, u - 1)
                    A(prob[:, 0:2 * W1].rearrange("p (g k) -> p g k", g=2), AUX[:, 0:2, 0:W1], ACT.Exp, bias=astat[:, u % 2, 2:3],
                      scale=ADIM ** -0.5, accum_out=astat[:, u % 2, 3:4]).then_inc(exp1, 1)
                    A(prob[:, 2 * W1:2 * W1 + W0], AUX[:, 2, 0:W0], ACT.Exp, bias=astat[:, u % 2, 2:3],
                      scale=ADIM ** -0.5, accum_out=astat[:, u % 2, 4:5]).then_inc(exp1, 1)
                elif kind == "T":
                    nb = nblk(qb)
                    wait(act, pv1_done, u)
                    for n in range(0, nb, 8):
                        bank = n // 4
                        act.wait_ge(tr1_done, TB[u] + bank + 1)
                        k = min(4, nb - n)
                        A(probT[:, n:n + k, :], AUX[:, (3, 0, 1)[bank], 0:k * P].rearrange("p (b q) -> p b q", q=P), ACT.Copy).then_inc(pT1_act, 1)
                elif kind == "X":
                    act.wait_ge(ot1_done, u + 1)
                    A(o1_hi[:, h, qb * P:(qb + 1) * P], AUX[:, 3, 0:P], ACT.Copy).then_inc(o1_high, 1)
            act.wait_ge(o1_ready, 16)
            for n in range(4):
                load(XT[:, 2 * n:2 * n + 2, :], xT.rearrange("(c p) t -> p c t", p=P)[:, 2 * n:2 * n + 2, :], x_in[n])
            for c in range(DC):
                act.wait_ge(mix_sum, c + 1)
                A(mix_hi[:, c, :], mixed[:, c, :], ACT.Copy).then_inc(mix_high, 1)
            for c in range(DC):
                act.wait_ge(evicted, 2 * PAN["mix"] + c + 1)
                high(opA_hi[:, c, :], XT[:, c, :], col("norm_ffn", c))
                squares(XT[:, c, :], 1, c)
            norm(1)

            def ffn1_body(i):
                for m in range(2):
                    act.wait_ge(evicted, 2 * PAN["ffn1"] + 4 * i + m + 1)
                    A(fg[:, m, :], facc[:, m, :], ACT.Silu).then_inc(fgate, 1)
                for m in range(2):
                    act.wait_ge(fprod, 2 * i + m + 1)
                    A(hid_hi[:, bass.ds(2 * i + m, 1), :], facc[:, 2 + m:3 + m, :], ACT.Copy).then_inc(hid_high, 1)

            with act.Fori(0, FP) as i:
                ffn1_body(i)
            for c in range(DC):
                act.wait_ge(evicted, 2 * PAN["down1"] + c + 1)
                squares(XT[:, c, :], 2, c)
            norm(2)

            def prepare(k, dst, name, first, src_ready):
                for c in range(DC):
                    act.wait_ge(res_ready, src_ready + c + 1)
                    high(dst[:, c, :], XT[:, c, :], col(name, first + c))
                    squares(XT[:, c, :], k, c)

            def branch_squares(key, k):
                for c in range(DC):
                    act.wait_ge(evicted, 2 * PAN[key] + c + 1)
                    squares(branch[:, c, :], k, c)
                norm(k)

            def fin(l, k):
                def body(i, first):
                    n0 = 44 * l
                    for half in range(2):
                        for m in range(2):
                            j = 2 * half + m
                            act.wait_ge(evicted, 2 * PAN[("fin", l)] + 4 * i + j + 1)
                            A(facc[:, j, :], fu[:, j, 2:2 + S], ACT.Identity, bias=col("ffn_conv_b_2", 44 * l + FT * half + m + 2 * i),
                              scale=col("ffn_conv_w_2", 132 * l + 88 + FT * half + m + 2 * i)).then_inc(fconv_t0, 1)
                        if half == 0:
                            for m in range(2):
                                act.wait_ge(fconv_tap, 88 * l + 8 * i + 3 + m)
                                A(fg[:, m, :], facc[:, m, :], ACT.Gelu_apprx_tanh).then_inc(fgate, 1)
                    for m in range(2):
                        act.wait_ge(fprod, FT * (l + 1) + 2 * i + m + 1)
                        A(hid_hi[:, bass.ds(2 * i + m, 1), :], facc[:, 2 + m:3 + m, :], ACT.Copy).then_inc(hid_high, 1)

                with act.Fori(0, FP) as i:
                    body(i, False)

            def softmax_units(names, fox):
                for tok in order2(names):
                    kind, u = tok[0], tok[1]
                    if kind in ("half", "epi"):
                        continue
                    U = 32 * fox + u
                    tile, qb = u // NB, u % NB
                    width = (qb + 1) * P
                    if kind == "M":
                        if fox and qb == 0 and tile < 7:
                            if tile:
                                act.wait_ge(sc_ready, 32 + 4 * tile)
                            load_negc(tile + 1)
                        act.wait_ge(negmax2, U + 1)
                        for e in range(2):
                            A(sc[:, u % 2, e, 0:width], sc[:, u % 2, e, 0:width], ACT.Exp, bias=bstat[:, u % 4, 2 + e:3 + e],
                              accum_out=bstat[:, u % 4, 4 + e:5 + e]).then_inc(exp2, 1)
                    elif kind == "T":
                        act.wait_ge(tr2_done, 32 + 2 * u + 1 if fox else u + 1)
                        if fox:
                            wait(act, pv2_done, U)
                            dst = pT[:, 0, 0:qb + 1, :]
                        else:
                            wait(act, pv2_done, U - 1)
                            dst = pT[:, u % 2, 0:qb + 1, :]
                        A(dst, AUX[:, 2, 0:width].rearrange("p (b q) -> p b q", q=P), ACT.Copy).then_inc(pT2_act, 1)
                    elif kind == "W" and not fox:
                        act.wait_ge(pv2_done, u + 1)
                        A(osq[:], AUX[:, 3, 0:P], ACT.Square, accum_out=bstat[:, u % 4, 8:9]).then_inc(o2_stat, 1)
                        act.wait_ge(o2_stat, 2 * u + 1)
                        A(bstat[:, u % 4, 9:10], bstat[:, u % 4, 8:9], ACT.Sqrt, bias=SUB_EPS, scale=1.0 / P).then_inc(o2_stat, 1)
                    elif kind == "X":
                        act.wait_ge(ot2_done, U + 1)
                        A(oT[:, tile, qb * P:(qb + 1) * P], AUX[:, 2 + fox, 0:P], ACT.Copy, scale=1.0 if fox else subg[:, 0:1]).then_inc(oT_ready, 1)

            def load_negc(tile):
                load(negc[:, tile % 2], bass.AP(tensor=c_dram.tensor, offset=2 * tile * S, ap=[[0, P], [S, 2], [1, S]]), negc_in[tile % 2])

            def wo_operand(key, units):
                act.wait_ge(oT_ready, units)
                for c in range(DC):
                    A(opA_hi[:, c, :], oT[:, c, :], ACT.Copy).then_inc(op_hi, 1)

            act.wait_ge(lam_step, 3)
            for n in range(2):
                A(lams[:, 2 + n:3 + n], lams[:, n:n + 1], ACT.Exp).then_inc(lam_act, 1)
            prepare(3, opA_hi, "a_norm_pre_2", 0, 0)
            act.wait_ge(evicted, 2 * PAN["down1"] + DC)
            act.wait_ge(hid_ready, FT)
            act.wait_ge(bias_out, 16)
            load(tbias[:], bass.AP(tensor=bias_dram.tensor, offset=P - 1, ap=[[LINE - 1, P], [P * LINE, H2], [1, S]]), tbias_in)
            norm(3)
            softmax_units(("q2", "k2", "v2"), 0)
            wo_operand("awo", 32)
            branch_squares("awo", 4)
            prepare(5, opA_hi, "ffn_norm_pre_2", 0, DC)
            norm(5)
            fin(0, 5)
            branch_squares(("fout", 0), 6)
            prepare(7, opA_hi, "kv_norm_2", 0, 2 * DC)
            for c in range(DC):
                high(opB_hi[:, c, :], XT[:, c, :], col("b_norm_pre_2", c))
            norm(7)
            A(bfv[:, 1:2], bfv[:, 0:1], ACT.Copy, scale=-1.0).then_inc(lam_act, 1)
            act.wait_ge(lam_act, 3)
            softplus((fx, fa, fe), fx, 3, -1.0, bfv[:, 1:2], 2 * (PAN["f"] + 1))
            act.wait_ge(sp_step, 19 + 15)
            load(c_dram, fc[:], c_out)
            act.wait_ge(c_out, 16)
            load_negc(0)
            act.wait_ge(c_tr, 1)
            A(ccol[:].rearrange("p t h -> p (t h)"), AUX[:, 3, 0:NB * BH], ACT.Copy).then_inc(ccol_ready, 1)
            softmax_units(("q3", "k3", "v3"), 1)
            wo_operand("bwo", 64)
            branch_squares("bwo", 8)
            prepare(9, opA_hi, "ffn_norm_pre_2", 8, 3 * DC)
            norm(9)
            fin(1, 9)
            branch_squares(("fout", 1), 10)

        @block.vector
        def _(dve):
            V = nc.vector

            def col(name, n):
                return vec[:, COL[name] + n:COL[name] + n + 1] if isinstance(n, int) else vec[:, bass.ds(COL[name] + n, 1)]

            dve.wait_ge(const_in, 16 * N_CONST)
            V.tensor_copy(relw[:], relb[:].unsqueeze(2).broadcast_to([BUCKETS, H2, P])).then_inc(relw_ready, 1)
            V.tensor_copy(mask1[:], mask_in[:]).then_inc(relw_ready, 1)
            V.tensor_copy(ident_bf[:], ident[:]).then_inc(relw_ready, 1)
            for h in range(H2):
                dve.wait_ge(line_mm, h + 1)
                b = 2 * (h % 2)
                V.tensor_tensor(line[:, h, 0:S], AUX[:, b, :], future[:, 0:S], ALU.add).then_inc(line_ready, 1)
                V.tensor_tensor(line[:, h, S:LINE], AUX[:, b + 1, 0:P], future[:, S:LINE], ALU.add).then_inc(line_ready, 1)

            V.tensor_tensor(lamt[:], lamv[:, 0:4:2, :], lamv[:, 1:4:2, :], ALU.mult).then_inc(lam_step, 1)
            dve.wait_ge(lam_step, 1)
            V.tensor_reduce(lams[:, 0:2], lamt[:], AX.X, ALU.add).then_inc(lam_step, 1)
            V.tensor_scalar(subg[:], col("a_subln_2", 0), 1.0 - LAM0, None, ALU.mult).then_inc(lam_step, 1)

            n_op = [0]

            def low(dst, src, gain, high_part):
                n_op[0] += 1
                dve.wait_ge(op_hi, n_op[0])
                if gain is None:
                    V.tensor_tensor(dst, src, high_part.bitcast(F32), ALU.subtract).then_inc(op_ready, 1)
                else:
                    V.scalar_tensor_tensor(dst, src, gain, high_part.bitcast(F32), ALU.mult, ALU.subtract).then_inc(op_ready, 1)

            def add_squares(k, c):
                dve.wait_ge(sq_ready, 8 * k + c + 1)
                if c == 0:
                    wait(dve, ss_done, k)
                    V.tensor_copy(acc[:], sq[:, 0, :]).then_inc(acc_ready, 1)
                else:
                    dve.wait_ge(acc_ready, 8 * k + c)
                    V.tensor_tensor(acc[:], acc[:], sq[:, c % 2, :], ALU.add).then_inc(acc_ready, 1)

            def norm(k):
                dve.wait_ge(std_ready, k + 1)
                V.reciprocal(rstd_col[:], std[:]).then_inc(rstd_ready, 1)
                dve.wait_ge(rstd_ready, k + 1)
                for t in range(NB):
                    V.tensor_scalar(diag[:, t, :], ident[:], rstd_col[:, t:t + 1], None, ALU.mult).then_inc(diag_ready, 1)
                dve.wait_ge(bc_done, k + 1)
                V.tensor_copy(rstd_bc[:], AUX[:, 3, :]).then_inc(bc_ready, 1)
                dve.wait_ge(bc_ready, k + 1)

            for c in range(DC):
                dve.wait_ge(x_in[c // 2], 16)
                low(opA_lo[:, c, :], XT[:, c, :], col("norm_mix", c), opA_hi[:, c, :])
                add_squares(0, c)
            norm(0)
            dve.wait_ge(op_ready, DC)
            V.memset(cu[:, :, 0:KCONV - 1], 0.0).then_inc(pads, 1)
            dve.wait_ge(pads, 1)

            def done(key, panel, i=0):
                dve.wait_ge(slab_done, slab_end(key, panel) + 2 * len(SPLIT[key]) * i)

            def conv_panel(key, panel, q0):
                done(key, panel)
                for m in range(2):
                    wait(dve, conv_t0, q0 + m - 1)
                    wait(dve, conv_tap, 3 * q0 + m - 1 if q0 else 0)
                    V.tensor_tensor(cu[:, m, KCONV - 1:KCONV - 1 + S], psum_fm(key, panel, m), rstd_bc[:], ALU.mult).then_inc(evicted, 1)
                for j in range(KCONV - 1):
                    for m in range(2):
                        q = q0 + m
                        tile = q + 20 if q < 4 else q + 12 if q < 8 else q - 8
                        if j == 0:
                            dve.wait_ge(conv_t0, q + 1)
                        else:
                            dve.wait_ge(conv_tap, 3 * q0 + 2 * j - 1 + m)
                        V.scalar_tensor_tensor(cacc[:, m, :], cu[:, m, j:j + S], col("conv_w", 24 * j + tile), cacc[:, m, :],
                                               ALU.mult, ALU.add).then_inc(conv_tap, 1)

            conv_panel("C", 0, 0)
            conv_panel("C", 1, 2)
            conv_panel("B", 0, 4)
            conv_panel("B", 1, 6)

            def softplus(p, s0, a0):
                a, e, r_, z, z2, q = p
                n = [s0]

                def step(ins):
                    n[0] += 1
                    ins.then_inc(sp_step, 1)
                    dve.wait_ge(sp_step, n[0])

                dve.wait_ge(sp_act, a0 + 2)
                step(V.tensor_scalar(r_[:], e[:], 2.0, None, ALU.add))
                step(V.reciprocal(r_[:], r_[:]))
                step(V.tensor_tensor(z[:], e[:], r_[:], ALU.mult))
                step(V.tensor_tensor(z2[:], z[:], z[:], ALU.mult))
                step(V.tensor_scalar(q[:], z2[:], 1.0 / 15, None, ALU.mult))
                for k in (13, 11, 9, 7, 5, 3):
                    step(V.scalar_tensor_tensor(q[:], q[:], 1.0 / k, z2[:], ALU.add, ALU.mult))
                step(V.scalar_tensor_tensor(q[:], q[:], 1.0, z[:], ALU.add, ALU.mult))
                dve.wait_ge(sp_act, a0 + 3)
                return step, q, a

            dve.wait_ge(bias_out, 16)
            done("dt", 0)
            V.tensor_tensor(dx[:], psum_fm("dt", 0, 0)[0:NH, :], rstd_bc[0:NH, :], ALU.mult).then_inc(evicted, 2)
            step, q, a = softplus((da, de, dr, dz, dz2, dq), 0, 0)
            step(V.scalar_tensor_tensor(ddt[:], q[:], 2.0, a[:], ALU.mult, ALU.add))
            dve.wait_ge(a_neg, 1)
            step(V.tensor_scalar(dz[:], ddt[:], dtv[:, 2:3], -1.0, ALU.mult, ALU.mult))
            for t in range(NB):
                step(V.tensor_tensor_scan(dacs[:, t * P:(t + 1) * P], ones[0:NH, :], dz[:, t * P:(t + 1) * P], 0.0, ALU.mult, ALU.add))
            dve.wait_ge(pack_act, 3)
            V.tensor_tensor(pack[2 * NH:3 * NH, :], ddt[:], ddec[:], ALU.mult).then_inc(sp_step, 1)
            conv_panel(("xs", 0), 0, 8)
            conv_panel(("xs", 0), 1, 10)

            def heads(ap):
                return ap.rearrange("p (h d) -> p h d", d=HD)

            def spread(ap):
                return ap.unsqueeze(2).broadcast_to([P, HG, HD])

            n_state, n_y = [0], [0]

            def scan_step(tok):
                kind, u = tok[0], tok[1]
                g, c = (u // NB, u % NB) if kind in ("A", "Bp", "N", "Cp") else (u, 0)
                hs = slice(g * HG, (g + 1) * HG)
                if kind == "G":
                    dve.wait_ge(aux1_done, USE1[tok] + 1)
                    V.tensor_copy(btok[:].rearrange("p t n -> p (t n)"), AUX[:, 1, :]).then_inc(aux1_read, 1)
                elif kind == "A":
                    dve.wait_ge(acs_in[u % 2], 16 * (u // 2 + 1))
                    if u == 0:
                        dve.wait_ge(tokc_ready, 1)
                    wait(dve, ydiag_done, u - 1)
                    V.tensor_tensor(M[:, u % 2], acs_row[:, u % 2], tokc[:, c, 1, hs].unsqueeze(2).broadcast_to([P, HG, P]),
                                    ALU.subtract).then_inc(decay_step, 1)
                    dve.wait_ge(decay_step, 2 * u + 1)
                    V.tensor_scalar(M[:, u % 2], M[:, u % 2], 0.0, None, ALU.min).then_inc(decay_step, 1)
                    xs = heads(xs_tok[:, g % 2, c, :])
                    dve.wait_ge(aux0_read, USE0[("xt", 4 * g + 3)] + 1)
                    V.tensor_tensor(heads(xdt[:, u % 2, :]), xs, spread(tokc[:, c, 0, hs]), ALU.mult).then_inc(xdt_ready, 1)
                    if c < NB - 1:
                        V.tensor_tensor(heads(xdd[:, u % 2, :]), xs, spread(tokc[:, c, 2, hs]), ALU.mult).then_inc(xdd_ready, 1)
                    dve.wait_ge(aux1_done, USE1[tok] + 1)
                    V.tensor_tensor(cbm[:, u % 2, :], AUX[:, 1, 0:P], tri[:], ALU.mult).then_inc(aux1_read, 1)
                    dve.wait_ge(aux1_read, READ1[tok] + 1)
                    dve.wait_ge(decay_exp, 2 * u + 1)
                    V.tensor_tensor(M[:, u % 2], M[:, u % 2], cbm[:, u % 2, :].unsqueeze(1).broadcast_to([P, HG, P]), ALU.mult).then_inc(m_step, 2)
                elif kind == "Bp":
                    if c:
                        dve.wait_ge(yoff_done, u - g)
                    if c < NB - 1:
                        dve.wait_ge(decay_exp, 2 * u + 2)
                        if c:
                            V.tensor_tensor(heads(state[:]), heads(state[:]), spread(etot[:, u % 2, :]), ALU.mult).then_inc(state_step, 1)
                            dve.wait_ge(state_step, STSTEPS[u] + 1)
                            dve.wait_ge(aux1_done, USE1[tok] + 1)
                            V.tensor_tensor(state[:], state[:], AUX[:, 1, :], ALU.add).then_inc(state_step, 1)
                        else:
                            dve.wait_ge(aux1_done, USE1[tok] + 1)
                            V.tensor_copy(state[:], AUX[:, 1, :]).then_inc(state_step, 1)
                        dve.wait_ge(state_step, STSTEPS[u + 1])
                    y0 = YSTEPS[u]
                    k = [y0]

                    def step(ins):
                        k[0] += 1
                        ins.then_inc(y_step, 1)
                        dve.wait_ge(y_step, k[0])

                    wait(dve, y_stat, 2 * u)
                    wait(dve, yn_ready, u)
                    step(V.tensor_tensor(heads(yb[:]), heads(xs_tok[:, g % 2, c, :]), spread(dsk[:, hs]), ALU.mult))
                    if c:
                        step(V.tensor_tensor(heads(yoffb[:]), heads(AUX[:, 3, :]), spread(tokc[:, c, 3, hs]), ALU.mult))
                    dve.wait_ge(ydiag_done, u + 1)
                    step(V.tensor_tensor(yb[:], yb[:], AUX[:, 2, :], ALU.add))
                    if c:
                        step(V.tensor_tensor(yb[:], yb[:], yoffb[:], ALU.add))
                    dve.wait_ge(z_ready, 2 * g + 2)
                    step(V.tensor_tensor(yb[:], yb[:], zbuf[:, c, :], ALU.mult))
                elif kind == "N":
                    dve.wait_ge(y_stat, 2 * u + 2)
                    V.reciprocal(ystat[:, u % 2, 2:3], ystat[:, u % 2, 1:2]).then_inc(y_rstd, 1)
                    dve.wait_ge(y_rstd, u + 1)
                    dve.wait_ge(gain_in[g % 2], 16 * (g // 2 + 1))
                    if u >= 3:
                        dve.wait_ge(aux0_done, USE0[("Cp", u - 3)] + 1)
                    V.scalar_tensor_tensor(yn[:, u % 3, :], yb[:], ystat[:, u % 2, 2:3], gain[:, g % 2, :], ALU.mult, ALU.mult).then_inc(yn_ready, 1)
                elif kind == "Cp":
                    dve.wait_ge(y_hi, u + 1)
                    part = slice(c * P, (c + 1) * P)
                    V.tensor_tensor(yT_lo[:, :, part], AUX[:, 0, :].rearrange("p (j t) -> p j t", t=P), yT_hi[:, :, part].bitcast(F32),
                                    ALU.subtract).then_inc(aux0_read, 1)

            def gate_panel(key, panel):
                done(key, panel)
                g = key[1]
                for t in range(NB):
                    ins = V.tensor_scalar(zbuf[:, t, panel * PANEL:(panel + 1) * PANEL], psum_tm(key, panel)[:, t, :], rstd_col[:, t:t + 1], None, ALU.mult)
                    if t % 2:
                        ins.then_inc(evicted, 1)

            def add_scan_out(key, panel):
                done(key, panel)
                for m in range(2):
                    c = 2 * panel + m
                    if key[1] == 0:
                        V.tensor_copy(y_ssm[:, c, :], psum_fm(key, panel, m)).then_inc(evicted, 1)
                    else:
                        V.tensor_tensor(y_ssm[:, c, :], y_ssm[:, c, :], psum_fm(key, panel, m), ALU.add).then_inc(evicted, 1)

            n_rope = [0]

            def rotate_panel(key):
                name, j, gi = key
                done(key, 0)
                dst = (q1 if name == "q1" else k1)[j]
                T = 2 * PAN[key]
                for m in range(2):
                    ps = psum_fm(key, 0, m)
                    wait(dve, rope_done, n_rope[0] + m - 1)
                    V.tensor_tensor(dst[:, 2 * gi + m, :], ps, cosr[:], ALU.mult)
                    V.tensor_tensor(rsin[0:64, m, :], ps[64:P], sinr[64:P, :], ALU.mult)
                    V.tensor_tensor(rsin[64:P, m, :], ps[0:64], sinr[0:64, :], ALU.mult).then_inc(evicted, 1)
                for m in range(2):
                    dve.wait_ge(evicted, T + m + 1)
                    V.tensor_tensor(dst[:, 2 * gi + m, :], dst[:, 2 * gi + m, :], rsin[:, m, :], ALU.add).then_inc(rope_done, 1)
                n_rope[0] += 2

            def values_panel(key, dst, first):
                done(key, 0)
                for t in range(NB):
                    ins = V.tensor_scalar(dst[:, t, first:first + PANEL], psum_tm(key, 0)[:, t, :], rstd_col[:, t:t + 1], None, ALU.mult)
                    if t % 2:
                        ins.then_inc(evicted, 1)

            def qkv1(key):
                if key[0] == "v1":
                    values_panel(key, v1[key[1]], key[2] * PANEL)
                else:
                    rotate_panel(key)

            def scale_rotations():
                dve.wait_ge(rope_in, 32)
                V.tensor_tensor(cosr[:], cosr[:], rstd_bc[:], ALU.mult).then_inc(rope_scaled, 1)
                V.tensor_tensor(sinr[:], sinr[:], rstd_bc[:], ALU.mult).then_inc(rope_scaled, 1)
                dve.wait_ge(rope_scaled, 2)

            for tok in SCAN:
                if tok[0] == "epi":
                    key, panel = tok[1], tok[2]
                    if key[0] == "z":
                        gate_panel(key, panel)
                    elif key[0] == "xs":
                        conv_panel(key, panel, 8 + 4 * key[1] + 2 * panel)
                    elif key[0] == "so":
                        add_scan_out(key, panel)
                    else:
                        if key == QKV1(0)[0]:
                            scale_rotations()
                        qkv1(key)
                elif tok[0] != "mm":
                    scan_step(tok)
            for key in QKV1(0)[2:]:
                qkv1(key)

            for tok in ATT1:
                kind, u = tok[0], tok[1]
                if kind == "epi" and tok[1] == "gates":
                    panel = tok[2]
                    gi = panel % 2
                    done("gates", panel)
                    for m in range(2):
                        wait(dve, gate_sig, 2 * panel + m - 1)
                        V.tensor_tensor(gtmp[:, m, :], psum_fm("gates", panel, m), rstd_bc[:], ALU.mult).then_inc(evicted, 1)
                    if gi == 0:
                        for m in range(2):
                            c = 2 * (panel // 2) + m
                            dve.wait_ge(gate_sig, 2 * panel + m + 1)
                            V.tensor_tensor(mixed[:, c, :], gtmp[:, m, :], y_ssm[:, c, :], ALU.mult).then_inc(gate_mul, 1)
                elif kind == "epi":
                    qkv1(tok[1])
                if kind in ("half", "epi"):
                    continue
                h, qb = u // NB, u % NB
                W1, W0 = w1(qb)
                st = astat[:, u % 2]
                if kind == "S":
                    dve.wait_ge(s1_done, u + 1)
                    V.tensor_reduce(st[:, 0:1], AUX[:, 0:2, 0:W1], AX.XY, ALU.max).then_inc(max1, 1)
                    V.tensor_reduce(st[:, 1:2], AUX[:, 2, 0:W0], AX.X, ALU.max).then_inc(max1, 1)
                    dve.wait_ge(max1, 2 * u + 2)
                    V.tensor_scalar(st[:, 2:3], st[:, 0:1], st[:, 1:2], -(ADIM ** -0.5), ALU.max, ALU.mult).then_inc(negmax1, 1)
                elif kind == "T":
                    if nblk(qb) > 4:
                        nb = min(4, nblk(qb) - 4)
                        dve.wait_ge(tr1_done, TB[u] + 2)
                        V.tensor_copy(probT[:, 4:4 + nb, :], AUX[:, 0, 0:nb * P].rearrange("p (b q) -> p b q", q=P)).then_inc(pT1_dve, 1)
                    dve.wait_ge(exp1, 2 * u + 2)
                    V.tensor_tensor(st[:, 5:6], st[:, 3:4], st[:, 4:5], ALU.add).then_inc(den1, 1)
                    dve.wait_ge(den1, u + 1)
                    V.reciprocal(st[:, 6:7], st[:, 5:6]).then_inc(rden1, 1)
                elif kind == "V":
                    dve.wait_ge(pv1_done, u + 1)
                    dve.wait_ge(rden1, u + 1)
                    wait(dve, ot1_done, u - 1)
                    V.tensor_scalar(osb[:, u % 2, :], AUX[:, 2, 0:P], st[:, 6:7], None, ALU.mult).then_inc(o1_read, 1)
                elif kind == "X":
                    dve.wait_ge(o1_high, u + 1)
                    part = slice(qb * P, (qb + 1) * P)
                    V.tensor_tensor(o1_lo[:, h, part], AUX[:, 3, 0:P], o1_hi[:, h, part].bitcast(F32), ALU.subtract).then_inc(o1_ready, 1)

            dve.wait_ge(gate_sig, 16)
            dve.wait_ge(gate_mul, 8)
            for panel in range(4):
                done("ao", panel)
                for m in range(2):
                    c = 2 * panel + m
                    wait(dve, mix_sum, c - 1)
                    V.tensor_tensor(gtmp[:, m, :], psum_fm("ao", panel, m), gate1[:, c, :], ALU.mult).then_inc(evicted, 1)
                for m in range(2):
                    c = 2 * panel + m
                    dve.wait_ge(evicted, 2 * (PAN["ao"] + panel) + m + 1)
                    V.tensor_tensor(mixed[:, c, :], mixed[:, c, :], gtmp[:, m, :], ALU.add).then_inc(mix_sum, 1)
                for m in range(2):
                    c = 2 * panel + m
                    dve.wait_ge(mix_sum, c + 1)
                    dve.wait_ge(mix_high, c + 1)
                    V.tensor_tensor(mix_lo[:, c, :], mixed[:, c, :], mix_hi[:, c, :].bitcast(F32), ALU.subtract).then_inc(mix_ready, 1)
            for panel in range(4):
                done("mix", panel)
                for m in range(2):
                    c = 2 * panel + m
                    dve.wait_ge(x_in[c // 2], 32)
                    V.tensor_tensor(XT[:, c, :], XT[:, c, :], psum_fm("mix", panel, m), ALU.add).then_inc(evicted, 1)
                for m in range(2):
                    c = 2 * panel + m
                    dve.wait_ge(evicted, 2 * PAN["mix"] + c + 1)
                    low(opA_lo[:, c, :], XT[:, c, :], col("norm_ffn", c), opA_hi[:, c, :])
                    add_squares(1, c)
            norm(1)

            with dve.Fori(0, FP) as i:
                T = 2 * PAN["ffn1"]
                done("ffn1", 0, i)
                wait(dve, hid_ready, 2 * i)
                for m in range(2):
                    V.tensor_tensor(facc[:, m, :], psum_fm("ffn1", 0, m), rstd_bc[:], ALU.mult).then_inc(evicted, 1)
                done("ffn1", 1, i)
                for m in range(2):
                    V.tensor_tensor(facc[:, 2 + m, :], psum_fm("ffn1", 1, m), rstd_bc[:], ALU.mult).then_inc(evicted, 1)
                for m in range(2):
                    dve.wait_ge(fgate, 2 * i + m + 1)
                    dve.wait_ge(evicted, T + 4 * i + 3 + m)
                    V.tensor_tensor(facc[:, 2 + m, :], facc[:, 2 + m, :], fg[:, m, :], ALU.mult).then_inc(fprod, 1)
                for m in range(2):
                    dve.wait_ge(hid_high, 2 * i + m + 1)
                    V.tensor_tensor(hid_lo[:, bass.ds(2 * i + m, 1), :], facc[:, 2 + m:3 + m, :], hid_hi[:, bass.ds(2 * i + m, 1), :].bitcast(F32),
                                    ALU.subtract).then_inc(hid_ready, 1)
            for panel in range(4):
                done("down1", panel)
                for m in range(2):
                    c = 2 * panel + m
                    V.tensor_tensor(XT[:, c, :], XT[:, c, :], psum_fm("down1", panel, m), ALU.add).then_inc(evicted, 1)
                for m in range(2):
                    add_squares(2, 2 * panel + m)
            norm(2)

            def lows(k, dst, hi, name, first, c):
                low(dst[:, c, :], XT[:, c, :], col(name, first + c), hi[:, c, :])
                add_squares(k, c)

            dve.wait_ge(sq_ready, 8 * 3)
            for c in range(DC):
                V.scalar_tensor_tensor(XT[:, c, :], XT[:, c, :], col("norm_final", c), rstd_bc[:], ALU.mult, ALU.mult).then_inc(res_ready, 1)
                if c:
                    dve.wait_ge(res_ready, c)
                    lows(3, opA_lo, opA_hi, "a_norm_pre_2", 0, c - 1)
            dve.wait_ge(res_ready, DC)
            lows(3, opA_lo, opA_hi, "a_norm_pre_2", 0, DC - 1)

            def take_branch(key, k):
                for panel in range(4):
                    done(key, panel)
                    for m in range(2):
                        V.tensor_copy(branch[:, 2 * panel + m, :], psum_fm(key, panel, m)).then_inc(evicted, 1)
                    for m in range(2):
                        add_squares(k, 2 * panel + m)
                norm(k)

            n_res = [DC]

            def residual(name, first, nxt):
                for c in range(DC):
                    n = n_res[0] + c - DC
                    V.tensor_tensor(branch[:, c, :], branch[:, c, :], rstd_bc[:], ALU.mult).then_inc(res_scaled, 1)
                    dve.wait_ge(res_scaled, n + 1)
                    V.scalar_tensor_tensor(XT[:, c, :], branch[:, c, :], col(name, first + c), XT[:, c, :], ALU.mult, ALU.add).then_inc(res_ready, 1)
                    if nxt and c:
                        dve.wait_ge(res_ready, n_res[0] + c)
                        nxt(c - 1)
                n_res[0] += DC
                if nxt:
                    dve.wait_ge(res_ready, n_res[0])
                    nxt(DC - 1)

            def fin(l):
                T = 2 * PAN[("fin", l)]
                V.memset(fu[:, :, 0:2], 0.0).then_inc(pads, 1)
                dve.wait_ge(pads, 2 + l)
                with dve.Fori(0, FP) as i:
                    for half in range(2):
                        done(("fin", l), half, i)
                        for m in range(2):
                            j = 2 * half + m
                            V.tensor_tensor(fu[:, j, 2:2 + S], psum_fm(("fin", l), half, m), rstd_bc[:], ALU.mult).then_inc(evicted, 1)
                        for tap in range(2):
                            for m in range(2):
                                j = 2 * half + m
                                if tap == 0:
                                    dve.wait_ge(fconv_t0, 44 * l + 4 * i + j + 1)
                                else:
                                    dve.wait_ge(fconv_tap, 88 * l + 8 * i + 4 * half + 1 + m)
                                V.scalar_tensor_tensor(facc[:, j, :], fu[:, j, tap:tap + S], col("ffn_conv_w_2", 132 * l + 44 * tap + FT * half + m + 2 * i),
                                                       facc[:, j, :], ALU.mult, ALU.add).then_inc(fconv_tap, 1)
                    for m in range(2):
                        dve.wait_ge(fgate, FT * (l + 1) + 2 * i + m + 1)
                        dve.wait_ge(fconv_tap, 88 * l + 8 * i + 7 + m)
                        V.tensor_tensor(facc[:, 2 + m, :], facc[:, 2 + m, :], fg[:, m, :], ALU.mult).then_inc(fprod, 1)
                    for m in range(2):
                        dve.wait_ge(hid_high, FT * (l + 1) + 2 * i + m + 1)
                        V.tensor_tensor(hid_lo[:, bass.ds(2 * i + m, 1), :], facc[:, 2 + m:3 + m, :], hid_hi[:, bass.ds(2 * i + m, 1), :].bitcast(F32),
                                        ALU.subtract).then_inc(hid_ready, 1)

            def qkv2(key):
                name, j = key
                if name[0] == "v":
                    values_panel(key, v2[j % 2], 0)
                    return
                done(key, 0)
                for m in range(2):
                    if name[0] == "q":
                        V.scalar_tensor_tensor(q2[j % 2][:, m, :], psum_fm(key, 0, m), 0.125, rstd_bc[:], ALU.mult, ALU.mult).then_inc(evicted, 1)
                    else:
                        V.tensor_tensor(k2[j % 2][:, m, :], psum_fm(key, 0, m), rstd_bc[:], ALU.mult).then_inc(evicted, 1)

            def softmax_units(names, fox):
                for tok in order2(names):
                    kind, u = tok[0], tok[1]
                    if kind == "half":
                        continue
                    if kind == "epi":
                        qkv2(tok[1])
                        continue
                    U = 32 * fox + u
                    tile, qb = u // NB, u % NB
                    width = (qb + 1) * P
                    st = bstat[:, u % 4]
                    if kind == "M":
                        dve.wait_ge(s2_done, U + 1)
                        if fox:
                            wait(dve, tr2_done, 32 + 2 * u - 2 if u > 1 else 0)
                        x = sc[:, u % 2, :, 0:width]
                        if fox:
                            dve.wait_ge(negc_in[tile % 2], 16 * (tile // 2 + 1))
                            dve.wait_ge(ccol_ready, 1)
                            for e in range(2):
                                ins = V.scalar_tensor_tensor(x[:, e], negc[:, tile % 2, e, 0:width], ccol[:, qb, 2 * tile + e:2 * tile + e + 1],
                                                             AUX[:, e, 0:width], ALU.subtract, ALU.add)
                            ins.then_inc(sc_ready, 1)
                        else:
                            if u == 0:
                                dve.wait_ge(tbias_in, 16)
                            V.tensor_tensor(x, AUX[:, 0:2, 0:width], tbias[:, tile, S - width:S].unsqueeze(1).broadcast_to([P, 2, width]),
                                            ALU.add).then_inc(sc_ready, 1)
                        dve.wait_ge(sc_ready, U + 1)
                        V.tensor_reduce(st[:, 0:2], x, AX.X, ALU.max).then_inc(max2, 1)
                        dve.wait_ge(max2, U + 1)
                        V.tensor_scalar(st[:, 2:4], st[:, 0:2], -1.0, None, ALU.mult).then_inc(negmax2, 1)
                    elif kind == "T" and fox:
                        dve.wait_ge(tr2_done, 32 + 2 * u + 2)
                        wait(dve, pv2_done, U)
                        V.tensor_copy(pT[:, 1, 0:qb + 1, :], AUX[:, 3, 0:width].rearrange("p (b q) -> p b q", q=P)).then_inc(pT2_dve, 1)
                    elif kind == "D":
                        dve.wait_ge(exp2, 2 * U + 2)
                        V.reciprocal(st[:, 6:8], st[:, 4:6]).then_inc(r2_step, 1)
                        if not fox:
                            wait(dve, tr2_done, u - 1)
                            r0 = 4 * u
                            dve.wait_ge(r2_step, r0 + 1)
                            V.tensor_scalar(st[:, 10:11], st[:, 7:8], lams[:, 4:5], None, ALU.mult).then_inc(r2_step, 1)
                            dve.wait_ge(r2_step, r0 + 2)
                            V.tensor_scalar(dif[:, u % 2, 0:width], sc[:, u % 2, 1, 0:width], st[:, 10:11], None, ALU.mult).then_inc(r2_step, 1)
                            dve.wait_ge(r2_step, r0 + 3)
                            V.scalar_tensor_tensor(dif[:, u % 2, 0:width], sc[:, u % 2, 0, 0:width], st[:, 6:7], dif[:, u % 2, 0:width],
                                                   ALU.mult, ALU.subtract).then_inc(r2_step, 1)
                    elif kind == "W":
                        wait(dve, ot2_done, U - 1)
                        if fox:
                            dve.wait_ge(pv2_done, U + 1)
                            dve.wait_ge(r2_step, 128 + u + 1)
                            for e in range(2):
                                V.tensor_scalar(osb2[:, u % 2, 64 * e:64 * e + 64], AUX[:, 2, 64 * e:64 * e + 64], st[:, 6 + e:7 + e], None,
                                                ALU.mult).then_inc(o2_read, 1)
                        else:
                            dve.wait_ge(o2_stat, 2 * u + 2)
                            V.reciprocal(st[:, 11:12], st[:, 9:10]).then_inc(o2_rstd, 1)
                            dve.wait_ge(o2_rstd, u + 1)
                            V.tensor_scalar(osb2[:, u % 2, :], AUX[:, 3, 0:P], st[:, 11:12], None, ALU.mult).then_inc(o2_read, 1)

            def wo_operand():
                for c in range(DC):
                    low(opA_lo[:, c, :], oT[:, c, :], None, opA_hi[:, c, :])

            dve.wait_ge(lam_act, 2)
            V.scalar_tensor_tensor(lams[:, 4:5], lams[:, 2:3], LAM0, lams[:, 3:4], ALU.add, ALU.subtract).then_inc(lam_step, 1)
            dve.wait_ge(lam_step, 4)
            norm(3)
            for name in ("q2", "k2", "v2"):
                qkv2((name, 0))
            softmax_units(("q2", "k2", "v2"), 0)
            wo_operand()
            take_branch("awo", 4)
            residual("a_norm_post_2", 0, lambda c: lows(5, opA_lo, opA_hi, "ffn_norm_pre_2", 0, c))
            norm(5)
            fin(0)
            take_branch(("fout", 0), 6)
            residual("ffn_norm_post_2", 0, lambda c: lows(7, opA_lo, opA_hi, "kv_norm_2", 0, c))
            for c in range(DC):
                low(opB_lo[:, c, :], XT[:, c, :], col("b_norm_pre_2", c), opB_hi[:, c, :])
            norm(7)
            done("f", 0)
            V.tensor_tensor(fx[:], psum_fm("f", 0, 0)[0:BH, :], rstd_bc[0:BH, :], ALU.mult).then_inc(evicted, 2)
            step, q, a = softplus((fa, fe, fr, fz, fz2, fq), 19, 3)
            step(V.scalar_tensor_tensor(fz[:], q[:], 2.0, a[:], ALU.mult, ALU.add))
            step(V.memset(fr[:], 1.0))
            step(V.tensor_tensor_scan(fc[:], fr[:], fz[:], 0.0, ALU.mult, ALU.add))
            for name in ("q3", "k3", "v3"):
                qkv2((name, 0))
            softmax_units(("q3", "k3", "v3"), 1)
            wo_operand()
            take_branch("bwo", 8)
            residual("b_norm_post_2", 0, lambda c: lows(9, opA_lo, opA_hi, "ffn_norm_pre_2", 8, c))
            norm(9)
            fin(1)
            take_branch(("fout", 1), 10)
            residual("ffn_norm_post_2", 8, None)

    return nc


def shape_constants():
    f = np.float32
    c = {}
    d = S - 1 - np.arange(LINE)
    exact = BUCKETS // 2
    far = exact + (np.log(np.maximum(d, 1).astype(f) / f(exact)) / f(math.log(128 / exact)) * f(BUCKETS - exact)).astype(np.int32)
    bucket = np.where(np.maximum(d, 0) < exact, np.maximum(d, 0), np.minimum(far, BUCKETS - 1))
    c["c_onehot"] = (bucket[None, :] == np.arange(BUCKETS)[:, None]).astype(f)
    c["c_future"] = np.broadcast_to(np.where(d < 0, f(NEG), f(0)), (P, LINE)).astype(f)
    c["c_ident"] = np.eye(P, dtype=f)
    c["c_ones"] = np.ones((P, P), f)
    c["c_tri"] = (np.arange(P)[None, :] >= np.arange(P)[:, None]).astype(f)
    q, k = np.arange(P)[:, None], np.arange(P)[None, :]
    parts = []
    for dilation in (4, 16):
        same = (q - k) % dilation == 0
        parts += [same] * (NB - 1) + [same & (k <= q)]
    parts += [k >= q, k <= q]
    c["c_mask"] = np.where(np.concatenate(parts, 1), f(0), f(NEG))
    inv = f(10000.0) ** (-np.arange(ADIM // 2, dtype=f) / f(ADIM // 2))
    angle = np.arange(S, dtype=f)[None, :] * inv[:, None]
    c["c_cos"] = np.concatenate([np.cos(angle)] * 2).astype(f)
    c["c_sin"] = np.concatenate([np.sin(angle), -np.sin(angle)]).astype(f)
    return c


def kernel(**inputs):
    import concourse.bacc as bacc
    from concourse.bass_utils import run_bass_kernel_spmd

    a = {n: np.asarray(v) for n, v in inputs.items()}
    data = {"xT": a["x"][0].T}
    for n in WEIGHTS:
        data[n] = a[n[:-2]][int(n[-1])] if n[:-2] in a else a[n].reshape(a[n].shape[-2:])
    data["vec"] = np.concatenate([a[n].reshape(-1, P) for n, _ in VEC]).T
    data["dtv"] = np.stack([a["dt_bias"][0], a["a_log"][0]], 1)
    data["bfv"] = a["b_f_2"].reshape(BH, 1)
    data["d_skip"] = a["d_skip"].reshape(NH)
    data["lam"] = np.concatenate([a[n].reshape(-1) for n in ("a_lam_q1_2", "a_lam_k1_2", "a_lam_q2_2", "a_lam_k2_2")])
    data["ssm_norm"] = a["ssm_norm"].reshape(DI)
    data["rel_bias_2"] = a["rel_bias_2"]
    data.update(shape_constants())

    nc = bacc.Bacc("TRN2", target_bir_lowering=False, num_devices=1)
    arrays, I = {}, {}
    for n, v in data.items():
        arrays[f"in_{n}_dram"] = v = np.ascontiguousarray(v)
        I[n] = nc.dram_tensor(f"in_{n}_dram", v.shape, mybir.dt.from_np(v.dtype), kind="ExternalInput").ap()
    out = nc.dram_tensor("out_0_dram", (D, S), F32, kind="ExternalOutput").ap()
    build(nc, I, out)
    r = run_bass_kernel_spmd(nc, [arrays], core_ids=[0])
    return np.ascontiguousarray(r.results[0]["out_0_dram"].T).reshape(1, S, D)
```

```python
import math
from contextlib import ExitStack

import numpy as np
import concourse.bass as bass
from concourse import mybir

F32 = mybir.dt.float32
F32R = mybir.dt.float32r
BF16 = mybir.dt.bfloat16
ACT = mybir.ActivationFunctionType
ALU = mybir.AluOpType
AX = mybir.AxisListType

P = 128
S = 512
NB = S // P
D = 1024
DC = D // P
PANEL = 256
SLAB = 2
WARM_SQUARES, WARM_FACTORS, WARM_RESIDUAL, WARM_BANKS, WARM_UNIT = 14, 15, 14, 9, 7
WARM_START = 6
RAW = 8
SPL = 4
EPS, SUB_EPS = 1e-6, 1e-5
NEG = -1e30

DI, HD, NG, NS, KCONV = 2048, 64, 4, 128, 4
NH = DI // HD
HG = NH // NG
GW = DI // NG
XBC = DI + 2 * NG * NS
AH, AG = 4, 3
ADIM = 128
QKV0 = DI + XBC + NH
GATE0 = QKV0 + 3 * AH * AG * ADIM
DFF = 2816
FT = DFF // P
FP = DFF // PANEL
H2 = 8
PAIRS = 4
BH = 16
BUCKETS = 32
LINE = S + P
LAM0 = 0.8 - 0.6 * math.exp(0.0)

VEC = [("norm_mix", 8), ("b_gate", 16), ("conv_w", 96), ("conv_b", 24), ("norm_ffn", 8), ("norm_final", 8),
       ("a_norm_pre_2", 8), ("a_norm_post_2", 8), ("a_subln_2", 1), ("kv_norm_2", 8), ("b_norm_pre_2", 8),
       ("b_norm_post_2", 8), ("ffn_norm_pre_2", 16), ("ffn_norm_post_2", 16), ("ffn_conv_w_2", 264),
       ("ffn_conv_b_2", 88)]
COL, NCOL = {}, 0
for _n, _w in VEC:
    COL[_n] = NCOL
    NCOL += _w

K512, K1024, K2816 = ((SLAB,) * (k // P // SLAB) for k in (GW, D, DFF))
STREAM = [("C", 2, K1024), ("B", 2, K1024), ("dt", 1, K1024), (("xs", 0), 2, K1024)]
for _g in range(NG):
    STREAM.append((("z", _g), 2, K1024))
    if _g:
        STREAM.append((("so", _g - 1), 4, K512))
    if _g < NG - 1:
        STREAM.append((("xs", _g + 1), 2, K1024))


def QKV1(j):
    if j == 0:
        return [("v1", 0, 0), ("v1", 0, 1)] + [(n, 0, gi) for gi in range(AG) for n in ("q1", "k1")] + [("v1", 0, 2)]
    return [(n, j, gi) for gi in range(AG) for n in ("q1", "k1", "v1")]


STREAM += [(k, 1, K1024) for k in QKV1(0)[:2]] + [(("so", 3), 4, K512)]
STREAM += [(k, 1, K1024) for k in QKV1(0)[2:] + QKV1(1)]
STREAM += [("gates", 8, K1024), ("ao", 4, K512), ("mix", 4, K1024), ("ffn1", 2 * FP, K1024), ("down1", 4, K2816)]
STREAM += [((n, j), 1, K1024) for j in range(PAIRS) for n in ("q2", "k2", "v2")]
STREAM += [("awo", 4, K1024), (("fin", 0), 2 * FP, K1024), (("fout", 0), 4, K2816)]
STREAM += [(k, 1, K1024) for k in (("k3", 0), "f", ("v3", 0), ("q3", 0))]
STREAM += [((n, j), 1, K1024) for j in range(1, PAIRS) for n in ("q3", "k3", "v3")]
STREAM += [("bwo", 4, K1024), (("fin", 1), 2 * FP, K1024), (("fout", 1), 4, K2816)]
PAN, SLB, SPLIT, NPAN = {}, {}, {}, {}
_p = _s = 0
for _k, _n, _c in STREAM:
    PAN[_k], SLB[_k], SPLIT[_k], NPAN[_k] = _p, _s, _c, _n
    _p += _n
    _s += _n * len(_c)
SLABS = _s


TWINS = {(a, 0): b for a, b in (("C", ("C", 1)), ("ffn1", ("ffn1", 1)), (("q2", 0), (("k2", 0), 0)), ("awo", ("awo", 1)),
                                (("fin", 0), (("fin", 0), 1)), (("k3", 0), ("f", 0)), ("bwo", ("bwo", 1)), (("fin", 1), (("fin", 1), 1)))}
SECOND = {b: a for a, b in TWINS.items()}


def slab_no(key, panel, k):
    if (key, panel) in TWINS:
        return SLB[key] + 2 * k
    if (key, panel) in SECOND:
        return SLB[SECOND[key, panel][0]] + 2 * k + 1
    return SLB[key] + panel * len(SPLIT[key]) + k


def slab_end(key, panel):
    return slab_no(key, panel, len(SPLIT[key]) - 1) + 1


SCAN = []
for _g in range(NG):
    _u = 4 * _g
    _z, _so, _xs = ("z", _g), ("so", _g - 1), ("xs", _g + 1)
    SCAN += [("mm", _z, 0)] + [("Cp", _u - 2)] * (_g > 0) + [("xt", _u + 2), ("xt", _u + 3), ("G", _g), ("A", _u)]
    SCAN += [("N", _u - 1)] * (_g > 0) + [("epi", _z, 0), ("mm", _z, 1)] + [("Cp", _u - 1)] * (_g > 0) + [("A", _u + 1), ("epi", _z, 1)]
    for _h in range(4):
        if _g:
            SCAN.append(("mm", _so, _h))
        SCAN += ([("Bp", _u)], [("A", _u + 2), ("N", _u)], [("Bp", _u + 1)], [("Cp", _u), ("A", _u + 3), ("N", _u + 1)])[_h]
        if _g:
            SCAN.append(("epi", _so, _h))
    if _g < NG - 1:
        SCAN += [("mm", _xs, 0), ("Cp", _u + 1), ("Bp", _u + 2), ("epi", _xs, 0)]
        SCAN += [("mm", _xs, 1), ("xt", _u + 4), ("xt", _u + 5), ("N", _u + 2), ("Bp", _u + 3), ("epi", _xs, 1)]
_va, _vb = QKV1(0)[:2]
SCAN += [("mm", _va, 0, 0, 2), ("Cp", 13), ("Bp", 14), ("mm", _va, 0, 2, 4), ("N", 14), ("Bp", 15), ("mm", _vb, 0, 0, 2), ("Cp", 14),
         ("mm", _vb, 0, 2, 3), ("N", 15), ("mm", _vb, 0, 3, 4), ("Cp", 15), ("epi", _va, 0), ("epi", _vb, 0)]
for _h in range(4):
    SCAN += [("mm", ("so", 3), _h), ("epi", ("so", 3), _h)]
USE0 = {t: n for n, t in enumerate([("xt", 0), ("xt", 1)] + [t for t in SCAN if t[0] in ("xt", "Cp")])}
USE1, READ1, LAST1 = {}, {}, {}
_last = None
for _t in SCAN:
    if _t[0] == "G" or _t[0] == "A" or (_t[0] == "Bp" and _t[1] % NB < NB - 1):
        USE1[_t] = len(USE1)
        LAST1[_t] = _last
        _last = _t
        if _t[0] != "Bp":
            READ1[_t] = len(READ1)
YSTEPS = [0]
for _u in range(16):
    YSTEPS.append(YSTEPS[-1] + (3 if _u % NB == 0 else 5))
STSTEPS = [0]
for _u in range(16):
    STSTEPS.append(STSTEPS[-1] + (1, 2, 2, 0)[_u % NB])

ATT1 = []
_fill = [("slab", k, 0, h) for k in QKV1(1) for h in range(4)], [("slab", "gates", n, h) for n in range(8) for h in range(4)]
for _j in range(2):
    slots = 0
    for _u in range(8 * _j, 8 * _j + 8):
        ATT1.append(("S", _u))
        if _u:
            ATT1.append(("X", _u - 1))
        for _part in ("T", "V"):
            for t in _fill[_j][len(_fill[_j]) * slots // 16:len(_fill[_j]) * (slots + 1) // 16]:
                ATT1.append(t)
                if t[3] == len(K1024) - 1:
                    ATT1.append(("epi", t[1], t[2]))
            slots += 1
            ATT1.append((_part, _u))
ATT1.append(("X", 15))


def w1(qb):
    return (qb + 1) * P, P if qb == 0 else 2 * P


def nblk(qb):
    return 2 * (qb + 1) + (1 if qb == 0 else 2)


TB, TA, TV = [0], [0], [0]
for _u in range(16):
    _n = -(-nblk(_u % 4) // 4)
    TB.append(TB[-1] + _n)
    TA.append(TA[-1] + (_n + 1) // 2)
    TV.append(TV[-1] + _n // 2)


def order2(names):
    project = "awo" if names[0] == "q2" else "bwo"
    out = [("S", 0), ("S", 1), ("M", 0), ("D", 0)]
    late = []
    for j in range(PAIRS):
        fill = [("slab", (n, j + 1), 0, h) for n in names for h in range(4)] if j < PAIRS - 1 else []
        for n in range(9, len(fill) + 3, 2):
            fill.insert(n, None)
        if j == PAIRS - 1:
            fill = [None] * 2 + [("slab", project, n, k) for k in range(3) for n in range(2)]
        for u in range(8 * j, 8 * j + 8):
            if u < 31:
                out.append(("M", u + 1))
            out += [("W", u - 1)] * (u > 0 and names[0] == "q3") + [("T", u)]
            if u < 30:
                out.append(("S", u + 2))
            out += [("W", u - 1)] * (u > 0 and names[0] != "q3")
            if u < 31:
                out.append(("D", u + 1))
            out += late
            late = []
            done = (u - 5) // NB
            if u % NB == 1 and u > NB and names[0] == "q2":
                out.append(("Y", done))
            for part in ("V", "X"):
                if part == "X" and u % NB == 2 and u > NB:
                    out.append(("X", done))
                if fill and (j < PAIRS - 1 or part == "X"):
                    t = fill.pop(0)
                    out += [t] * (t is not None)
                    if t is not None and t[1] != project and t[3] == len(K1024) - 1:
                        late = [("epi", t[1], t[2])]
                if part == "V":
                    out.append(("V", u))
            if u in range(24, 31):
                out.append(("O", u - 24))
    return out + [("W", 31)] + [("Y", 7)] * (names[0] == "q2") + [("X", 7), ("O", 7)]
WEIGHTS = ["w_in", "w_ssm_out", "w_att_out", "w_mix_out", "w_ffn_gate", "w_ffn_up", "w_ffn_down", "a_w_qkv_2", "a_w_o_2", "w_kvf_2",
           "b_w_q_2", "b_w_o_2", "ffn_w_in_2_0", "ffn_w_in_2_1", "ffn_w_out_2_0", "ffn_w_out_2_1"]


def build(nc, I, out):
    ctx = ExitStack()
    with ctx:
        def sem(n):
            return ctx.enter_context(nc.semaphore(n))

        class Region:
            def __init__(self, at, end):
                self.at, self.end = at, end

            def put(self, n, shape, dt=F32):
                size = -(-int(np.prod(shape[1:])) * (2 if dt == BF16 else 4) // 32) * 32
                assert self.at + size <= self.end, (n, self.at + size - self.end)
                t = nc.alloc_sbuf_tensor_at(n, list(shape), dt, offset=self.at)
                self.at += size
                return t

        KB = 1024
        BASE = -(-nc.sbuf_base // 64) * 64
        TOP = nc.sbuf_usable_end // 64 * 64
        r = Region(BASE, TOP)
        raw = [r.put(f"raw{i}", [P, SLAB, PANEL]) for i in range(RAW)]
        whi = [r.put(f"whi{i}", [P, SLAB, PANEL], F32R) for i in range(SPL)]
        wlo = [r.put(f"wlo{i}", [P, SLAB, PANEL], F32R) for i in range(SPL)]
        opA_hi = r.put("opA_hi", [P, DC, S], F32R)
        opA_lo = r.put("opA_lo", [P, DC, S], F32R)
        vec = r.put("vec", [P, NCOL])
        ident = r.put("ident", [P, P])
        zero = r.put("zero", [P, 1])
        ones = r.put("ones", [P, P])
        tri = r.put("tri", [P, P])
        norm_tmp = r.at
        sq = r.put("sq", [P, 2, S])
        acc = r.put("acc", [P, S])
        r.at = norm_tmp + 8 * KB
        rstd_bc = r.put("rstd_bc", [P, S])
        std = r.put("std", [P, NB])
        rstd_col = r.put("rstd_col", [P, NB])
        lamv = r.put("lamv", [P, 4, 64])
        lamt = r.put("lamt", [P, 2, 64])
        lams = r.put("lams", [P, 8])
        subg = r.put("subg", [P, 1])
        dsk = r.put("dsk", [P, NH])
        dtv = r.put("dtv", [P, 3, NH])
        bfv = r.put("bfv", [P, BH])
        mask1 = r.put("mask1", [P, 2 * S + 2 * P], BF16)
        ident_bf = r.put("ident_bf", [P, P], BF16)
        A0 = r.at
        XT_AT = TOP - 16 * KB
        XT = Region(XT_AT, TOP).put("XT", [P, DC, S])
        r = Region(A0, XT_AT)
        oneh = r.put("oneh", [BUCKETS, LINE])
        relb = r.put("relb", [BUCKETS, H2])
        relw = r.put("relw", [BUCKETS, H2, P])
        future = r.put("future", [P, LINE])
        line = r.put("line", [P, H2, LINE])
        mask_in = r.put("mask_in", [P, 2 * S + 2 * P])
        r = Region(A0, TOP)
        yT_hi = r.put("yT_hi", [P, 4, S], F32R)
        yT_lo = r.put("yT_lo", [P, 4, S], F32R)
        y_ssm = r.put("y_ssm", [P, DC, S])
        AFTER_Y = r.at
        xs_tok = r.put("xs_tok", [P, 2, NB, GW])
        zbuf = r.put("zbuf", [P, NB, GW])
        bcf = r.put("bcf", [P, 2 * NG, S])
        btok = r.put("btok", [P, NB, P])
        tokc = r.put("tokc", [P, NB, 4, NH])
        acs_row = r.put("acs_row", [P, 2, HG, P])
        M_AT = r.at
        M = r.put("M", [P, 2, HG, P])
        xdt = r.put("xdt", [P, 2, GW])
        xdd_at = r.at
        xdd = r.put("xdd", [P, 2, GW])
        state = r.put("state", [P, GW])
        y_at = r.at
        yb = r.put("yb", [P, GW])
        yt = r.put("yt", [P, GW])
        yoffb = r.put("yoffb", [P, GW])
        yn = r.put("yn", [P, 3, GW])
        cbm = r.put("cbm", [P, 2, P])
        gain = r.put("gain", [P, 2, GW])
        etot = r.put("etot", [P, 2, HG])
        ystat = r.put("ystat", [P, 2, 4])
        cu = r.put("cu", [P, 2, S + KCONV - 1])
        cacc = Region(norm_tmp, norm_tmp + 4 * KB).put("cacc", [P, 2, S])
        xsf = Region(norm_tmp + 4 * KB, norm_tmp + 8 * KB).put("xsf", [P, 2, S])
        r = Region(A0, A0 + 16 * KB)
        dx, da, de, dr, dz, dz2, dq, ddec = [r.put(n, [P, NB, NH]) for n in ("dx", "da", "de", "dr", "dz", "dz2", "dq", "ddec")]
        dacs, dt_rows = r.put("dacs", [NH, S]), r.put("dt_rows", [NH, S])
        r = Region(A0, TOP)
        o1_hi = r.put("o1_hi", [P, AH, S], F32R)
        o1_lo = r.put("o1_lo", [P, AH, S], F32R)
        assert r.at == A0 + 16 * KB
        r.at = AFTER_Y
        q1, k1, v1, pair_at = [], [], [], []
        for j in range(2):
            pair_at.append(r.at)
            q1.append(r.put(f"q1_{j}", [P, 2 * AG, S]))
            k1.append(r.put(f"k1_{j}", [P, 2 * AG, S]))
            v1.append(r.put(f"v1_{j}", [P, NB, AG * PANEL]))
        prob = r.put("prob", [P, 2 * S + 2 * P])
        probT = r.put("probT", [P, 10, P])
        osb = r.put("osb", [P, 2, P])
        cosr = r.put("cosr", [P, S])
        sinr = r.put("sinr", [P, S])
        rsin = r.put("rsin", [P, 2, S])
        astat = r.put("astat", [P, 2, 8])
        r = Region(pair_at[0], pair_at[1])
        mixed = r.put("mixed", [P, DC, S])
        gate1 = r.put("gate1", [P, DC, S])
        r = Region(pair_at[1], XT_AT)
        mix_hi = r.put("mix_hi", [P, DC, S], F32R)
        mix_lo = r.put("mix_lo", [P, DC, S], F32R)
        gtmp = Region(norm_tmp, norm_tmp + 4 * KB).put("gtmp", [P, 2, S])
        r = Region(A0, XT_AT)
        hid_hi = r.put("hid_hi", [P, FT, S], F32R)
        hid_lo = r.put("hid_lo", [P, FT, S], F32R)
        F_AT = r.at
        fu = r.put("fu", [P, 4, S + 2])
        facc = r.put("facc", [P, 4, S])
        fg = r.put("fg", [P, 2, S])
        branch = Region(F_AT, XT_AT).put("branch", [P, DC, S])
        r = Region(A0, XT_AT)
        opB_hi = r.put("opB_hi", [P, DC, S], F32R)
        opB_lo = r.put("opB_lo", [P, DC, S], F32R)
        tbias = Region(A0, A0 + 16 * KB).put("tbias", [P, H2, S])
        q2 = [r.put(f"q2_{j}", [P, 2, S]) for j in range(2)]
        k2 = [r.put(f"k2_{j}", [P, 2, S]) for j in range(2)]
        v2 = [r.put(f"v2_{j}", [P, NB, PANEL]) for j in range(2)]
        oT = r.put("oT", [P, DC, S])
        sc = r.put("sc", [P, 2, 2, S])
        pT = r.put("pT", [P, 2, NB, P])
        dif = Region(A0 + 16 * KB, A0 + 20 * KB).put("dif", [P, 2, S])
        osb2 = r.put("osb2", [P, 2, NB, P])
        osq = r.put("osq", [P, P])
        ostat = r.put("ostat", [P, 2, 3 * NB])
        bstat = r.put("bstat", [P, 4, 16])
        ccol = r.put("ccol", [P, NB, BH])
        negc = r.put("negc", [P, 2, 2, S])
        r = Region(A0 + 64 * KB, A0 + 80 * KB)
        fx, fa, fe, fr, fz, fz2, fq = [r.put(n, [P, NB, BH]) for n in ("fx", "fa", "fe", "fr", "fz", "fz2", "fq")]
        fc, f_rows = r.put("fc", [BH, S]), r.put("f_rows", [BH, S])
        PS = ctx.enter_context(nc.psum_tensor("PS", [P, 4, S], F32))
        AUX = ctx.enter_context(nc.psum_tensor("AUX", [P, 4, S], F32))
        x_in = [sem(f"x_in{n}") for n in range(4)]
        warm_ready = sem("warm_ready")
        first_in, const_in = sem("first_in"), sem("const_in")
        w_loaded = [sem(f"w_loaded{n}") for n in range(RAW)]
        slab_go, w_high, slab_split = sem("slab_go"), sem("w_high"), sem("slab_split")
        zero_ready = sem("zero_ready")
        slab_done = sem("slab_done")
        evicted = sem("evicted")
        op_hi, op_ready = sem("op_hi"), sem("op_ready")
        sq_ready, acc_ready = sem("sq_ready"), sem("acc_ready")
        ss_done, std_ready, rstd_ready = sem("ss_done"), sem("std_ready"), sem("rstd_ready")
        bc_done, bc_ready = sem("bc_done"), sem("bc_ready")
        relw_ready, line_mm, line_ready, bias_out, tbias_in = (sem(n) for n in ("relw_ready", "line_mm", "line_ready", "bias_out", "tbias_in"))
        pads = sem("pads")
        conv_t0, conv_tap, xbc_ready = sem("conv_t0"), sem("conv_tap"), sem("xbc_ready")
        narrow_done = sem("narrow_done")
        sp_act, sp_step = sem("sp_act"), sem("sp_step")
        a_exp, cum_done, dec_ready, tokc_ready, acs_ready, acs_out = (sem(n) for n in ("a_exp", "cum_done", "dec_ready", "tokc_ready", "acs_ready", "acs_out"))
        acs_in = [sem(f"acs_in{n}") for n in range(2)]
        gain_in = [sem(f"gain_in{n}") for n in range(2)]
        aux0_done, aux0_read, aux1_done, aux1_read = (sem(n) for n in ("aux0_done", "aux0_read", "aux1_done", "aux1_read"))
        decay_step, decay_exp, m_step, xdt_ready, xdd_ready = (sem(n) for n in ("decay_step", "decay_exp", "m_step", "xdt_ready", "xdd_ready"))
        ydiag_done, yoff_done, y_step, y_stat, y_rstd, yn_ready, y_hi = (sem(n) for n in ("ydiag_done", "yoff_done", "y_step", "y_stat", "y_rstd", "yn_ready", "y_hi"))
        state_step, z_ready = sem("state_step"), sem("z_ready")
        rope_in, rope_scaled, rope_done = sem("rope_in"), sem("rope_scaled"), sem("rope_done")
        s1_done, max1, negmax1, exp1, den1, rden1 = (sem(n) for n in ("s1_done", "max1", "negmax1", "exp1", "den1", "rden1"))
        tr1_done, pT1_act, pT1_dve, pv1_done, o1_read, ot1_done, o1_high, o1_ready = (
            sem(n) for n in ("tr1_done", "pT1_act", "pT1_dve", "pv1_done", "o1_read", "ot1_done", "o1_high", "o1_ready"))
        gate_sig, gate_mul, mix_sum, mix_high, mix_ready = (sem(n) for n in ("gate_sig", "gate_mul", "mix_sum", "mix_high", "mix_ready"))
        fgate, fprod, hid_high, hid_ready = (sem(n) for n in ("fgate", "fprod", "hid_high", "hid_ready"))
        fconv_t0, fconv_tap = sem("fconv_t0"), sem("fconv_tap")
        res_scaled, res_ready = sem("res_scaled"), sem("res_ready")
        lam_step, lam_act = sem("lam_step"), sem("lam_act")
        s2_done, sc_ready, max2, negmax2, exp2, r2_step = (sem(n) for n in ("s2_done", "sc_ready", "max2", "negmax2", "exp2", "r2_step"))
        tr2_done, pT2_act, pT2_dve, pv2_done, o2_stat, o2_rstd, o2_read, ot2_done, oT_ready = (
            sem(n) for n in ("tr2_done", "pT2_act", "pT2_dve", "pv2_done", "o2_stat", "o2_rstd", "o2_read", "ot2_done", "oT_ready"))
        o2_std, o2_normed = sem("o2_std"), sem("o2_normed")
        c_out, c_done, ccol_ready = sem("c_out"), sem("c_done"), sem("ccol_ready")
        negc_in = [sem(f"negc_in{n}") for n in range(2)]
        stored = sem("stored")

        acs_dram = nc.dram_tensor("acs_dram", (NH, S), F32, kind="Internal").ap()
        c_dram = nc.dram_tensor("c_dram", (BH, S), F32, kind="Internal").ap()
        bias_dram = nc.dram_tensor("bias_dram", (H2, P, LINE), F32, kind="Internal").ap()

        W = {n: I[n].rearrange("(c p) n -> p c n", p=P) for n in WEIGHTS}
        xT = I["xT"]
        N_FIRST, N_CONST = 3, 9

        def wait(eng, s, v):
            if not isinstance(v, int) or v > 0:
                eng.wait_ge(s, v)

        def source(key, panel, i):
            name = key if isinstance(key, str) else key[0]
            a = None if isinstance(key, str) else key[1]
            flat = (panel + 2 * i) * PANEL
            twin = panel % 2, (panel // 2 + i) * PANEL
            if name in ("C", "B", "xs", "z"):
                first = {"C": DI + DI + NG * NS, "B": DI + DI, "xs": DI + GW * (a or 0), "z": GW * (a or 0)}[name]
                return W["w_in"], 0, first + flat, PANEL
            if name == "dt":
                return W["w_in"], 0, DI + XBC, NH
            if name in ("q1", "k1", "v1"):
                part = ("q1", "k1", "v1").index(name)
                return W["w_in"], 0, QKV0 + part * AH * AG * ADIM + (key[2] * AH + 2 * a) * ADIM, PANEL
            if name == "gates":
                return W["w_in"], 0, GATE0 + twin[0] * D + twin[1], PANEL
            if name == "so":
                return W["w_ssm_out"], 4 * a, flat, PANEL
            if name == "ffn1":
                return W[("w_ffn_gate", "w_ffn_up")[twin[0]]], 0, twin[1], PANEL
            if name == "fin":
                return W[f"ffn_w_in_2_{a}"], 0, twin[0] * DFF + twin[1], PANEL
            if name in ("q2", "k2", "v2"):
                return W["a_w_qkv_2"], 0, ("q2", "k2", "v2").index(name) * D + a * PANEL, PANEL
            if name in ("k3", "v3"):
                return W["w_kvf_2"], 0, ("k3", "v3").index(name) * D + a * PANEL, PANEL
            if name == "q3":
                return W["b_w_q_2"], 0, a * PANEL, PANEL
            if name == "f":
                return W["w_kvf_2"], 0, 2 * D, BH
            return W[{"ao": "w_att_out", "mix": "w_mix_out", "down1": "w_ffn_down", "awo": "a_w_o_2", "bwo": "b_w_o_2",
                      "fout": f"ffn_w_out_2_{a}"}[name]], 0, flat, PANEL

        def psum_fm(key, panel, m):
            return PS[:, 2 * ((PAN[key] + panel) % 2) + m, :]

        def psum_tm(key, panel):
            b = 2 * ((PAN[key] + panel) % 2)
            return PS[:, b:b + 2, :].rearrange("p b (t n) -> p (b t) n", n=PANEL)

        def place(key, panel, k, i):
            return slab_no(key, panel, k) if isinstance(i, int) else SLB[key] + panel * len(SPLIT[key]) + k

        TOKEN_MAJOR = ("z", "v1", "v2", "v3")
        block = ctx.enter_context(nc.Block())

        @block.sync
        def _(sp):
            def load_x(n):
                sp.dma_start(XT[:, 2 * n:2 * n + 2, :], xT.rearrange("(c p) t -> p c t", p=P)[:, 2 * n:2 * n + 2, :]).then_inc(x_in[n], 16)

            def fetch_slab(key, panel, k, i):
                w, c0, col, n = source(key, panel, i)
                c0, chunks = c0 + sum(SPLIT[key][:k]), SPLIT[key][k]
                s = place(key, panel, k, i)
                wait(sp, slab_split, s + 2 * len(SPLIT[key]) * i - RAW + 1)
                cols = slice(col, col + n) if isinstance(col, int) else bass.ds(col, n)
                sp.dma_start(raw[s % RAW][:, 0:chunks, 0:n], w[:, c0:c0 + chunks, cols]).then_inc(w_loaded[s % RAW], 16)

            def fetch(key, panel, i=0):
                for k in range(len(SPLIT[key])):
                    fetch_slab(key, panel, k, i)

            for k in range(len(K1024)):
                load_x(k)
                fetch_slab("C", 0, k, 0)
                fetch_slab("C", 1, k, 0)
            for key, n, _ in STREAM:
                first = 0
                if (key, 0) in SECOND:
                    continue
                if (key, 0) in TWINS:
                    twin = TWINS[key, 0]
                    for k in range(len(SPLIT[key]) if key != "C" else 0):
                        fetch_slab(key, 0, k, 0)
                        fetch_slab(*twin, k, 0)
                    first = 2 if twin[0] == key else 1
                if n < 8:
                    for panel in range(first, n):
                        fetch(key, panel)
                else:
                    with sp.Fori(first // 2, n // 2) as i:
                        fetch(key, 0, i)
                        fetch(key, 1, i)
            for c in range(DC):
                sp.wait_ge(res_ready, 4 * DC + c + 1)
                sp.dma_start(out[c * P:(c + 1) * P, :], XT[:, c, :]).then_inc(stored, 16)
            sp.wait_ge(stored, 16 * DC)

        @block.gpsimd
        def _(pool):
            def split(s, i):
                slot, raw_slot = s % SPL, s % RAW
                wait(pool, w_loaded[raw_slot], 16 * (s // RAW + i + 1))
                wait(pool, slab_done, s + RAW * i - SPL + 1)
                pool.sem_inc(slab_go, 1)
                nc.gpsimd.tensor_tensor(whi[slot][:], raw[raw_slot][:], zero[:, 0:1].unsqueeze(2).broadcast_to([P, SLAB, PANEL]),
                                        ALU.add).then_inc(w_high, 1)
                wait(pool, w_high, s + RAW * i + 1)
                nc.gpsimd.tensor_tensor(wlo[slot][:], raw[raw_slot][:], whi[slot][:].bitcast(F32), ALU.subtract).then_inc(slab_split, 1)

            nc.gpsimd.memset(zero[:], 0.0).then_inc(zero_ready, 1)
            pool.wait_ge(zero_ready, 1)
            for s in range(RAW):
                split(s, 0)
            with pool.Fori(0, SLABS // RAW - 1) as i:
                for s in range(RAW):
                    split(RAW + s, i)
            for s in range(SLABS // RAW * RAW, SLABS):
                split(s, 0)

        @block.tensor
        def _(pe):
            def operand(key):
                name = key if isinstance(key, str) else key[0]
                return {"so": (yT_hi, yT_lo), "ao": (o1_hi, o1_lo), "mix": (mix_hi, mix_lo), "down1": (hid_hi, hid_lo),
                        "fout": (hid_hi, hid_lo), "q3": (opB_hi, opB_lo)}.get(name, (opA_hi, opA_lo))

            FIRST_USE = {"C": (op_ready, 0), "ffn1": (op_ready, 8), ("q2", 0): (op_ready, 16), "awo": (op_ready, 24),
                         ("fin", 0): (op_ready, 32), ("k3", 0): (op_ready, 40), ("q3", 0): (op_ready, 48), "bwo": (op_ready, 56),
                         ("fin", 1): (op_ready, 64), "mix": (mix_ready, 0), "down1": (hid_ready, 0),
                         ("fout", 0): (hid_ready, FT), ("fout", 1): (hid_ready, 2 * FT)}

            def chunk(key, panel, s, c, k, total):
                hi, lo = operand(key)
                wh, wl = whi[s % SPL], wlo[s % SPL]
                name = key if isinstance(key, str) else key[0]
                if name in TOKEN_MAJOR:
                    for t in range(NB):
                        xh, xl = hi[:, k, t * P:(t + 1) * P], lo[:, k, t * P:(t + 1) * P]
                        for n, (a, b) in enumerate(((xh, wh), (xl, wh), (xh, wl))):
                            last = nc.tensor.matmul(psum_tm(key, panel)[:, t, :], a, b[:, c, :], start=t % 2 == 0 and k + n == 0,
                                                    stop=k == total - 1 and n == 2, skip_group_check=True)
                    return last
                for m in range(1 if name in ("dt", "f") else 2):
                    ah, al = wh[:, c, m * P:(m + 1) * P], wl[:, c, m * P:(m + 1) * P]
                    for n, (a, b) in enumerate(((ah, hi), (ah, lo), (al, hi))):
                        last = nc.tensor.matmul(psum_fm(key, panel, m), a, b[:, k, :], start=k + n == 0, stop=k == total - 1 and n == 2)
                return last

            def twin_mm(key, norm):
                a, b = (key, 0), TWINS[key, 0]
                wait(pe, evicted, 2 * (PAN[a[0]] + 1) - 2)
                wait(pe, evicted, 2 * PAN[key])
                total = sum(SPLIT[key])
                ready, base = FIRST_USE[key]
                order = [(t, c) for c in range(total - 2) for t in (a, b)] + [(a, total - 2), (a, total - 1), (b, total - 2), (b, total - 1)]
                for t, c in order:
                    s = slab_no(*t, c // SLAB)
                    if c % SLAB == 0:
                        pe.wait_ge(slab_split, s + 1)
                    if t == a:
                        pe.wait_ge(ready, base + c + 1)
                    last = chunk(*t, s, c % SLAB, c, total)
                    if c % SLAB == SLAB - 1:
                        last.then_inc(slab_done, 1)
                    if (t, c) == (a, total - 1):
                        sum_squares(norm)

            def slab(key, panel, k, i=0):
                name = key if isinstance(key, str) else key[0]
                hi, lo = operand(key)
                p = PAN[key] + panel
                nk = len(SPLIT[key])
                s = place(key, panel, k, i)
                if k == 0:
                    wait(pe, evicted, 2 * (p + 2 * i) - 2)
                    if name == "so" and panel == 0:
                        pe.wait_ge(aux0_read, USE0[("Cp", 4 * key[1] + 3)] + 1)
                    if name == "ao" and panel == 0:
                        pe.wait_ge(o1_ready, 16)
                wait(pe, slab_split, s + 2 * nk * i + 1)
                wh, wl = whi[s % SPL], wlo[s % SPL]
                c0 = sum(SPLIT[key][:k])
                total = sum(SPLIT[key])
                for c in range(SPLIT[key][k]):
                    if panel == 0 and key in FIRST_USE:
                        ready, base = FIRST_USE[key]
                        pe.wait_ge(ready, base + c0 + c + 1)
                    last = chunk(key, panel, s, c, c0 + c, total)
                last.then_inc(slab_done, 1)

            def panel_mm(key, panel, i=0):
                for k in range(len(SPLIT[key])):
                    slab(key, panel, k, i)

            def sum_squares(k):
                if k == 0:
                    pe.wait_ge(first_in, 16 * N_FIRST)
                pe.wait_ge(acc_ready, DC * (k + 1))
                for t in range(NB):
                    last = nc.tensor.matmul(AUX[:, 3, t:t + 1], acc[:, t * P:(t + 1) * P], ones[:, 0:1], start=True, stop=True)
                last.then_inc(ss_done, 1)

            def keep_warm(n, bank=0):
                for _ in range(n):
                    nc.tensor.matmul(AUX[:, bank, :], ident_bf[:], mask1[:, 0:S], start=True, stop=True)

            def spread(k):
                pe.wait_ge(rstd_ready, k + 1)
                for t in range(NB):
                    last = nc.tensor.matmul(AUX[:, 3, t * P:(t + 1) * P], rstd_col[:, t:t + 1].broadcast_to([P, P]), ident[:], start=True, stop=True)
                last.then_inc(bc_done, 1)

            def branch_norm(k):
                keep_warm(WARM_SQUARES)
                sum_squares(k)
                keep_warm(WARM_FACTORS)
                spread(k)
                keep_warm(WARM_RESIDUAL)

            def after_norm(key, k, panels):
                twin_mm(key, k)
                spread(k)
                if k:
                    keep_warm(WARM_BANKS)
                if panels > 2:
                    with pe.Fori(1, panels // 2) as i:
                        panel_mm(key, 0, i)
                        panel_mm(key, 1, i)

            def bias_line(h):
                if h == 0:
                    pe.wait_ge(relw_ready, 3)
                    pe.wait_ge(bc_ready, 1)
                if h >= 2:
                    pe.wait_ge(line_ready, 2 * (h - 1))
                b = 2 * (h % 2)
                nc.tensor.matmul(AUX[:, b, :], relw[:, h, :], oneh[:, 0:S], start=True, stop=True)
                nc.tensor.matmul(AUX[:, b + 1, 0:P], relw[:, h, :], oneh[:, S:LINE], start=True, stop=True).then_inc(line_mm, 1)

            pe.wait_ge(warm_ready, 1)
            for _ in range(WARM_START):
                nc.tensor.matmul(AUX[:, 0, :], rstd_bc[:, 0:P], rstd_bc[:], start=True, stop=True)
            after_norm("C", 0, 2)
            for n in range(2):
                for k in range(len(K1024)):
                    slab("B", n, k)
                    bias_line(4 * n + k)
            def narrow_transposes(key, rows, width):
                pe.wait_ge(evicted, 2 * (PAN[key] + 1))
                for t in range(NB):
                    last = nc.tensor.transpose(AUX[:, 3, t * width:(t + 1) * width], rows[:, t * P:(t + 1) * P], ident[0:width, 0:width])
                last.then_inc(narrow_done, 1)

            panel_mm("dt", 0)
            slab(("xs", 0), 0, 0)
            pe.wait_ge(line_ready, 2 * H2)
            narrow_transposes("dt", dt_rows, NH)
            for k in range(1, len(K1024)):
                slab(("xs", 0), 0, k)
            pe.wait_ge(sp_step, 15)
            for t in range(NB):
                nc.tensor.matmul(AUX[:, 3, t * NH:(t + 1) * NH], tri[:], dz[:, t, :], start=True, stop=True)
                nc.tensor.matmul(AUX[:, 3, (NB + t) * NH:(NB + t + 1) * NH], ones[:], dz[:, t, :], start=True, stop=True)
                last = nc.tensor.matmul(AUX[0:NH, 2, t * P:(t + 1) * P], dz[:, t, :], tri[:], start=True, stop=True)
            last.then_inc(cum_done, 1)
            panel_mm(("xs", 0), 1)

            def bank1_free(tok):
                last = LAST1[tok]
                if last is not None and last[0] == "Bp":
                    pe.wait_ge(state_step, STSTEPS[last[1] + 1])
                elif last is not None:
                    pe.wait_ge(aux1_read, READ1[last] + 1)

            def scan_step(tok):
                kind, u = tok[0], tok[1]
                g, c = (u // NB, u % NB) if kind in ("A", "Bp", "Cp") else (u, 0)
                if kind == "xt":
                    pe.wait_ge(xbc_ready, 2 * NG + u + 1)
                    wait(pe, aux0_read, USE0[tok])
                    for t in range(NB):
                        last = nc.tensor.transpose(AUX[:, 0, t * P:(t + 1) * P], xsf[:, u % 2, t * P:(t + 1) * P], ident[:])
                    last.then_inc(aux0_done, 1)
                elif kind == "G":
                    pe.wait_ge(xbc_ready, 2 * NG)
                    bank1_free(tok)
                    for t in range(NB):
                        last = nc.tensor.transpose(AUX[:, 1, t * P:(t + 1) * P], bcf[:, NG + g, t * P:(t + 1) * P], ident[:])
                    last.then_inc(aux1_done, 1)
                elif kind == "A":
                    bank1_free(tok)
                    nc.tensor.matmul(AUX[:, 1, 0:P], bcf[:, NG + g, c * P:(c + 1) * P], bcf[:, g, c * P:(c + 1) * P],
                                     start=True, stop=True).then_inc(aux1_done, 1)
                elif kind == "Bp":
                    pe.wait_ge(m_step, 2 * u + 2)
                    pe.wait_ge(xdt_ready, u + 1)
                    if u:
                        pe.wait_ge(y_step, YSTEPS[u])
                    if u == 0:
                        pe.wait_ge(tokc_ready, 2)
                    for h in range(HG):
                        last = nc.tensor.matmul(AUX[:, 2, h * HD:(h + 1) * HD], M[:, u % 2, h, :], xdt[:, u % 2, h * HD:(h + 1) * HD],
                                                start=True, stop=True)
                    last.then_inc(ydiag_done, 1)
                    if c:
                        pe.wait_ge(state_step, STSTEPS[u])
                        nc.tensor.matmul(AUX[:, 3, :], bcf[:, g, c * P:(c + 1) * P], state[:], start=True, stop=True).then_inc(yoff_done, 1)
                    if c < NB - 1:
                        pe.wait_ge(xdd_ready, u - g + 1)
                        bank1_free(tok)
                        nc.tensor.matmul(AUX[:, 1, :], btok[:, c, :], xdd[:, u % 2, :], start=True, stop=True).then_inc(aux1_done, 1)
                elif kind == "Cp":
                    pe.wait_ge(yn_ready, u + 1)
                    wait(pe, aux0_read, USE0[tok])
                    for n in range(4):
                        last = nc.tensor.transpose(AUX[:, 0, n * P:(n + 1) * P], yn[:, u % 3, n * P:(n + 1) * P], ident[:])
                    last.then_inc(aux0_done, 1)

            scan_step(("xt", 0))
            scan_step(("xt", 1))
            for tok in SCAN:
                if tok[0] == "mm":
                    for k in range(*tok[3:]) if len(tok) > 3 else range(len(SPLIT[tok[1]])):
                        slab(tok[1], tok[2], k)
                elif tok[0] != "epi":
                    scan_step(tok)

            for key in QKV1(0)[2:]:
                panel_mm(key, 0)
            for tok in ATT1:
                kind, u = tok[0], tok[1]
                if kind == "slab":
                    slab(tok[1], tok[2], tok[3])
                    continue
                if kind == "epi":
                    continue
                h, qb = u // NB, u % NB
                j, hh = h // 2, h % 2
                W1, W0 = w1(qb)
                q0 = qb * P
                if kind == "S":
                    wait(pe, o1_read, u)
                    if qb == 0 and hh == 0:
                        pe.wait_ge(rope_done, 12 * (j + 1))
                    for bank, gi, k0, width, m0 in ((0, 1, 0, W1, S - W1), (1, 2, 0, W1, 2 * S - W1), (2, 0, q0 + P - W0, W0, 2 * S + 2 * P - W0)):
                        nc.tensor.matmul(AUX[:, bank, 0:width], q1[j][:, 2 * gi + hh, q0:q0 + P], k1[j][:, 2 * gi + hh, k0:k0 + width],
                                         start=True, stop=False)
                        last = nc.tensor.matmul(AUX[:, bank, 0:width], ident_bf[:], mask1[:, m0:m0 + width], start=False, stop=True)
                    last.then_inc(s1_done, 1)
                elif kind == "T":
                    pe.wait_ge(exp1, 2 * u + 2)
                    wait(pe, o1_ready, u)
                    nb = nblk(qb)
                    for n in range(nb):
                        last = nc.tensor.transpose(AUX[:, (3, 0, 1)[n // 4], (n % 4) * P:(n % 4 + 1) * P], prob[:, n * P:(n + 1) * P], ident[:])
                        if n % 4 == 3 or n == nb - 1:
                            last.then_inc(tr1_done, 1)
                elif kind == "V":
                    pe.wait_ge(pT1_act, TA[u + 1])
                    wait(pe, pT1_dve, TV[u + 1])
                    if qb == 0 and hh == 0:
                        pe.wait_ge(evicted, 2 * (PAN[("v1", j, AG - 1)] + 1))
                    blocks = [(1, b) for b in range(qb + 1)] + [(2, b) for b in range(qb + 1)] + [(0, b) for b in range(max(qb - 1, 0), qb + 1)]
                    for n, (gi, b) in enumerate(blocks):
                        last = nc.tensor.matmul(AUX[:, 2, 0:P], probT[:, n, :], v1[j][:, b, gi * PANEL + hh * P:gi * PANEL + (hh + 1) * P],
                                                start=n == 0, stop=n == len(blocks) - 1)
                    last.then_inc(pv1_done, 1)
                elif kind == "X":
                    pe.wait_ge(o1_read, u + 1)
                    nc.tensor.transpose(AUX[:, 3, 0:P], osb[:, u % 2, :], ident[:]).then_inc(ot1_done, 1)

            for key in ("ao", "mix"):
                for n in range(4):
                    panel_mm(key, n)
            after_norm("ffn1", 1, 2 * FP)
            for n in range(4):
                panel_mm("down1", n)
            branch_norm(2)

            def attention(names, fox):
                u_base = 32 * fox

                def scores(u):
                    tile, qb = u // NB, u % NB
                    j, hh = tile // 2, tile % 2
                    width, q0 = (qb + 1) * P, qb * P
                    if qb == 0 and hh == 0:
                        pe.wait_ge(evicted, 2 * (max(PAN[(names[0], j)], PAN[(names[1], j)]) + 1))
                    wait(pe, sc_ready, u_base + u)
                    for e in range(2):
                        rows = slice(64 * e, 64 * e + 64)
                        last = nc.tensor.matmul(AUX[:, e, 0:width], q2[j % 2][rows, hh, q0:q0 + P], k2[j % 2][rows, hh, 0:width],
                                                start=True, stop=True)
                        if fox:
                            last = nc.tensor.matmul(AUX[:, e, q0:width], ident_bf[:], mask1[:, 2 * S + P:2 * S + 2 * P],
                                                    start=False, stop=True, skip_group_check=True)
                    last.then_inc(s2_done, 1)

                tiles = 8 * fox
                for tok in order2(names):
                    kind, u = tok[0], tok[1]
                    if kind == "slab":
                        slab(tok[1], tok[2], tok[3])
                    elif kind == "S":
                        scores(u)
                    elif kind == "X":
                        if fox:
                            pe.wait_ge(o2_read, 32 + 8 * (u + 1))
                        else:
                            pe.wait_ge(o2_normed, u + 1)
                        for n in range(NB):
                            last = nc.tensor.transpose(AUX[:, 2 + fox, n * P:(n + 1) * P], osb2[:, u % 2, n, :], ident[:])
                        last.then_inc(ot2_done, 1)
                        tiles += 1
                    elif kind in "TV":
                        tile, qb = u // NB, u % NB
                        j, hh = tile // 2, tile % 2
                        U = u_base + u
                        if kind == "T":
                            wait(pe, oT_ready, tiles)
                            if u % (8 * (PAIRS - 1)) < 2:
                                keep_warm(WARM_UNIT, 2 + fox)
                            if fox:
                                wait(pe, exp2, 2 * U + 2)
                                wait(pe, o2_read, 2 * u + 32)
                            else:
                                pe.wait_ge(r2_step, 4 * u + 4)
                            for e in range(1 + fox):
                                for b in range(qb + 1):
                                    src = sc[:, u % 2, e, b * P:(b + 1) * P] if fox else dif[:, u % 2, b * P:(b + 1) * P]
                                    last = nc.tensor.transpose(AUX[:, 2 + e, b * P:(b + 1) * P], src, ident[:])
                                last.then_inc(tr2_done, 1)
                        elif kind == "V":
                            pe.wait_ge(pT2_act, U + 1)
                            if qb == 0 and hh == 0:
                                pe.wait_ge(evicted, 2 * (PAN[(names[2], j)] + 1))
                            if fox:
                                pe.wait_ge(pT2_dve, u + 1)
                                for e in range(2):
                                    for b in range(qb + 1):
                                        last = nc.tensor.matmul(AUX[:, 2, e * 64:e * 64 + 64], pT[:, e, b, :],
                                                                v2[j % 2][:, b, hh * P + e * 64:hh * P + e * 64 + 64], start=b == 0, stop=b == qb)
                            else:
                                wait(pe, o2_read, u)
                                for b in range(qb + 1):
                                    last = nc.tensor.matmul(AUX[:, 3, 0:P], pT[:, u % 2, b, :], v2[j % 2][:, b, hh * P:(hh + 1) * P],
                                                            start=b == 0, stop=b == qb)
                            last.then_inc(pv2_done, 1)

            twin_mm(("q2", 0), 3)
            spread(3)
            keep_warm(WARM_BANKS)
            panel_mm(("v2", 0), 0)
            attention(("q2", "k2", "v2"), 0)
            for n in range(2):
                slab("awo", n, 3)
            for n in range(2, 4):
                panel_mm("awo", n)
            branch_norm(4)
            after_norm(("fin", 0), 5, 2 * FP)
            for n in range(4):
                panel_mm(("fout", 0), n)
            branch_norm(6)
            twin_mm(("k3", 0), 7)
            spread(7)
            keep_warm(WARM_BANKS)
            slab(("v3", 0), 0, 0)
            narrow_transposes("f", f_rows, BH)
            for k in range(1, len(K1024)):
                slab(("v3", 0), 0, k)
            slab(("q3", 0), 0, 0)
            pe.wait_ge(sp_step, 31)
            for t in range(NB):
                for b in range(t + 1):
                    part = tri if b == t else ones
                    nc.tensor.matmul(AUX[:, 3, t * BH:(t + 1) * BH], part[:], fz[:, b, :], start=b == 0, stop=b == t)
                for b in range(t + 1):
                    part = tri if b == t else ones
                    last = nc.tensor.matmul(AUX[0:BH, 2, t * P:(t + 1) * P], fz[:, b, :], part[:], start=b == 0, stop=b == t)
            last.then_inc(c_done, 1)
            for k in range(1, len(K1024)):
                slab(("q3", 0), 0, k)
            pe.wait_ge(ccol_ready, 2)
            attention(("q3", "k3", "v3"), 1)
            for n in range(2):
                slab("bwo", n, 3)
            for n in range(2, 4):
                panel_mm("bwo", n)
            branch_norm(8)
            after_norm(("fin", 1), 9, 2 * FP)
            for n in range(4):
                panel_mm(("fout", 1), n)
            branch_norm(10)

        @block.scalar
        def _(act):
            A = nc.scalar.activation

            def col(name, n):
                return vec[:, COL[name] + n:COL[name] + n + 1] if isinstance(n, int) else vec[:, bass.ds(COL[name] + n, 1)]

            def load(dst, src, s):
                act.dma_start(dst, src).then_inc(s, 16)

            for dst, name in ((vec, "vec"), (ident, "c_ident"), (ones, "c_ones")):
                load(dst[:], I[name], first_in)

            def load_constants():
                for dst, name in ((relb, "rel_bias_2"), (oneh, "c_onehot"), (future, "c_future"), (mask_in, "c_mask"), (tri, "c_tri")):
                    load(dst[:], I[name], const_in)
                load(dtv[:, 0:2, :].rearrange("p a n -> p (a n)"), bass.AP(tensor=I["dtv"].tensor, offset=0, ap=[[0, P], [1, 2 * NH]]), const_in)
                load(bfv[:], bass.AP(tensor=I["bfv"].tensor, offset=0, ap=[[0, P], [1, BH]]), const_in)
                load(dsk[:], bass.AP(tensor=I["d_skip"].tensor, offset=0, ap=[[0, P], [1, NH]]), const_in)
                load(lamv[:].rearrange("p a n -> p (a n)"), bass.AP(tensor=I["lam"].tensor, offset=0, ap=[[0, P], [1, 4 * 64]]), const_in)

            def squares(src, k, c):
                wait(act, acc_ready, DC * k + c - 1)
                A(sq[:, c % 2, :], src, ACT.Square).then_inc(sq_ready, 1)

            def high(dst, src, gain):
                A(dst, src, ACT.Copy, scale=gain).then_inc(op_hi, 1)

            def norm(k):
                act.wait_ge(ss_done, k + 1)
                A(std[:], AUX[:, 3, 0:NB], ACT.Sqrt, bias=EPS, scale=1.0 / D).then_inc(std_ready, 1)

            act.wait_ge(first_in, 16 * N_FIRST)
            for c in range(DC):
                act.wait_ge(x_in[c // 2], 16)
                high(opA_hi[:, c, :], XT[:, c, :], col("norm_mix", c))
                squares(XT[:, c, :], 0, c)
            load_constants()
            norm(0)
            act.wait_ge(const_in, 16 * N_CONST)

            def conv(q):
                tile = q + 20 if q < 4 else q + 12 if q < 8 else q - 8
                return tile

            def conv_panel(key, panel, q0):
                for m in range(2):
                    q = q0 + m
                    act.wait_ge(evicted, 2 * (PAN[key] + panel) + m + 1)
                    if q >= 2:
                        act.wait_ge(xbc_ready, q - 1)
                    tile = conv(q)
                    A(cacc[:, q % 2, :], cu[:, q % 2, KCONV - 1:KCONV - 1 + S], ACT.Identity, bias=col("conv_b", tile),
                      scale=col("conv_w", 24 * (KCONV - 1) + tile)).then_inc(conv_t0, 1)
                for m in range(2):
                    q = q0 + m
                    act.wait_ge(conv_tap, 6 * (q0 // 2) + 5 + m)
                    if q >= 10:
                        act.wait_ge(aux0_done, USE0[("xt", q - 10)] + 1)
                    dst = bcf[:, q, :] if q < 8 else xsf[:, q % 2, :]
                    A(dst, cacc[:, q % 2, :], ACT.Silu).then_inc(xbc_ready, 1)

            conv_panel("C", 0, 0)
            conv_panel("C", 1, 2)
            act.wait_ge(line_ready, 2 * H2)
            act.dma_start(bias_dram.rearrange("h p n -> p h n"), line[:]).then_inc(bias_out, 16)
            conv_panel("B", 0, 4)
            conv_panel("B", 1, 6)

            def softplus(p, x, a0, s0, sign):
                act.wait_ge(sp_step, s0 + 1)
                A(p[0][:], x[:], ACT.Abs).then_inc(sp_act, 1)
                act.wait_ge(sp_act, a0 + 1)
                A(p[1][:], p[0][:], ACT.Exp, scale=-1.0).then_inc(sp_act, 1)
                act.wait_ge(sp_act, a0 + 2)
                A(p[0][:], x[:], ACT.Relu, scale=sign).then_inc(sp_act, 1)

            A(dtv[:, 2, :], dtv[:, 1, :], ACT.Exp).then_inc(a_exp, 1)
            softplus((da, de), dx, 0, 0, 1.0)
            act.wait_ge(cum_done, 1)
            A(dacs[:], AUX[0:NH, 2, :], ACT.Copy).then_inc(acs_ready, 1)
            act.wait_ge(acs_ready, 1)
            load(acs_dram, dacs[:], acs_out)
            act.wait_ge(sp_step, 16)
            A(ddec[:], ddec[:], ACT.Exp).then_inc(dec_ready, 1)
            cum = AUX[:, 3, 0:NB * NH].rearrange("p (t h) -> p t h", h=NH)
            A(tokc[:, :, 1, :], cum, ACT.Copy).then_inc(tokc_ready, 1)
            A(tokc[:, :, 3, :], cum, ACT.Exp).then_inc(tokc_ready, 1)
            conv_panel(("xs", 0), 0, 8)
            act.wait_ge(acs_out, 16)

            def load_decay(u):
                g, c = u // NB, u % NB
                load(acs_row[:, u % 2], bass.AP(tensor=acs_dram.tensor, offset=g * HG * S + c * P, ap=[[0, P], [S, HG], [1, P]]), acs_in[u % 2])

            def load_gain(g):
                load(gain[:, g % 2, :], bass.AP(tensor=I["ssm_norm"].tensor, offset=g * GW, ap=[[0, P], [1, GW]]), gain_in[g % 2])

            act.wait_ge(op_ready, DC)
            act.wait_ge(sq_ready, DC)
            load_decay(0)
            load_gain(0)

            def silu_gate(g, panel):
                act.wait_ge(evicted, 2 * (PAN[("z", g)] + panel) + 2)
                part = zbuf[:, :, panel * PANEL:(panel + 1) * PANEL]
                A(part, part, ACT.Silu).then_inc(z_ready, 1)

            def scan_step(tok):
                kind, u = tok[0], tok[1]
                if kind == "xt":
                    act.wait_ge(aux0_done, USE0[tok] + 1)
                    if u >= 8 and u % 4 == 0:
                        act.wait_ge(y_step, YSTEPS[4 * (u // 4 - 1)])
                        act.wait_ge(xdt_ready, 4 * (u // 4 - 1))
                        act.wait_ge(xdd_ready, 3 * (u // 4 - 1))
                    A(xs_tok[:, (u // 4) % 2, :, (u % 4) * P:(u % 4 + 1) * P], AUX[:, 0, :].rearrange("p (t n) -> p t n", n=P),
                      ACT.Copy).then_inc(aux0_read, 1)
                elif kind == "A":
                    act.wait_ge(acs_in[u % 2], 16 * (u // 2 + 1))
                    act.wait_ge(decay_step, 2 * u + 2)
                    A(M[:, u % 2], M[:, u % 2], ACT.Exp).then_inc(decay_exp, 1)
                    A(etot[:, u % 2, :], acs_row[:, u % 2, :, P - 1], ACT.Exp).then_inc(decay_exp, 1)
                    if u < 15:
                        if u:
                            act.wait_ge(decay_step, 2 * u)
                            act.wait_ge(decay_exp, 2 * u)
                        load_decay(u + 1)
                    if u % 4 == 1 and u < 12:
                        if u > 4:
                            act.wait_ge(yn_ready, u - 1)
                        load_gain(u // 4 + 1)
                elif kind == "Bp":
                    act.wait_ge(y_step, YSTEPS[u + 1])
                    if u:
                        act.wait_ge(yn_ready, u)
                    A(yt[:], yb[:], ACT.Square, accum_out=ystat[:, u % 2, 0:1]).then_inc(y_stat, 1)
                    act.wait_ge(y_stat, 2 * u + 1)
                    A(ystat[:, u % 2, 1:2], ystat[:, u % 2, 0:1], ACT.Sqrt, bias=EPS, scale=1.0 / GW).then_inc(y_stat, 1)
                elif kind == "Cp":
                    g, c = u // NB, u % NB
                    act.wait_ge(aux0_done, USE0[tok] + 1)
                    if g:
                        act.wait_ge(slab_done, slab_end(("so", g - 1), 3))
                    A(yT_hi[:, :, c * P:(c + 1) * P], AUX[:, 0, :].rearrange("p (j t) -> p j t", t=P), ACT.Copy).then_inc(y_hi, 1)

            scan_step(("xt", 0))
            scan_step(("xt", 1))
            conv_panel(("xs", 0), 1, 10)
            for tok in SCAN:
                if tok[0] == "epi":
                    key, panel = tok[1], tok[2]
                    if key[0] == "z":
                        silu_gate(key[1], panel)
                    elif key[0] == "xs":
                        conv_panel(key, panel, 8 + 4 * key[1] + 2 * panel)
                elif tok[0] != "mm":
                    scan_step(tok)
                if tok == ("Cp", 15):
                    act.wait_ge(aux0_done, len(USE0))
                    act.wait_ge(yn_ready, 16)
                    act.wait_ge(xbc_ready, 24)
                    load(cosr[:], I["c_cos"], rope_in)
                    load(sinr[:], I["c_sin"], rope_in)

            for tok in ATT1:
                kind, u = tok[0], tok[1]
                if kind == "epi" and tok[1] == "gates":
                    panel = tok[2]
                    for m in range(2):
                        gi, c = panel % 2, 2 * (panel // 2) + m
                        act.wait_ge(evicted, 2 * (PAN["gates"] + panel) + m + 1)
                        A(gate1[:, c, :] if gi else gtmp[:, m, :], gtmp[:, m, :], ACT.Sigmoid, bias=col("b_gate", 8 * gi + c)).then_inc(gate_sig, 1)
                if kind in ("slab", "epi"):
                    continue
                h, qb = u // NB, u % NB
                W1, W0 = w1(qb)
                if kind == "S":
                    act.wait_ge(negmax1, u + 1)
                    wait(act, tr1_done, TB[u])
                    wait(act, den1, u - 1)
                    A(prob[:, 0:2 * W1].rearrange("p (g k) -> p g k", g=2), AUX[:, 0:2, 0:W1], ACT.Exp, bias=astat[:, u % 2, 2:3],
                      scale=ADIM ** -0.5, accum_out=astat[:, u % 2, 3:4]).then_inc(exp1, 1)
                    A(prob[:, 2 * W1:2 * W1 + W0], AUX[:, 2, 0:W0], ACT.Exp, bias=astat[:, u % 2, 2:3],
                      scale=ADIM ** -0.5, accum_out=astat[:, u % 2, 4:5]).then_inc(exp1, 1)
                elif kind == "T":
                    nb = nblk(qb)
                    wait(act, pv1_done, u)
                    for n in range(0, nb, 8):
                        bank = n // 4
                        act.wait_ge(tr1_done, TB[u] + bank + 1)
                        k = min(4, nb - n)
                        A(probT[:, n:n + k, :], AUX[:, (3, 0, 1)[bank], 0:k * P].rearrange("p (b q) -> p b q", q=P), ACT.Copy).then_inc(pT1_act, 1)
                elif kind == "X":
                    act.wait_ge(ot1_done, u + 1)
                    A(o1_hi[:, h, qb * P:(qb + 1) * P], AUX[:, 3, 0:P], ACT.Copy).then_inc(o1_high, 1)
            act.wait_ge(o1_ready, 16)
            for n in range(4):
                load(XT[:, 2 * n:2 * n + 2, :], xT.rearrange("(c p) t -> p c t", p=P)[:, 2 * n:2 * n + 2, :], x_in[n])
            for c in range(DC):
                act.wait_ge(mix_sum, c + 1)
                A(mix_hi[:, c, :], mixed[:, c, :], ACT.Copy).then_inc(mix_high, 1)
            for c in range(DC):
                act.wait_ge(evicted, 2 * PAN["mix"] + c + 1)
                high(opA_hi[:, c, :], XT[:, c, :], col("norm_ffn", c))
                squares(XT[:, c, :], 1, c)
            norm(1)

            def ffn1_body(i):
                for m in range(2):
                    act.wait_ge(evicted, 2 * PAN["ffn1"] + 4 * i + m + 1)
                    A(fg[:, m, :], facc[:, m, :], ACT.Silu).then_inc(fgate, 1)
                for m in range(2):
                    act.wait_ge(fprod, 2 * i + m + 1)
                    A(hid_hi[:, bass.ds(2 * i + m, 1), :], facc[:, 2 + m:3 + m, :], ACT.Copy).then_inc(hid_high, 1)

            with act.Fori(0, FP) as i:
                ffn1_body(i)
            for c in range(DC):
                act.wait_ge(evicted, 2 * PAN["down1"] + c + 1)
                squares(XT[:, c, :], 2, c)
            norm(2)

            def prepare(k, dst, name, first, src_ready):
                for c in range(DC):
                    act.wait_ge(res_ready, src_ready + c + 1)
                    high(dst[:, c, :], XT[:, c, :], col(name, first + c))
                    squares(XT[:, c, :], k, c)

            def branch_squares(key, k):
                for c in range(DC):
                    act.wait_ge(evicted, 2 * PAN[key] + c + 1)
                    squares(branch[:, c, :], k, c)
                norm(k)

            def fin(l, k):
                def body(i, first):
                    n0 = 44 * l
                    for half in range(2):
                        for m in range(2):
                            j = 2 * half + m
                            act.wait_ge(evicted, 2 * PAN[("fin", l)] + 4 * i + j + 1)
                            A(facc[:, j, :], fu[:, j, 2:2 + S], ACT.Identity, bias=col("ffn_conv_b_2", 44 * l + FT * half + m + 2 * i),
                              scale=col("ffn_conv_w_2", 132 * l + 88 + FT * half + m + 2 * i)).then_inc(fconv_t0, 1)
                        if half == 0:
                            for m in range(2):
                                act.wait_ge(fconv_tap, 88 * l + 8 * i + 3 + m)
                                A(fg[:, m, :], facc[:, m, :], ACT.Gelu_apprx_tanh).then_inc(fgate, 1)
                    for m in range(2):
                        act.wait_ge(fprod, FT * (l + 1) + 2 * i + m + 1)
                        A(hid_hi[:, bass.ds(2 * i + m, 1), :], facc[:, 2 + m:3 + m, :], ACT.Copy).then_inc(hid_high, 1)

                with act.Fori(0, FP) as i:
                    body(i, False)

            def softmax_units(names, fox):
                for tok in order2(names):
                    kind, u = tok[0], tok[1]
                    if kind in ("slab", "epi"):
                        continue
                    U = 32 * fox + u
                    tile, qb = u // NB, u % NB
                    width = (qb + 1) * P
                    if kind == "M":
                        if fox and qb == 0 and tile < 7:
                            if tile:
                                act.wait_ge(sc_ready, 32 + 4 * tile)
                            load_negc(tile + 1)
                        act.wait_ge(negmax2, U + 1)
                        for e in range(2):
                            A(sc[:, u % 2, e, 0:width], sc[:, u % 2, e, 0:width], ACT.Exp, bias=bstat[:, u % 4, 2 + e:3 + e],
                              accum_out=bstat[:, u % 4, 4 + e:5 + e]).then_inc(exp2, 1)
                    elif kind == "T":
                        act.wait_ge(tr2_done, 32 + 2 * u + 1 if fox else u + 1)
                        if fox:
                            wait(act, pv2_done, U)
                            dst = pT[:, 0, 0:qb + 1, :]
                        else:
                            wait(act, pv2_done, U - 1)
                            dst = pT[:, u % 2, 0:qb + 1, :]
                        A(dst, AUX[:, 2, 0:width].rearrange("p (b q) -> p b q", q=P), ACT.Copy).then_inc(pT2_act, 1)
                    elif kind == "W" and not fox:
                        act.wait_ge(o2_read, u + 1)
                        wait(act, o2_stat, u)
                        A(osq[:], osb2[:, tile % 2, qb, :], ACT.Square, accum_out=ostat[:, tile % 2, qb:qb + 1]).then_inc(o2_stat, 1)
                    elif kind == "Y":
                        act.wait_ge(o2_stat, NB * (u + 1))
                        A(ostat[:, u % 2, NB:2 * NB], ostat[:, u % 2, 0:NB], ACT.Sqrt, bias=SUB_EPS, scale=1.0 / P).then_inc(o2_std, 1)
                    elif kind == "X":
                        act.wait_ge(ot2_done, 8 * fox + u + 1)
                        A(oT[:, u, :], AUX[:, 2 + fox, :], ACT.Copy, scale=1.0 if fox else subg[:, 0:1]).then_inc(oT_ready, 1)
                    elif kind == "O":
                        act.wait_ge(slab_done, slab_end((names[2], PAIRS - 1), 0))
                        act.wait_ge(oT_ready, 8 * fox + u + 1)
                        A(opA_hi[:, u, :], oT[:, u, :], ACT.Copy).then_inc(op_hi, 1)

            def load_negc(tile):
                load(negc[:, tile % 2], bass.AP(tensor=c_dram.tensor, offset=2 * tile * S, ap=[[0, P], [S, 2], [1, S]]), negc_in[tile % 2])

            act.wait_ge(lam_step, 3)
            for n in range(2):
                A(lams[:, 2 + n:3 + n], lams[:, n:n + 1], ACT.Exp).then_inc(lam_act, 1)
            prepare(3, opA_hi, "a_norm_pre_2", 0, 0)
            act.wait_ge(evicted, 2 * PAN["down1"] + DC)
            act.wait_ge(hid_ready, FT)
            act.wait_ge(bias_out, 16)
            load(tbias[:], bass.AP(tensor=bias_dram.tensor, offset=P - 1, ap=[[LINE - 1, P], [P * LINE, H2], [1, S]]), tbias_in)
            norm(3)
            softmax_units(("q2", "k2", "v2"), 0)
            branch_squares("awo", 4)
            prepare(5, opA_hi, "ffn_norm_pre_2", 0, DC)
            norm(5)
            fin(0, 5)
            branch_squares(("fout", 0), 6)
            prepare(7, opA_hi, "kv_norm_2", 0, 2 * DC)
            norm(7)
            softplus((fa, fe), fx, 3, 17, -1.0)
            for c in range(DC):
                high(opB_hi[:, c, :], XT[:, c, :], col("b_norm_pre_2", c))
            act.wait_ge(c_done, 1)
            A(fc[:], AUX[0:BH, 2, :], ACT.Copy).then_inc(ccol_ready, 1)
            act.wait_ge(ccol_ready, 1)
            load(c_dram, fc[:], c_out)
            A(ccol[:].rearrange("p t h -> p (t h)"), AUX[:, 3, 0:NB * BH], ACT.Copy).then_inc(ccol_ready, 1)
            act.wait_ge(c_out, 16)
            load_negc(0)
            softmax_units(("q3", "k3", "v3"), 1)
            branch_squares("bwo", 8)
            prepare(9, opA_hi, "ffn_norm_pre_2", 8, 3 * DC)
            norm(9)
            fin(1, 9)
            branch_squares(("fout", 1), 10)

        @block.vector
        def _(dve):
            V = nc.vector

            def col(name, n):
                return vec[:, COL[name] + n:COL[name] + n + 1] if isinstance(n, int) else vec[:, bass.ds(COL[name] + n, 1)]

            V.memset(rstd_bc[:], 1.0).then_inc(warm_ready, 1)
            dve.wait_ge(first_in, 16 * N_FIRST)
            n_op = [0]

            def low(dst, src, gain, high_part):
                n_op[0] += 1
                dve.wait_ge(op_hi, n_op[0])
                if gain is None:
                    V.tensor_tensor(dst, src, high_part.bitcast(F32), ALU.subtract).then_inc(op_ready, 1)
                else:
                    V.scalar_tensor_tensor(dst, src, gain, high_part.bitcast(F32), ALU.mult, ALU.subtract).then_inc(op_ready, 1)

            def add_squares(k, c):
                dve.wait_ge(sq_ready, DC * k + c + 1)
                if c == 0:
                    wait(dve, ss_done, k)
                    V.tensor_copy(acc[:], sq[:, 0, :]).then_inc(acc_ready, 1)
                else:
                    dve.wait_ge(acc_ready, DC * k + c)
                    V.tensor_tensor(acc[:], acc[:], sq[:, c % 2, :], ALU.add).then_inc(acc_ready, 1)

            def norm(k, first=None):
                dve.wait_ge(std_ready, k + 1)
                V.reciprocal(rstd_col[:], std[:]).then_inc(rstd_ready, 1)
                dve.wait_ge(bc_done, k + 1)
                if first:
                    first(AUX[:, 3, :])
                V.tensor_copy(rstd_bc[:], AUX[:, 3, :]).then_inc(bc_ready, 1)
                dve.wait_ge(bc_ready, k + 1)

            for c in range(DC):
                dve.wait_ge(x_in[c // 2], 16)
                low(opA_lo[:, c, :], XT[:, c, :], col("norm_mix", c), opA_hi[:, c, :])
                add_squares(0, c)
            dve.wait_ge(const_in, 16 * N_CONST)
            V.tensor_copy(relw[:], relb[:].unsqueeze(2).broadcast_to([BUCKETS, H2, P])).then_inc(relw_ready, 1)
            V.tensor_copy(mask1[:], mask_in[:]).then_inc(relw_ready, 1)
            V.tensor_copy(ident_bf[:], ident[:]).then_inc(relw_ready, 1)
            norm(0)
            dve.wait_ge(op_ready, DC)
            V.memset(cu[:, :, 0:KCONV - 1], 0.0).then_inc(pads, 1)
            dve.wait_ge(pads, 1)

            def done(key, panel, i=0):
                dve.wait_ge(slab_done, place(key, panel, len(SPLIT[key]) - 1, i) + 1 + 2 * len(SPLIT[key]) * i)

            def conv_panel(key, panel, q0):
                done(key, panel)
                for m in range(2):
                    wait(dve, conv_t0, q0 + m - 1)
                    wait(dve, conv_tap, 3 * q0 + m - 1 if q0 else 0)
                    V.tensor_tensor(cu[:, m, KCONV - 1:KCONV - 1 + S], psum_fm(key, panel, m), rstd_bc[:], ALU.mult).then_inc(evicted, 1)
                for j in range(KCONV - 1):
                    for m in range(2):
                        q = q0 + m
                        tile = q + 20 if q < 4 else q + 12 if q < 8 else q - 8
                        if j == 0:
                            dve.wait_ge(conv_t0, q + 1)
                        else:
                            dve.wait_ge(conv_tap, 3 * q0 + 2 * j - 1 + m)
                        V.scalar_tensor_tensor(cacc[:, m, :], cu[:, m, j:j + S], col("conv_w", 24 * j + tile), cacc[:, m, :],
                                               ALU.mult, ALU.add).then_inc(conv_tap, 1)

            conv_panel("C", 0, 0)

            def bias_line(h):
                dve.wait_ge(line_mm, h + 1)
                b = 2 * (h % 2)
                V.tensor_tensor(line[:, h, 0:S], AUX[:, b, :], future[:, 0:S], ALU.add).then_inc(line_ready, 1)
                V.tensor_tensor(line[:, h, S:LINE], AUX[:, b + 1, 0:P], future[:, S:LINE], ALU.add).then_inc(line_ready, 1)

            for h in range(2):
                bias_line(h)
            conv_panel("C", 1, 2)
            for h in range(2, H2):
                bias_line(h)
            V.tensor_tensor(lamt[:], lamv[:, 0:4:2, :], lamv[:, 1:4:2, :], ALU.mult).then_inc(lam_step, 1)
            dve.wait_ge(lam_step, 1)
            V.tensor_reduce(lams[:, 0:2], lamt[:], AX.X, ALU.add).then_inc(lam_step, 1)
            V.tensor_scalar(subg[:], col("a_subln_2", 0), 1.0 - LAM0, None, ALU.mult).then_inc(lam_step, 1)
            conv_panel("B", 0, 4)
            conv_panel("B", 1, 6)

            def softplus(p, s0, a0):
                a, e, r_, z, z2, q = p
                n = [s0]

                def step(ins):
                    n[0] += 1
                    ins.then_inc(sp_step, 1)
                    dve.wait_ge(sp_step, n[0])

                dve.wait_ge(sp_act, a0 + 2)
                step(V.tensor_scalar(r_[:], e[:], 2.0, None, ALU.add))
                step(V.reciprocal(r_[:], r_[:]))
                step(V.tensor_tensor(z[:], e[:], r_[:], ALU.mult))
                step(V.tensor_tensor(z2[:], z[:], z[:], ALU.mult))
                step(V.tensor_scalar(q[:], z2[:], 1.0 / 15, None, ALU.mult))
                for k in (13, 11, 9, 7, 5, 3):
                    step(V.scalar_tensor_tensor(q[:], q[:], 1.0 / k, z2[:], ALU.add, ALU.mult))
                step(V.scalar_tensor_tensor(q[:], q[:], 1.0, z[:], ALU.add, ALU.mult))
                dve.wait_ge(sp_act, a0 + 3)
                return step, q, a

            def narrow_out(key, rows, x, bias, n, width):
                done(key, 0)
                V.tensor_tensor(rows[:], psum_fm(key, 0, 0)[0:width, :], rstd_bc[0:width, :], ALU.mult).then_inc(evicted, 2)
                dve.wait_ge(narrow_done, n)
                V.tensor_tensor(x[:], AUX[:, 3, 0:NB * width].rearrange("p (t h) -> p t h", h=width),
                                bias.unsqueeze(1).broadcast_to([P, NB, width]), ALU.add).then_inc(sp_step, 1)

            dve.wait_ge(bias_out, 16)
            narrow_out("dt", dt_rows, dx, dtv[:, 0, :], 1, NH)
            step, q, a = softplus((da, de, dr, dz, dz2, dq), 1, 0)
            step(V.scalar_tensor_tensor(tokc[:, :, 0, :], q[:], 2.0, a[:], ALU.mult, ALU.add))
            dve.wait_ge(a_exp, 1)
            step(V.scalar_tensor_tensor(dz[:], tokc[:, :, 0, :], -1.0, dtv[:, 2, :].unsqueeze(1).broadcast_to([P, NB, NH]), ALU.mult, ALU.mult))
            dve.wait_ge(cum_done, 1)
            both = AUX[:, 3, 0:2 * NB * NH].rearrange("p (k t h) -> p k t h", k=2, h=NH)
            V.tensor_copy(ddec[:], both[:, 1]).then_inc(dec_ready, 1)
            dve.wait_ge(dec_ready, 1)
            step(V.tensor_tensor(ddec[:], ddec[:], both[:, 0], ALU.subtract))
            dve.wait_ge(dec_ready, 2)
            step(V.tensor_tensor(tokc[:, :, 2, :], tokc[:, :, 0, :], ddec[:], ALU.mult))
            conv_panel(("xs", 0), 0, 8)
            conv_panel(("xs", 0), 1, 10)

            def heads(ap):
                return ap.rearrange("p (h d) -> p h d", d=HD)

            def spread(ap):
                return ap.unsqueeze(2).broadcast_to([P, HG, HD])

            n_state, n_y = [0], [0]

            def scan_step(tok):
                kind, u = tok[0], tok[1]
                g, c = (u // NB, u % NB) if kind in ("A", "Bp", "N", "Cp") else (u, 0)
                hs = slice(g * HG, (g + 1) * HG)
                if kind == "G":
                    dve.wait_ge(aux1_done, USE1[tok] + 1)
                    V.tensor_copy(btok[:].rearrange("p t n -> p (t n)"), AUX[:, 1, :]).then_inc(aux1_read, 1)
                elif kind == "A":
                    dve.wait_ge(acs_in[u % 2], 16 * (u // 2 + 1))
                    if u == 0:
                        dve.wait_ge(tokc_ready, 2)
                    wait(dve, ydiag_done, u - 1)
                    V.tensor_tensor(M[:, u % 2], acs_row[:, u % 2], tokc[:, c, 1, hs].unsqueeze(2).broadcast_to([P, HG, P]),
                                    ALU.subtract).then_inc(decay_step, 1)
                    dve.wait_ge(decay_step, 2 * u + 1)
                    V.tensor_scalar(M[:, u % 2], M[:, u % 2], 0.0, None, ALU.min).then_inc(decay_step, 1)
                    xs = heads(xs_tok[:, g % 2, c, :])
                    dve.wait_ge(aux0_read, USE0[("xt", 4 * g + 3)] + 1)
                    V.tensor_tensor(heads(xdt[:, u % 2, :]), xs, spread(tokc[:, c, 0, hs]), ALU.mult).then_inc(xdt_ready, 1)
                    if c < NB - 1:
                        V.tensor_tensor(heads(xdd[:, u % 2, :]), xs, spread(tokc[:, c, 2, hs]), ALU.mult).then_inc(xdd_ready, 1)
                    dve.wait_ge(aux1_done, USE1[tok] + 1)
                    V.tensor_tensor(cbm[:, u % 2, :], AUX[:, 1, 0:P], tri[:], ALU.mult).then_inc(aux1_read, 1)
                    dve.wait_ge(aux1_read, READ1[tok] + 1)
                    dve.wait_ge(decay_exp, 2 * u + 1)
                    V.tensor_tensor(M[:, u % 2], M[:, u % 2], cbm[:, u % 2, :].unsqueeze(1).broadcast_to([P, HG, P]), ALU.mult).then_inc(m_step, 2)
                elif kind == "Bp":
                    if c:
                        dve.wait_ge(yoff_done, u - g)
                    if c < NB - 1:
                        dve.wait_ge(decay_exp, 2 * u + 2)
                        if c:
                            V.tensor_tensor(heads(state[:]), heads(state[:]), spread(etot[:, u % 2, :]), ALU.mult).then_inc(state_step, 1)
                            dve.wait_ge(state_step, STSTEPS[u] + 1)
                            dve.wait_ge(aux1_done, USE1[tok] + 1)
                            V.tensor_tensor(state[:], state[:], AUX[:, 1, :], ALU.add).then_inc(state_step, 1)
                        else:
                            dve.wait_ge(aux1_done, USE1[tok] + 1)
                            V.tensor_copy(state[:], AUX[:, 1, :]).then_inc(state_step, 1)
                        dve.wait_ge(state_step, STSTEPS[u + 1])
                    y0 = YSTEPS[u]
                    k = [y0]

                    def step(ins):
                        k[0] += 1
                        ins.then_inc(y_step, 1)
                        dve.wait_ge(y_step, k[0])

                    wait(dve, y_stat, 2 * u)
                    wait(dve, yn_ready, u)
                    step(V.tensor_tensor(heads(yb[:]), heads(xs_tok[:, g % 2, c, :]), spread(dsk[:, hs]), ALU.mult))
                    if c:
                        step(V.tensor_tensor(heads(yoffb[:]), heads(AUX[:, 3, :]), spread(tokc[:, c, 3, hs]), ALU.mult))
                    dve.wait_ge(ydiag_done, u + 1)
                    step(V.tensor_tensor(yb[:], yb[:], AUX[:, 2, :], ALU.add))
                    if c:
                        step(V.tensor_tensor(yb[:], yb[:], yoffb[:], ALU.add))
                    dve.wait_ge(z_ready, 2 * g + 2)
                    step(V.tensor_tensor(yb[:], yb[:], zbuf[:, c, :], ALU.mult))
                elif kind == "N":
                    dve.wait_ge(y_stat, 2 * u + 2)
                    V.reciprocal(ystat[:, u % 2, 2:3], ystat[:, u % 2, 1:2]).then_inc(y_rstd, 1)
                    dve.wait_ge(y_rstd, u + 1)
                    dve.wait_ge(gain_in[g % 2], 16 * (g // 2 + 1))
                    if u >= 3:
                        dve.wait_ge(aux0_done, USE0[("Cp", u - 3)] + 1)
                    V.scalar_tensor_tensor(yn[:, u % 3, :], yb[:], ystat[:, u % 2, 2:3], gain[:, g % 2, :], ALU.mult, ALU.mult).then_inc(yn_ready, 1)
                elif kind == "Cp":
                    dve.wait_ge(y_hi, u + 1)
                    part = slice(c * P, (c + 1) * P)
                    V.tensor_tensor(yT_lo[:, :, part], AUX[:, 0, :].rearrange("p (j t) -> p j t", t=P), yT_hi[:, :, part].bitcast(F32),
                                    ALU.subtract).then_inc(aux0_read, 1)

            def gate_panel(key, panel):
                done(key, panel)
                g = key[1]
                for t in range(NB):
                    ins = V.tensor_scalar(zbuf[:, t, panel * PANEL:(panel + 1) * PANEL], psum_tm(key, panel)[:, t, :], rstd_col[:, t:t + 1], None, ALU.mult)
                    if t % 2:
                        ins.then_inc(evicted, 1)

            def add_scan_out(key, panel):
                done(key, panel)
                for m in range(2):
                    c = 2 * panel + m
                    if key[1] == 0:
                        V.tensor_copy(y_ssm[:, c, :], psum_fm(key, panel, m)).then_inc(evicted, 1)
                    else:
                        V.tensor_tensor(y_ssm[:, c, :], y_ssm[:, c, :], psum_fm(key, panel, m), ALU.add).then_inc(evicted, 1)

            n_rope = [0]

            def rotate_panel(key):
                name, j, gi = key
                done(key, 0)
                dst = (q1 if name == "q1" else k1)[j]
                T = 2 * PAN[key]
                for m in range(2):
                    ps = psum_fm(key, 0, m)
                    wait(dve, rope_done, n_rope[0] + m - 1)
                    V.tensor_tensor(dst[:, 2 * gi + m, :], ps, cosr[:], ALU.mult)
                    V.tensor_tensor(rsin[0:64, m, :], ps[64:P], sinr[64:P, :], ALU.mult)
                    V.tensor_tensor(rsin[64:P, m, :], ps[0:64], sinr[0:64, :], ALU.mult).then_inc(evicted, 1)
                for m in range(2):
                    dve.wait_ge(evicted, T + m + 1)
                    V.tensor_tensor(dst[:, 2 * gi + m, :], dst[:, 2 * gi + m, :], rsin[:, m, :], ALU.add).then_inc(rope_done, 1)
                n_rope[0] += 2

            def values_panel(key, dst, first):
                done(key, 0)
                for t in range(NB):
                    ins = V.tensor_scalar(dst[:, t, first:first + PANEL], psum_tm(key, 0)[:, t, :], rstd_col[:, t:t + 1], None, ALU.mult)
                    if t % 2:
                        ins.then_inc(evicted, 1)

            def qkv1(key):
                if key[0] == "v1":
                    values_panel(key, v1[key[1]], key[2] * PANEL)
                else:
                    rotate_panel(key)

            def scale_rotations():
                dve.wait_ge(rope_in, 32)
                V.tensor_tensor(cosr[:], cosr[:], rstd_bc[:], ALU.mult).then_inc(rope_scaled, 1)
                V.tensor_tensor(sinr[:], sinr[:], rstd_bc[:], ALU.mult).then_inc(rope_scaled, 1)
                dve.wait_ge(rope_scaled, 2)

            for tok in SCAN:
                if tok[0] == "epi":
                    key, panel = tok[1], tok[2]
                    if key[0] == "z":
                        gate_panel(key, panel)
                    elif key[0] == "xs":
                        conv_panel(key, panel, 8 + 4 * key[1] + 2 * panel)
                    elif key[0] == "so":
                        add_scan_out(key, panel)
                    else:
                        qkv1(key)
                elif tok[0] != "mm":
                    scan_step(tok)
            scale_rotations()
            for key in QKV1(0)[2:]:
                qkv1(key)

            for tok in ATT1:
                kind, u = tok[0], tok[1]
                if kind == "epi" and tok[1] == "gates":
                    panel = tok[2]
                    gi = panel % 2
                    done("gates", panel)
                    for m in range(2):
                        wait(dve, gate_sig, 2 * panel + m - 1)
                        V.tensor_tensor(gtmp[:, m, :], psum_fm("gates", panel, m), rstd_bc[:], ALU.mult).then_inc(evicted, 1)
                    if gi == 0:
                        for m in range(2):
                            c = 2 * (panel // 2) + m
                            dve.wait_ge(gate_sig, 2 * panel + m + 1)
                            V.tensor_tensor(mixed[:, c, :], gtmp[:, m, :], y_ssm[:, c, :], ALU.mult).then_inc(gate_mul, 1)
                elif kind == "epi":
                    qkv1(tok[1])
                if kind in ("slab", "epi"):
                    continue
                h, qb = u // NB, u % NB
                W1, W0 = w1(qb)
                st = astat[:, u % 2]
                if kind == "S":
                    dve.wait_ge(s1_done, u + 1)
                    V.tensor_reduce(st[:, 0:1], AUX[:, 0:2, 0:W1], AX.XY, ALU.max).then_inc(max1, 1)
                    V.tensor_reduce(st[:, 1:2], AUX[:, 2, 0:W0], AX.X, ALU.max).then_inc(max1, 1)
                    dve.wait_ge(max1, 2 * u + 2)
                    V.tensor_scalar(st[:, 2:3], st[:, 0:1], st[:, 1:2], -(ADIM ** -0.5), ALU.max, ALU.mult).then_inc(negmax1, 1)
                elif kind == "T":
                    if nblk(qb) > 4:
                        nb = min(4, nblk(qb) - 4)
                        dve.wait_ge(tr1_done, TB[u] + 2)
                        V.tensor_copy(probT[:, 4:4 + nb, :], AUX[:, 0, 0:nb * P].rearrange("p (b q) -> p b q", q=P)).then_inc(pT1_dve, 1)
                    dve.wait_ge(exp1, 2 * u + 2)
                    V.tensor_tensor(st[:, 5:6], st[:, 3:4], st[:, 4:5], ALU.add).then_inc(den1, 1)
                    dve.wait_ge(den1, u + 1)
                    V.reciprocal(st[:, 6:7], st[:, 5:6]).then_inc(rden1, 1)
                elif kind == "V":
                    dve.wait_ge(pv1_done, u + 1)
                    dve.wait_ge(rden1, u + 1)
                    wait(dve, ot1_done, u - 1)
                    V.tensor_scalar(osb[:, u % 2, :], AUX[:, 2, 0:P], st[:, 6:7], None, ALU.mult).then_inc(o1_read, 1)
                elif kind == "X":
                    dve.wait_ge(o1_high, u + 1)
                    part = slice(qb * P, (qb + 1) * P)
                    V.tensor_tensor(o1_lo[:, h, part], AUX[:, 3, 0:P], o1_hi[:, h, part].bitcast(F32), ALU.subtract).then_inc(o1_ready, 1)

            dve.wait_ge(gate_sig, 16)
            dve.wait_ge(gate_mul, 8)
            for panel in range(4):
                done("ao", panel)
                for m in range(2):
                    c = 2 * panel + m
                    wait(dve, mix_sum, c - 1)
                    V.tensor_tensor(gtmp[:, m, :], psum_fm("ao", panel, m), gate1[:, c, :], ALU.mult).then_inc(evicted, 1)
                for m in range(2):
                    c = 2 * panel + m
                    dve.wait_ge(evicted, 2 * (PAN["ao"] + panel) + m + 1)
                    V.tensor_tensor(mixed[:, c, :], mixed[:, c, :], gtmp[:, m, :], ALU.add).then_inc(mix_sum, 1)
                for m in range(2):
                    c = 2 * panel + m
                    dve.wait_ge(mix_sum, c + 1)
                    dve.wait_ge(mix_high, c + 1)
                    V.tensor_tensor(mix_lo[:, c, :], mixed[:, c, :], mix_hi[:, c, :].bitcast(F32), ALU.subtract).then_inc(mix_ready, 1)
            for panel in range(4):
                done("mix", panel)
                for m in range(2):
                    c = 2 * panel + m
                    dve.wait_ge(x_in[c // 2], 32)
                    V.tensor_tensor(XT[:, c, :], XT[:, c, :], psum_fm("mix", panel, m), ALU.add).then_inc(evicted, 1)
                for m in range(2):
                    c = 2 * panel + m
                    dve.wait_ge(evicted, 2 * PAN["mix"] + c + 1)
                    low(opA_lo[:, c, :], XT[:, c, :], col("norm_ffn", c), opA_hi[:, c, :])
                    add_squares(1, c)
            norm(1)

            def ffn1(i):
                T = 2 * PAN["ffn1"]
                done("ffn1", 0, i)
                wait(dve, hid_ready, 2 * i)
                for m in range(2):
                    V.tensor_tensor(facc[:, m, :], psum_fm("ffn1", 0, m), rstd_bc[:], ALU.mult).then_inc(evicted, 1)
                done("ffn1", 1, i)
                for m in range(2):
                    V.tensor_tensor(facc[:, 2 + m, :], psum_fm("ffn1", 1, m), rstd_bc[:], ALU.mult).then_inc(evicted, 1)
                for m in range(2):
                    dve.wait_ge(fgate, 2 * i + m + 1)
                    dve.wait_ge(evicted, T + 4 * i + 3 + m)
                    V.tensor_tensor(facc[:, 2 + m, :], facc[:, 2 + m, :], fg[:, m, :], ALU.mult).then_inc(fprod, 1)
                for m in range(2):
                    dve.wait_ge(hid_high, 2 * i + m + 1)
                    V.tensor_tensor(hid_lo[:, bass.ds(2 * i + m, 1), :], facc[:, 2 + m:3 + m, :], hid_hi[:, bass.ds(2 * i + m, 1), :].bitcast(F32),
                                    ALU.subtract).then_inc(hid_ready, 1)
            ffn1(0)
            with dve.Fori(1, FP) as i:
                ffn1(i)
            for panel in range(4):
                done("down1", panel)
                for m in range(2):
                    c = 2 * panel + m
                    V.tensor_tensor(XT[:, c, :], XT[:, c, :], psum_fm("down1", panel, m), ALU.add).then_inc(evicted, 1)
                for m in range(2):
                    add_squares(2, 2 * panel + m)

            def next_operand(k, name, first):
                return lambda c: low(opA_lo[:, c, :], XT[:, c, :], col(name, first + c), opA_hi[:, c, :]), lambda c: add_squares(k, c)

            def chunks(one, nxt, k, ready0):
                def step(c, factors):
                    one(c, factors)
                    if nxt:
                        dve.wait_ge(res_ready, ready0 + c + 1 if c == 0 else ready0 + c)

                norm(k, lambda factors: step(0, factors))
                if nxt:
                    nxt[0](0)
                for c in range(1, DC):
                    step(c, rstd_bc[:])
                    if nxt:
                        if c > 1:
                            nxt[0](c - 1)
                        nxt[1](c - 1)
                if nxt:
                    dve.wait_ge(res_ready, ready0 + DC)
                    nxt[0](DC - 1)
                    nxt[1](DC - 1)

            dve.wait_ge(sq_ready, 8 * 3)
            chunks(lambda c, factors: V.scalar_tensor_tensor(XT[:, c, :], XT[:, c, :], col("norm_final", c), factors, ALU.mult, ALU.mult).then_inc(res_ready, 1),
                   next_operand(3, "a_norm_pre_2", 0), 2, 0)

            def residual(key, k, name, first, nxt, layer):
                for panel in range(4):
                    done(key, panel)
                    for m in range(2):
                        V.tensor_copy(branch[:, 2 * panel + m, :], psum_fm(key, panel, m)).then_inc(evicted, 1)
                    for m in range(2):
                        add_squares(k, 2 * panel + m)

                def one(c, factors):
                    V.tensor_tensor(branch[:, c, :], branch[:, c, :], factors, ALU.mult).then_inc(res_scaled, 1)
                    dve.wait_ge(res_scaled, DC * layer + c + 1)
                    V.scalar_tensor_tensor(XT[:, c, :], branch[:, c, :], col(name, first + c), XT[:, c, :], ALU.mult, ALU.add).then_inc(res_ready, 1)

                chunks(one, nxt, k, DC * (layer + 1))

            def fin(l):
                T = 2 * PAN[("fin", l)]
                V.memset(fu[:, :, 0:2], 0.0).then_inc(pads, 1)
                dve.wait_ge(pads, 2 + l)

                def pair(i):
                    for half in range(2):
                        done(("fin", l), half, i)
                        for m in range(2):
                            j = 2 * half + m
                            V.tensor_tensor(fu[:, j, 2:2 + S], psum_fm(("fin", l), half, m), rstd_bc[:], ALU.mult).then_inc(evicted, 1)
                        for tap in range(2):
                            for m in range(2):
                                j = 2 * half + m
                                if tap == 0:
                                    dve.wait_ge(fconv_t0, 44 * l + 4 * i + j + 1)
                                else:
                                    dve.wait_ge(fconv_tap, 88 * l + 8 * i + 4 * half + 1 + m)
                                V.scalar_tensor_tensor(facc[:, j, :], fu[:, j, tap:tap + S], col("ffn_conv_w_2", 132 * l + 44 * tap + FT * half + m + 2 * i),
                                                       facc[:, j, :], ALU.mult, ALU.add).then_inc(fconv_tap, 1)
                    for m in range(2):
                        dve.wait_ge(fgate, FT * (l + 1) + 2 * i + m + 1)
                        dve.wait_ge(fconv_tap, 88 * l + 8 * i + 7 + m)
                        V.tensor_tensor(facc[:, 2 + m, :], facc[:, 2 + m, :], fg[:, m, :], ALU.mult).then_inc(fprod, 1)
                    for m in range(2):
                        dve.wait_ge(hid_high, FT * (l + 1) + 2 * i + m + 1)
                        V.tensor_tensor(hid_lo[:, bass.ds(2 * i + m, 1), :], facc[:, 2 + m:3 + m, :], hid_hi[:, bass.ds(2 * i + m, 1), :].bitcast(F32),
                                        ALU.subtract).then_inc(hid_ready, 1)

                pair(0)
                with dve.Fori(1, FP) as i:
                    pair(i)

            def qkv2(key):
                name, j = key
                if name[0] == "v":
                    values_panel(key, v2[j % 2], 0)
                    return
                done(key, 0)
                for m in range(2):
                    if name[0] == "q":
                        V.scalar_tensor_tensor(q2[j % 2][:, m, :], psum_fm(key, 0, m), 0.125, rstd_bc[:], ALU.mult, ALU.mult).then_inc(evicted, 1)
                    else:
                        V.tensor_tensor(k2[j % 2][:, m, :], psum_fm(key, 0, m), rstd_bc[:], ALU.mult).then_inc(evicted, 1)

            def softmax_units(names, fox):
                for tok in order2(names):
                    kind, u = tok[0], tok[1]
                    if kind == "slab":
                        continue
                    if kind == "epi":
                        qkv2(tok[1])
                        continue
                    U = 32 * fox + u
                    tile, qb = u // NB, u % NB
                    width = (qb + 1) * P
                    st = bstat[:, u % 4]
                    if kind == "M":
                        dve.wait_ge(s2_done, U + 1)
                        if fox:
                            wait(dve, tr2_done, 32 + 2 * u - 2 if u > 1 else 0)
                        x = sc[:, u % 2, :, 0:width]
                        if fox:
                            dve.wait_ge(negc_in[tile % 2], 16 * (tile // 2 + 1))
                            dve.wait_ge(ccol_ready, 1)
                            for e in range(2):
                                ins = V.scalar_tensor_tensor(x[:, e], negc[:, tile % 2, e, 0:width], ccol[:, qb, 2 * tile + e:2 * tile + e + 1],
                                                             AUX[:, e, 0:width], ALU.subtract, ALU.add)
                            ins.then_inc(sc_ready, 1)
                        else:
                            if u == 0:
                                dve.wait_ge(tbias_in, 16)
                            V.tensor_tensor(x, AUX[:, 0:2, 0:width], tbias[:, tile, S - width:S].unsqueeze(1).broadcast_to([P, 2, width]),
                                            ALU.add).then_inc(sc_ready, 1)
                        dve.wait_ge(sc_ready, U + 1)
                        V.tensor_reduce(st[:, 0:2], x, AX.X, ALU.max).then_inc(max2, 1)
                        dve.wait_ge(max2, U + 1)
                        V.tensor_scalar(st[:, 2:4], st[:, 0:2], -1.0, None, ALU.mult).then_inc(negmax2, 1)
                    elif kind == "T" and fox:
                        dve.wait_ge(tr2_done, 32 + 2 * u + 2)
                        wait(dve, pv2_done, U)
                        V.tensor_copy(pT[:, 1, 0:qb + 1, :], AUX[:, 3, 0:width].rearrange("p (b q) -> p b q", q=P)).then_inc(pT2_dve, 1)
                    elif kind == "D":
                        dve.wait_ge(exp2, 2 * U + 2)
                        V.reciprocal(st[:, 6:8], st[:, 4:6]).then_inc(r2_step, 1)
                        if not fox:
                            wait(dve, tr2_done, u - 1)
                            r0 = 4 * u
                            dve.wait_ge(r2_step, r0 + 1)
                            V.tensor_scalar(st[:, 10:11], st[:, 7:8], lams[:, 4:5], None, ALU.mult).then_inc(r2_step, 1)
                            dve.wait_ge(r2_step, r0 + 2)
                            V.tensor_scalar(dif[:, u % 2, 0:width], sc[:, u % 2, 1, 0:width], st[:, 10:11], None, ALU.mult).then_inc(r2_step, 1)
                            dve.wait_ge(r2_step, r0 + 3)
                            V.scalar_tensor_tensor(dif[:, u % 2, 0:width], sc[:, u % 2, 0, 0:width], st[:, 6:7], dif[:, u % 2, 0:width],
                                                   ALU.mult, ALU.subtract).then_inc(r2_step, 1)
                    elif kind == "O":
                        low(opA_lo[:, u, :], oT[:, u, :], None, opA_hi[:, u, :])
                    elif kind == "W":
                        wait(dve, ot2_done, 8 * fox + tile - 1)
                        if fox:
                            dve.wait_ge(pv2_done, U + 1)
                            dve.wait_ge(r2_step, 128 + u + 1)
                            for e in range(2):
                                V.tensor_scalar(osb2[:, tile % 2, qb, 64 * e:64 * e + 64], AUX[:, 2, 64 * e:64 * e + 64], st[:, 6 + e:7 + e], None,
                                                ALU.mult).then_inc(o2_read, 1)
                        else:
                            dve.wait_ge(pv2_done, u + 1)
                            V.tensor_copy(osb2[:, tile % 2, qb, :], AUX[:, 3, 0:P]).then_inc(o2_read, 1)
                    elif kind == "Y":
                        dve.wait_ge(o2_std, u + 1)
                        V.reciprocal(ostat[:, u % 2, 2 * NB:3 * NB], ostat[:, u % 2, NB:2 * NB]).then_inc(o2_rstd, 1)
                        dve.wait_ge(o2_rstd, u + 1)
                        V.tensor_tensor(osb2[:, u % 2], osb2[:, u % 2], ostat[:, u % 2, 2 * NB:3 * NB].unsqueeze(2).broadcast_to([P, NB, P]),
                                        ALU.mult).then_inc(o2_normed, 1)

            dve.wait_ge(lam_act, 2)
            V.scalar_tensor_tensor(lams[:, 4:5], lams[:, 2:3], LAM0, lams[:, 3:4], ALU.add, ALU.subtract).then_inc(lam_step, 1)
            dve.wait_ge(lam_step, 4)
            norm(3)
            for name in ("q2", "k2", "v2"):
                qkv2((name, 0))
            softmax_units(("q2", "k2", "v2"), 0)
            residual("awo", 4, "a_norm_post_2", 0, next_operand(5, "ffn_norm_pre_2", 0), 0)
            norm(5)
            fin(0)
            residual(("fout", 0), 6, "ffn_norm_post_2", 0, next_operand(7, "kv_norm_2", 0), 1)
            norm(7)
            qkv2(("k3", 0))
            narrow_out("f", f_rows, fx, bfv[:], 2, BH)
            step, q, a = softplus((fa, fe, fr, fz, fz2, fq), 18, 3)
            step(V.scalar_tensor_tensor(fz[:], q[:], 2.0, a[:], ALU.mult, ALU.add))
            for c in range(DC):
                low(opB_lo[:, c, :], XT[:, c, :], col("b_norm_pre_2", c), opB_hi[:, c, :])
            qkv2(("v3", 0))
            qkv2(("q3", 0))
            softmax_units(("q3", "k3", "v3"), 1)
            residual("bwo", 8, "b_norm_post_2", 0, next_operand(9, "ffn_norm_pre_2", 8), 2)
            norm(9)
            fin(1)
            residual(("fout", 1), 10, "ffn_norm_post_2", 8, None, 3)

    return nc


def shape_constants():
    f = np.float32
    c = {}
    d = S - 1 - np.arange(LINE)
    exact = BUCKETS // 2
    far = exact + (np.log(np.maximum(d, 1).astype(f) / f(exact)) / f(math.log(128 / exact)) * f(BUCKETS - exact)).astype(np.int32)
    bucket = np.where(np.maximum(d, 0) < exact, np.maximum(d, 0), np.minimum(far, BUCKETS - 1))
    c["c_onehot"] = (bucket[None, :] == np.arange(BUCKETS)[:, None]).astype(f)
    c["c_future"] = np.broadcast_to(np.where(d < 0, f(NEG), f(0)), (P, LINE)).astype(f)
    c["c_ident"] = np.eye(P, dtype=f)
    c["c_ones"] = np.ones((P, P), f)
    c["c_tri"] = (np.arange(P)[None, :] >= np.arange(P)[:, None]).astype(f)
    q, k = np.arange(P)[:, None], np.arange(P)[None, :]
    parts = []
    for dilation in (4, 16):
        same = (q - k) % dilation == 0
        parts += [same] * (NB - 1) + [same & (k <= q)]
    parts += [k >= q, k <= q]
    c["c_mask"] = np.where(np.concatenate(parts, 1), f(0), f(NEG))
    inv = f(10000.0) ** (-np.arange(ADIM // 2, dtype=f) / f(ADIM // 2))
    angle = np.arange(S, dtype=f)[None, :] * inv[:, None]
    c["c_cos"] = np.concatenate([np.cos(angle)] * 2).astype(f)
    c["c_sin"] = np.concatenate([np.sin(angle), -np.sin(angle)]).astype(f)
    return c


def kernel(**inputs):
    import concourse.bacc as bacc
    from concourse.bass_utils import run_bass_kernel_spmd

    a = {n: np.asarray(v) for n, v in inputs.items()}
    data = {"xT": a["x"][0].T}
    for n in WEIGHTS:
        data[n] = a[n[:-2]][int(n[-1])] if n[:-2] in a else a[n].reshape(a[n].shape[-2:])
    data["vec"] = np.concatenate([a[n].reshape(-1, P) for n, _ in VEC]).T
    data["dtv"] = np.concatenate([a["dt_bias"].reshape(-1), a["a_log"].reshape(-1)])
    data["bfv"] = a["b_f_2"].reshape(BH)
    data["d_skip"] = a["d_skip"].reshape(NH)
    data["lam"] = np.concatenate([a[n].reshape(-1) for n in ("a_lam_q1_2", "a_lam_k1_2", "a_lam_q2_2", "a_lam_k2_2")])
    data["ssm_norm"] = a["ssm_norm"].reshape(DI)
    data["rel_bias_2"] = a["rel_bias_2"]
    data.update(shape_constants())

    nc = bacc.Bacc("TRN2", target_bir_lowering=False, num_devices=1)
    arrays, I = {}, {}
    for n, v in data.items():
        arrays[f"in_{n}_dram"] = v = np.ascontiguousarray(v)
        I[n] = nc.dram_tensor(f"in_{n}_dram", v.shape, mybir.dt.from_np(v.dtype), kind="ExternalInput").ap()
    out = nc.dram_tensor("out_0_dram", (D, S), F32, kind="ExternalOutput").ap()
    build(nc, I, out)
    r = run_bass_kernel_spmd(nc, [arrays], core_ids=[0])
    return np.ascontiguousarray(r.results[0]["out_0_dram"].T).reshape(1, S, D)
```
